# Optimizing a Trainium2 kernel written in Bass

```python
import math
import jax, jax.numpy as jnp
from jax import lax
import numpy as np

D_MODEL = 1024
BATCH = 1
SEQ = 512
DEPTH = 1
DEC_BATCH = 1
DEC_SEQ = 256
PAST_LEN = 128

GRID_W = 64
EPS = 1e-6
POOL_WIDTH = D_MODEL // 2
POOL_WINDOWS = (2, 4, 8, 16)
POOL_GROUPS = len(POOL_WINDOWS)
POOL_GROUP_DIM = POOL_WIDTH // POOL_GROUPS
HEAD_DIM = 64
N_Q_HEADS = 8
N_KV_HEADS = 2
GQA_GROUP = N_Q_HEADS // N_KV_HEADS
ATTN_WIDTH = N_Q_HEADS * HEAD_DIM
KV_WIDTH = N_KV_HEADS * HEAD_DIM
MIX_WIDTH = POOL_WIDTH + ATTN_WIDTH
IN_WIDTH = POOL_WIDTH + ATTN_WIDTH + 2 * KV_WIDTH
ROPE_HALF = HEAD_DIM // 2
ROPE_THETA = 10000.0
ATTN_SCALE = 1.0 / math.sqrt(HEAD_DIM)
Q_BLOCK = 128
PEER_HEADS = 8
PEER_NKEYS = 128
PEER_EXPERTS = PEER_NKEYS * PEER_NKEYS
PEER_KEY_DIM = 256
PEER_HALF = PEER_KEY_DIM // 2
PEER_TOPK = 16
PEER_CHUNK = 128

kernel_name = "hymba_pool_gqa_peer_encoder"

def rms_norm(x, g):
    xf = x.astype(jnp.float32)
    y = xf * lax.rsqrt(jnp.mean(xf * xf, axis=-1, keepdims=True) + EPS)
    return (y * g.astype(jnp.float32)).astype(x.dtype)

def axial_rope_angles(n):
    rows = n // GRID_W
    row = jnp.repeat(jnp.arange(rows, dtype=jnp.float32), GRID_W)
    col = jnp.tile(jnp.arange(GRID_W, dtype=jnp.float32), rows)
    inv = 1.0 / (ROPE_THETA ** (jnp.arange(0, ROPE_HALF, 2, dtype=jnp.float32) / ROPE_HALF))
    return row[:, None] * inv, col[:, None] * inv

def rotate(xh, ang):
    a, b = jnp.split(xh, 2, axis=-1)
    c = jnp.cos(ang)[None, :, None, :]
    s = jnp.sin(ang)[None, :, None, :]
    return jnp.concatenate([a * c - b * s, a * s + b * c], axis=-1)

def apply_axial_rope(x, ang_r, ang_c):
    xf = x.astype(jnp.float32)
    return jnp.concatenate([rotate(xf[..., :ROPE_HALF], ang_r),
                            rotate(xf[..., ROPE_HALF:], ang_c)], axis=-1)

def pool_mixer(xp, pool_w, pool_scale):
    b, n, _ = xp.shape
    xf = xp.astype(jnp.float32)
    cs = jnp.concatenate([jnp.zeros((b, 1, POOL_WIDTH), jnp.float32),
                          jnp.cumsum(xf, axis=1)], axis=1)
    t = jnp.arange(n)
    outs = []
    for gi, w in enumerate(POOL_WINDOWS):
        lo = jnp.clip(t - w // 2, 0, n)
        hi = jnp.clip(t + (w - w // 2), 0, n)
        sl = slice(gi * POOL_GROUP_DIM, (gi + 1) * POOL_GROUP_DIM)
        csg = cs[..., sl]
        mean = (csg[:, hi] - csg[:, lo]) / (hi - lo).astype(jnp.float32)[None, :, None]
        outs.append((mean - xf[..., sl]) @ pool_w[gi].astype(jnp.float32))
    return (jnp.concatenate(outs, axis=-1) * pool_scale.astype(jnp.float32)).astype(xp.dtype)

def gqa_attention(zq, zk, zv, q_norm_g, k_norm_g):
    b, n, _ = zq.shape
    q = zq.reshape(b, n, N_Q_HEADS, HEAD_DIM)
    k = zk.reshape(b, n, N_KV_HEADS, HEAD_DIM)
    v = zv.reshape(b, n, N_KV_HEADS, HEAD_DIM).astype(jnp.float32)
    ang_r, ang_c = axial_rope_angles(n)
    q = apply_axial_rope(rms_norm(q, q_norm_g), ang_r, ang_c) * ATTN_SCALE
    k = apply_axial_rope(rms_norm(k, k_norm_g), ang_r, ang_c)
    nb = n // Q_BLOCK
    qb = q.reshape(b, nb, Q_BLOCK, N_KV_HEADS, GQA_GROUP, HEAD_DIM).transpose(1, 0, 2, 3, 4, 5)

    def block_fn(qblk):
        s = jnp.einsum('bqkgd,bskd->bkgqs', qblk, k)
        p = jax.nn.softmax(s, axis=-1)
        return jnp.einsum('bkgqs,bskd->bqkgd', p, v)

    o = lax.map(block_fn, qb)
    return o.transpose(1, 0, 2, 3, 4, 5).reshape(b, n, ATTN_WIDTH).astype(zq.dtype)

def peer_ffn(xn, wq, subkeys, u, v):
    b, n, d = xn.shape
    xt = xn.reshape(-1, PEER_CHUNK, d)
    sk = subkeys.astype(jnp.float32)

    def chunk_fn(xc):
        q = (xc @ wq).astype(jnp.float32).reshape(PEER_CHUNK, PEER_HEADS, 2, PEER_HALF)
        s = jnp.einsum('chpe,hpke->chpk', q, sk)
        sv, si = lax.top_k(s, PEER_TOPK)
        comb = (sv[:, :, 0, :, None] + sv[:, :, 1, None, :]).reshape(PEER_CHUNK, PEER_HEADS, PEER_TOPK * PEER_TOPK)
        cv, ci = lax.top_k(comb, PEER_TOPK)
        i1 = jnp.take_along_axis(si[:, :, 0], ci // PEER_TOPK, axis=-1)
        i2 = jnp.take_along_axis(si[:, :, 1], ci % PEER_TOPK, axis=-1)
        e = i1 * PEER_NKEYS + i2
        g = jax.nn.softmax(cv, axis=-1)
        hid = jnp.einsum('cd,chkd->chk', xc, u[e], preferred_element_type=jnp.float32)
        a = jax.nn.gelu(hid, approximate=False) * g
        out = jnp.einsum('chk,chkd->cd', a, v[e].astype(jnp.float32))
        return out.astype(xc.dtype)

    return lax.map(chunk_fn, xt).reshape(b, n, d)

def encoder_layer(x, norm1_g, w_in, pool_w, pool_scale, q_norm_g, k_norm_g, w_out,
                  norm2_g, peer_wq, peer_subkeys, peer_u, peer_v):
    h = rms_norm(x, norm1_g)
    z = h @ w_in
    zp = z[..., :POOL_WIDTH]
    zq = z[..., POOL_WIDTH:POOL_WIDTH + ATTN_WIDTH]
    zk = z[..., POOL_WIDTH + ATTN_WIDTH:POOL_WIDTH + ATTN_WIDTH + KV_WIDTH]
    zv = z[..., POOL_WIDTH + ATTN_WIDTH + KV_WIDTH:]
    mix = jnp.concatenate([pool_mixer(zp, pool_w, pool_scale),
                           gqa_attention(zq, zk, zv, q_norm_g, k_norm_g)], axis=-1)
    x = x + mix @ w_out
    x = x + peer_ffn(rms_norm(x, norm2_g), peer_wq, peer_subkeys, peer_u, peer_v)
    return x

def setup_inputs(seed: int = 0) -> dict:
    key = jax.random.key(seed)
    ks = jax.random.split(key, 15)
    f32 = jnp.float32
    nrm = lambda k, shape, s: jax.random.normal(k, shape, f32) * s
    return {
        "x_prompt": nrm(ks[0], (BATCH, SEQ, D_MODEL), 1.0),
        "x_sample": nrm(ks[1], (DEC_BATCH, DEC_SEQ, D_MODEL), 1.0),
        "norm1_g": 1.0 + nrm(ks[2], (DEPTH, D_MODEL), 0.02),
        "w_in": nrm(ks[3], (DEPTH, D_MODEL, IN_WIDTH), D_MODEL ** -0.5),
        "pool_w": nrm(ks[4], (DEPTH, POOL_GROUPS, POOL_GROUP_DIM, POOL_GROUP_DIM), POOL_GROUP_DIM ** -0.5),
        "pool_scale": 1.0 + nrm(ks[5], (DEPTH, POOL_WIDTH), 0.02),
        "q_norm_g": 1.0 + nrm(ks[6], (DEPTH, HEAD_DIM), 0.02),
        "k_norm_g": 1.0 + nrm(ks[7], (DEPTH, HEAD_DIM), 0.02),
        "w_out": nrm(ks[8], (DEPTH, MIX_WIDTH, D_MODEL), MIX_WIDTH ** -0.5),
        "norm2_g": 1.0 + nrm(ks[9], (DEPTH, D_MODEL), 0.02),
        "peer_wq": nrm(ks[10], (DEPTH, D_MODEL, PEER_HEADS * PEER_KEY_DIM), D_MODEL ** -0.5),
        "peer_subkeys": nrm(ks[11], (DEPTH, PEER_HEADS, 2, PEER_NKEYS, PEER_HALF), PEER_HALF ** -0.5),
        "peer_u": nrm(ks[12], (DEPTH, PEER_EXPERTS, D_MODEL), D_MODEL ** -0.5),
        "peer_v": nrm(ks[13], (DEPTH, PEER_EXPERTS, D_MODEL), PEER_HEADS ** -0.5),
    }

def reference(x_prompt, x_sample, norm1_g, w_in, pool_w, pool_scale, q_norm_g, k_norm_g,
              w_out, norm2_g, peer_wq, peer_subkeys, peer_u, peer_v):
    y_prompt = x_prompt
    y_sample = x_sample
    for l in range(DEPTH):
        params = (norm1_g[l], w_in[l], pool_w[l], pool_scale[l], q_norm_g[l], k_norm_g[l],
                  w_out[l], norm2_g[l], peer_wq[l], peer_subkeys[l], peer_u[l], peer_v[l])
        y_prompt = encoder_layer(y_prompt, *params)
        y_sample = encoder_layer(y_sample, *params)
    return (y_prompt, y_sample)


_drawn_inputs = setup_inputs


def setup_inputs(seed=0):
    import zlib

    import numpy as np

    out = dict(_drawn_inputs(seed))
    spreads = {}
    factors = {'norm1_g': 2.779, 'pool_scale': 8.216, 'q_norm_g': 8.0, 'k_norm_g': 8.0, 'norm2_g': 21.362}
    for name, (base, spread) in spreads.items():
        noise = np.random.default_rng([zlib.crc32(name.encode()), seed]).standard_normal(out[name].shape)
        drawn = base * np.exp(spread * noise) if base else spread * noise
        out[name] = __import__('jax').numpy.asarray(drawn.astype(out[name].dtype))
    for name, factor in factors.items():
        out[name] = (out[name] * factor).astype(out[name].dtype)
    return out
```

```python
import numpy as np
from contextlib import ExitStack
import concourse.bass as bass
from concourse import mybir

P = 128
D = 1024
KD = D // P
SEQ_TILES = ((0, 4), (4, 2))
TT = 6
TOK = TT * P
HALF = TOK // 2
WC = 256
N_WIN, N_WOUT, HEADS = 5, 4, 8
N_W = N_WIN + N_WOUT + HEADS
QK = 640
K_COL, V_COL, POOL_COL = 512, 640, 768
ZW = 1280
NK = 128
TOPK = 16
EPS = 1e-6
LOWEST = -3.4028234663852886e38
GRID_W, ROPE_HALF, ROPE_THETA = 64, 32, 10000.0
WINDOWS = (2, 4, 8, 16)
UNITS_T = 8
PAIR = 2
SG = 4
NBLK = 12
BLK = 64


class Steps:

    def __init__(self, eng, sem):
        self.eng, self.sem, self.n = eng, sem, 0

    def did(self, instruction):
        instruction.then_inc(self.sem, 1)
        self.n += 1
        return self.n

    def settle(self):
        self.eng.wait_ge(self.sem, self.n)

    def step(self, instruction):
        self.did(instruction)
        self.settle()

    def rewind(self):
        self.settle()
        self.eng.sem_inc(self.sem, -self.n)
        self.n = 0


def build(nc, io):
    F32, F32R, U32 = mybir.dt.float32, mybir.dt.float32r, mybir.dt.uint32
    ALU, ACT, AX = mybir.AluOpType, mybir.ActivationFunctionType, mybir.AxisListType
    ds = bass.ds
    ctx = ExitStack()
    with ctx:
        def sb(name, words, dt=F32):
            return ctx.enter_context(nc.sbuf_tensor(name, [P, words], dt))

        def sem(name):
            return ctx.enter_context(nc.semaphore(name))

        FTh_ = sb("feat_hi", KD * TOK, F32R)
        FTl_ = sb("feat_lo", KD * TOK, F32R)
        Wr_ = sb("w_raw", 2 * KD * WC)
        Wh_ = sb("w_hi", 2 * KD * WC, F32R)
        Wl_ = sb("w_lo", 2 * KD * WC, F32R)
        A_ = sb("arena_a", 17664)
        B_ = sb("arena_b", 7680)
        vecs = sb("vecs", 20)
        ident = sb("ident", P)
        iota = sb("iota", P)
        poolw = sb("poolw", 4 * P)
        st = sb("stats", 384)
        iu = sb("index_u32", 96, U32)
        gate_r = sb("gate_r", P, F32R)
        ps = ctx.enter_context(nc.psum_tensor("ps", [P, 8, 512], F32))

        def view(buf, at, *shape):
            n = int(np.prod(shape))
            v = buf[:, at:at + n]
            if len(shape) == 2:
                return v.rearrange("p (a b) -> p a b", a=shape[0])
            if len(shape) == 3:
                return v.rearrange("p (a b c) -> p a b c", a=shape[0], b=shape[1])
            if len(shape) == 4:
                return v.rearrange("p (a b c d) -> p a b c d", a=shape[0], b=shape[1], c=shape[2])
            return v

        FTh, FTl = view(FTh_, 0, KD, TOK), view(FTl_, 0, KD, TOK)
        Wr, Wh, Wl = (view(w, 0, 2, KD, WC) for w in (Wr_, Wh_, Wl_))
        g1, g2, pool_scale = vecs[:, 0:8], vecs[:, 8:16], vecs[:, 16:20]
        y = view(A_, 0, TT, D)
        z = view(A_, 6144, TT, ZW)
        qkr = view(A_, 13824, TT, QK)
        qj = view(A_, 0, TT, P)
        qT = A_[:, 768:1536]
        PT = view(A_, 1536, 2, 4, 512)
        qpT = view(A_, 6144, 2, 2, TOK)
        s_sb = view(A_, 9216, 2, TT, 256)
        xs = view(A_, 12288, 2, D)
        xgf = view(A_, 14336, 2, 512)
        skT = view(A_, 15360, 16, P)
        xst = view(B_, 0, 2, TOK)
        pooled = view(B_, 0, 2, TOK)
        zn = view(B_, 1536, 2, QK)
        rt = view(B_, 2816, 2, 320)
        gqk = B_[:, 3456:4096]
        band = view(B_, 4096, 2, 5, P)
        Pb = view(B_, 5376, 2, 512)
        kT = B_[:, 6400:7168]
        cos = view(B_, 7168, TT, 2, 16)
        sin = view(B_, 7360, TT, 2, 16)
        ss1, rs1, ss2, rs2, tmp6 = (st[:, 6 * i:6 * i + 6] for i in range(5))
        ss10, rs10, tmp10 = st[:, 32:92], st[:, 92:152], st[:, 152:212]
        nmax, rsum, rrec = st[:, 212:224], st[:, 224:236], st[:, 236:248]
        ssum8, srec8 = st[:, 248:256], st[:, 256:264]
        ur = view(Wr_, 0, 2, KD, P)
        uh, ul = view(Wh_, 0, 2, KD, P), view(Wl_, 0, 2, KD, P)
        oh_gh = view(Wh_, 2048, 2, SG, P)
        oh_2 = view(Wh_, 3072, 2, SG, P)
        oh_gl = view(Wl_, 2048, 2, SG, P)
        Gst = view(A_, 0, 2, NK, BLK)
        gel = view(B_, 0, 2, TOK)
        s_in = view(B_, 1536, 2, P)
        s_cut = view(B_, 1792, 2, P)
        comb = B_[:, 2048:2304]
        comb_cut = B_[:, 2304:2560]
        eq = view(B_, 2560, 2, TOPK, TOPK)
        sv = view(B_, 3072, 2, TOPK)
        sif = view(B_, 3104, 2, TOPK)
        jf = view(B_, 3136, 2, TOPK)
        cvh = B_[:, 3168:3184]
        CV = view(B_, 3200, HEADS, TOPK)
        IDX = view(B_, 3328, 2, P)
        CE = view(B_, 3584, HEADS, TOPK)
        par = view(B_, 3712, 3, P)
        par_gl = B_[:, 4096:4224]
        cur = view(B_, 4224, 3, TOPK)
        cur2 = view(B_, 4272, 2, SG)
        si_u = iu[:, 0:32].rearrange("p (a b) -> p a b", a=2)
        ci_u = iu[:, 32:48]
        jj_u = iu[:, 48:80].rearrange("p (a b) -> p a b", a=2)
        vr = view(Wr_, 0, 4, D)
        vh, vl = view(Wh_, 0, 2, D), view(Wl_, 0, 2, D)
        Ah, Al = view(Wh_, 2048, 2, HALF), view(Wl_, 2048, 2, HALF)
        zero_r = Wh_[:, 2816:3328]
        gel2 = view(B_, 0, 4, HALF)
        G2 = view(B_, 1536, 2, 6, 4 * BLK)
        Aw = view(B_, 4608, 2, HALF)

        small_in = sem("small_in")
        xt_in = [sem(f"xt_in{i}") for i in range(2)]
        x_in, xr_in, sk_in = sem("x_in"), sem("xr_in"), sem("sk_in")
        w_in = [sem(f"w_in{i}") for i in range(2)]
        band_in = [sem(f"band_in{i}") for i in range(2)]
        ft_hi, ft_lo, w_hi, w_lo, w_used = (sem(n) for n in ("ft_hi", "ft_lo", "w_hi", "w_lo", "w_used"))
        sq1, var1, root1, rstd1_ok = (sem(n) for n in ("sq1", "var1", "root1", "rstd1_ok"))
        z_mm, z_ev = sem("z_mm"), sem("z_ev")
        var10, root10, zn_ok, rope_ok, rope_step = (sem(n) for n in ("var10", "root10", "zn_ok", "rope_ok", "rope_step"))
        pool_mm, pool_ev, mix_mm, mix_hi, mix_lo = (sem(n) for n in ("pool_mm", "pool_ev", "mix_mm", "mix_hi", "mix_lo"))
        k_tr, k_ev, q_sel, q_tr, q_ev = (sem(n) for n in ("k_tr", "k_ev", "q_sel", "q_tr", "q_ev"))
        qk_mm, max_ok, exp_ok, p_ok, p_tr, pt_ev, pv_mm, o_hi, o_lo = (
            sem(n) for n in ("qk_mm", "max_ok", "exp_ok", "p_ok", "p_tr", "pt_ev", "pv_mm", "o_hi", "o_lo"))
        y_mm, y_ev = sem("y_mm"), sem("y_ev")
        sq2, var2, root2, rstd2_ok, xs_ok, xn_tr, xg_ok, xn_hi, xn_lo = (
            sem(n) for n in ("sq2", "var2", "root2", "rstd2_ok", "xs_ok", "xn_tr", "xg_ok", "xn_hi", "xn_lo"))
        y_out, y_in = sem("y_out"), sem("y_in")
        qp_mm, qp_ev, s_mm, s_ev = (sem(n) for n in ("qp_mm", "qp_ev", "s_mm", "s_ev"))
        s_out = [sem(f"s_out{i}") for i in range(2)]
        u_in = [sem(f"u_in{i}") for i in range(2)]
        u_hi, u_lo, h_mm, gelu_ok = (sem(n) for n in ("u_hi", "u_lo", "h_mm", "gelu_ok"))
        gel_out = [sem(f"gel_out{i}") for i in range(2)]
        s_load, s_read, oh2_ok, ohg_ok, g_mm, g_ev = (sem(n) for n in ("s_load", "s_read", "oh2_ok", "ohg_ok", "g_mm", "g_ev"))
        g_out = [sem(f"g_out{i}") for i in range(2)]
        ce_ok, ce_exp, gate_ok, par_tr, par_ok = (sem(n) for n in ("ce_ok", "ce_exp", "gate_ok", "par_tr", "par_ok"))
        i2_ok = sem("i2_ok")
        v_in = [sem(f"v_in{i}") for i in range(4)]
        gel_in = [sem(f"gel_in{i}") for i in range(4)]
        G_in = [sem(f"G_in{i}") for i in range(2)]
        a_mul, a_hi, a_lo, v_hi, v_lo, v_mm, zero_ok, acc_done, acc_ev, y_fin, done = (
            sem(n) for n in ("a_mul", "a_hi", "a_lo", "v_hi", "v_lo", "v_mm", "zero_ok", "acc_done", "acc_ev", "y_fin", "done"))
        dve_step = sem("dve_step")

        x_tiles = [io["x_prompt"][0, P * t:P * t + P, :] for t in range(4)] + \
                  [io["x_sample"][0, P * t:P * t + P, :] for t in range(2)]
        out_tiles = [io["y_prompt"][0, P * t:P * t + P, :] for t in range(4)] + \
                    [io["y_sample"][0, P * t:P * t + P, :] for t in range(2)]
        smalls = [(vecs[:, :], io["vecs"]), (ident[:, :], io["ident"]), (iota[:, :], io["iota"]),
                  (poolw[:, :], io["pool_w"]), (gqk, io["gqk"].partition_broadcast(P)),
                  (B_[:, 7168:7552], io["rope"])]
        s_dram, gel_dram, g_dram, y_dram = io["s_dram"], io["gel_dram"], io["g_dram"], io["y_dram"]

        units, groups = [], []
        for q, (t0, n) in enumerate(SEQ_TILES):
            for hh in range(2):
                groups.append((q, hh, t0, n, len(units) + n - 1))
                units += [(q, hh, t, len(groups) - 1) for t in range(n)]
        NU = len(units)

        def pe_split_product(out, lh, ll, rh, rl, first, last):
            nc.tensor.matmul(out, lh, rh, start=first, stop=False)
            nc.tensor.matmul(out, lh, rl, start=False, stop=False)
            return nc.tensor.matmul(out, ll, rh, start=False, stop=last)

        block = ctx.enter_context(nc.Block())

        @block.sync
        def _(sp):
            for dst, src in smalls:
                sp.dma_start(dst, src).then_inc(small_in, 16)

            def load_xt(k):
                if k >= 2:
                    sp.wait_ge(ft_lo, k - 1)
                sp.dma_start(xst[:, k % 2, :], io["xT"][:, k, :]).then_inc(xt_in[k % 2], 16)

            def load_w(n, slot):
                sp.dma_start(Wr[:, slot, :, :], io["w_all"][ds(n, 1), :, :, :].squeeze(0)).then_inc(w_in[slot], 16)

            load_xt(0)
            load_xt(1)
            load_w(0, 0)
            for k in range(2, KD):
                load_xt(k)
            load_w(1, 1)
            for t in range(TT):
                sp.dma_start(y[:, t, :], x_tiles[t]).then_inc(x_in, 16)
            for gi in range(2):
                sp.dma_start(band[:, gi, :, :], io["band"][gi]).then_inc(band_in[gi], 16)
            for n in range(2, 2 + N_WIN):
                sp.wait_ge(w_lo, n - 1)
                load_w(n, n % 2)
            for gi in range(2, 4):
                sp.wait_ge(pool_mm, 2 * (gi - 1))
                sp.dma_start(band[:, gi % 2, :, :], io["band"][gi]).then_inc(band_in[gi % 2], 16)
            for n in range(7, 9):
                sp.wait_ge(w_lo, n - 1)
                load_w(n, n % 2)
            sp.wait_ge(o_lo, 2 + 8)
            sp.wait_ge(pv_mm, 2 + 16)
            for t in range(TT):
                sp.dma_start(y[:, t, :], x_tiles[t]).then_inc(xr_in, 16)
            sp.dma_start(skT, io["skT"]).then_inc(sk_in, 16)
            for n in range(9, 11):
                sp.wait_ge(w_lo, n - 1)
                load_w(n, n % 2)

            def head_io(i, s, more):
                h = i * 2 + s
                if more:
                    sp.wait_ge(w_lo, h + 10)
                    load_w(h + 11, (11 + s) % 2)
                sp.wait_ge(s_ev, h * TT + (TT + 4))
                sp.dma_start(s_dram[ds(h, 1), :, :, :].squeeze(0), s_sb[:, s, :, :]).then_inc(s_out[s], 16)

            with sp.Fori(0, 3) as i:
                for s in range(2):
                    head_io(i, s, True)
            sp.wait_ge(w_lo, N_W)
            for s in range(2):
                sp.dma_start(ur[:, s, :, :], io["uT"][s]).then_inc(u_in[s], 16)
            for s in range(2):
                head_io(3, s, False)
            for s in range(2):
                sp.wait_ge(s_out[s], 16 + 64)

            def load_s(t, h):
                sp.dma_start(s_in, s_dram[ds(h, 1), :, ds(t, 1), :].squeeze(2).squeeze(0)
                             .rearrange("p (a b) -> p a b", a=2)).then_inc(s_load, 16)

            load_s(0, 0)

            def unit(U, T, h, prefetch, topk):
                for s in range(2):
                    if prefetch:
                        sp.wait_ge(u_lo, U * 2 + (s + 1))
                        sp.dma_start(ur[:, s, :, :], io["uT"][ds(U * 2 + (s + 2), 1), :, :, :].squeeze(0)
                                     ).then_inc(u_in[s], 16)
                    sp.wait_ge(gelu_ok, U * 4 + (2 * s + 2 + 4))
                    for half in range(2):
                        sp.dma_start(gel_dram[half][ds(U * 2 + s, 1), :, :].squeeze(0),
                                     gel[:, s, half * HALF:(half + 1) * HALF]).then_inc(gel_out[s], 16)
                if topk == "next":
                    sp.wait_ge(s_read, U + 1)
                    load_s((U + 1) // UNITS_T, (U + 1) % UNITS_T)

            def store_g(Tb, hb):
                sp.wait_ge(g_ev, Tb * 32 + (hb * 16 + 16 + 2))
                sp.dma_start(g_dram[ds(Tb * 2 + hb, 1), :, :, :].squeeze(0), Gst[:, hb, :, :]).then_inc(g_out[hb], 16)

            with sp.Fori(0, UNITS_T) as h:
                unit(h, 0, h, True, "next")
            with sp.Fori(1, TT - 1) as T:
                for hb in range(2):
                    with sp.Fori(0, 4) as q:
                        unit(T * 8 + (q + 4 * hb), T, q + 4 * hb, True, "next")
                    store_g(T - 1, hb)
            for hb in range(2):
                n = 4 - hb
                with sp.Fori(0, n) as q:
                    unit(q + (40 + 4 * hb), 5, q + 4 * hb, True, "next")
                if hb:
                    unit(47, 5, 7, True, None)
                store_g(4, hb)
            for hb in range(2):
                with sp.Fori(0, 4) as q:
                    unit(q + (48 + 4 * hb), 6, q + 4 * hb, True, None)
                store_g(5, hb)
            with sp.Fori(56, 63) as U:
                unit(U, 7, U - 56, True, None)
            unit(63, 7, 7, False, None)
            for s in range(2):
                sp.wait_ge(g_out[s], 16 + 16 * TT)
                sp.wait_ge(gel_out[s], 32 + 32 * 64)
            for t in range(TT):
                sp.dma_start(y[:, t, :], y_dram[t]).then_inc(y_in, 16)
            sp.wait_ge(h_mm, 256)

            def expert_loads(p, i):
                for x in range(8):
                    E = i * 8 + (128 * p + x)
                    e = i * 8 + x
                    if x % 4 == 0:
                        b = x // 4
                        sp.wait_ge(a_mul, E + 4)
                        sp.dma_start(G2[:, b, :, :],
                                     g_dram[6 * p:6 * p + 6, :, ds(e, 4), :].rearrange("b p e t -> p b (e t)")
                                     ).then_inc(G_in[b], 16)
                    sp.wait_ge(a_mul, E + 5)
                    sp.dma_start(gel2[:, x % 4, :], gel_dram[p][ds(e, 1), :, :].squeeze(0)).then_inc(gel_in[x % 4], 16)
                    sp.wait_ge(v_lo, E + 1)
                    sp.dma_start(vr[:, x % 4, :], io["v"][ds(e, 1), :, :].squeeze(0)).then_inc(v_in[x % 4], 16)

            with sp.Fori(0, 16) as i:
                expert_loads(0, i)
            expert_loads(1, 0)
            sp.wait_ge(acc_ev, 6)
            for t in range(3):
                sp.dma_start(out_tiles[t], y[:, t, :]).then_inc(done, 16)
            with sp.Fori(1, 16) as i:
                expert_loads(1, i)
            for t in range(3, 6):
                sp.wait_ge(acc_ev, 2 * t + 2)
                sp.dma_start(out_tiles[t], y[:, t, :]).then_inc(done, 16)
            sp.wait_ge(done, 16 * TT)

        @block.scalar
        def _(act):
            act.sem_inc(exp_ok, 2)
            act.sem_inc(pt_ev, 2)
            act.sem_inc(q_ev, 2)
            act.sem_inc(z_ev, 6)
            act.sem_inc(qp_ev, 4)
            act.sem_inc(gelu_ok, 4)
            act.sem_inc(g_ev, 2)
            for s in range(2):
                act.sem_inc(gel_out[s], 32)
                act.sem_inc(g_out[s], 16)
                act.sem_inc(s_out[s], 16)
            act.wait_ge(small_in, 16 * len(smalls))
            for k in range(KD):
                act.wait_ge(xt_in[k % 2], 16 * (k // 2 + 1))
                nc.scalar.activation(FTh[:, k, :], xst[:, k % 2, :], ACT.Copy, scale=g1[:, k:k + 1]).then_inc(ft_hi, 1)

            def w_split_hi(n):
                act.wait_ge(w_in[n % 2], 16 * (n // 2 + 1))
                if n >= 2:
                    act.wait_ge(w_used, n - 1)
                nc.scalar.activation(Wh[:, n % 2, :, :], Wr[:, n % 2, :, :], ACT.Copy).then_inc(w_hi, 1)

            w_split_hi(0)
            w_split_hi(1)
            act.wait_ge(x_in, 16 * TT)
            for t in range(TT):
                if t:
                    act.wait_ge(sq1, t)
                nc.scalar.activation(ps[:, 6:8, :], y[:, t, :].rearrange("p (a b) -> p a b", a=2), ACT.Square,
                                     accum_out=ss1[:, t:t + 1]).then_inc(sq1, 1)
            act.wait_ge(var1, 1)
            nc.scalar.activation(rs1, tmp6, ACT.Sqrt).then_inc(root1, 1)
            act.wait_ge(rstd1_ok, 1)

            def z_out(c):
                for t in range(TT):
                    act.wait_ge(z_mm, 6 * c + t + 1)
                    nc.scalar.activation(z[:, t, c * WC:(c + 1) * WC], ps[:, t, 0:WC], ACT.Copy,
                                         scale=rs1[:, t:t + 1]).then_inc(z_ev, 1)

            for c in range(N_WIN):
                z_out(c)
                w_split_hi(c + 2)
                if c == 3:
                    act.wait_ge(var10, 1)
                    nc.scalar.activation(rs10, tmp10, ACT.Sqrt).then_inc(root10, 1)

            def pooled_out(gi):
                for q, (t0, n) in enumerate(SEQ_TILES):
                    act.wait_ge(pool_mm, 2 * gi + q + 1)
                    if gi >= 2:
                        act.wait_ge(mix_mm, 2 * (gi - 2) + q + 1)
                    nc.scalar.activation(pooled[:, gi % 2, t0 * P:(t0 + n) * P], ps[:, q, 0:n * P],
                                         ACT.Copy).then_inc(pool_ev, 1)

            def mix_out(gi):
                for q, (t0, n) in enumerate(SEQ_TILES):
                    act.wait_ge(mix_mm, 2 * gi + q + 1)
                    nc.scalar.activation(FTh[:, 4 + gi, t0 * P:(t0 + n) * P], ps[:, 2 + q, 0:n * P], ACT.Copy,
                                         scale=pool_scale[:, gi:gi + 1]).then_inc(mix_hi, 1)

            pooled_out(0)
            for gi in range(1, 4):
                pooled_out(gi)
                mix_out(gi - 1)
            mix_out(3)
            act.wait_ge(k_tr, 1)
            nc.scalar.activation(kT[:, 0:512], ps[:, 4, :], ACT.Copy).then_inc(k_ev, 1)
            nc.scalar.activation(kT[:, 512:768], ps[:, 5, 0:256], ACT.Copy).then_inc(k_ev, 1)
            with act.Fori(0, 4) as j:
                act.wait_ge(q_tr, j + 2)
                nc.scalar.activation(qT[:, 0:512], ps[:, 0, :], ACT.Copy).then_inc(q_ev, 1)
                nc.scalar.activation(qT[:, 512:768], ps[:, 1, 0:256], ACT.Copy).then_inc(q_ev, 1)

                def pt_out(u):
                    q, hh, t, g = units[u]
                    n = SEQ_TILES[q][1]
                    if t == 0:
                        act.wait_ge(pv_mm, j * 4 + (g + 1))
                    act.wait_ge(p_tr, j * NU + (u + 3))
                    nc.scalar.activation(PT[:, g % 2, 0:n, t * P:(t + 1) * P],
                                         ps[:, 4 + u % 2, 0:n * P].rearrange("p (a b) -> p a b", a=n),
                                         ACT.Copy).then_inc(pt_ev, 1)

                def o_out(q):
                    t0, n = SEQ_TILES[q]
                    act.wait_ge(pv_mm, j * 4 + (2 * q + 4))
                    nc.scalar.activation(FTh[:, ds(j, 1), t0 * P:(t0 + n) * P].squeeze(1), ps[:, 6 + q, 0:n * P],
                                         ACT.Copy).then_inc(o_hi, 1)

                for u, (q, hh, t, g) in enumerate(units):
                    n = SEQ_TILES[q][1]
                    act.wait_ge(max_ok, j * NU + (u + 1))
                    act.wait_ge(p_tr, j * NU + (u + 1))
                    nc.scalar.activation(Pb[:, u % 2, 0:n * P], ps[:, 2 + u % 2, 0:n * P], ACT.Exp,
                                         bias=nmax[:, u:u + 1], accum_out=rsum[:, u:u + 1]).then_inc(exp_ok, 1)
                    if u:
                        pt_out(u - 1)
                    if u == 10:
                        o_out(0)
                pt_out(NU - 1)
                o_out(1)
            for n in range(7, 11):
                w_split_hi(n)
            act.wait_ge(y_ev, 6 + 24)
            act.dma_start(y_dram.rearrange("t p d -> p t d"), y).then_inc(y_out, 16)
            for t in range(TT):
                if t:
                    act.wait_ge(sq2, t)
                nc.scalar.activation(ps[:, 6:8, :], y[:, t, :].rearrange("p (a b) -> p a b", a=2), ACT.Square,
                                     accum_out=ss2[:, t:t + 1]).then_inc(sq2, 1)
            act.wait_ge(var2, 1)
            nc.scalar.activation(rs2, tmp6, ACT.Sqrt).then_inc(root2, 1)
            act.wait_ge(rstd2_ok, 1)

            def scaled(t):
                if t >= 2:
                    act.wait_ge(xn_tr, t - 1)
                nc.scalar.activation(xs[:, t % 2, :], y[:, t, :], ACT.Copy, scale=rs2[:, t:t + 1]).then_inc(xs_ok, 1)

            scaled(0)
            for t in range(TT):
                if t + 1 < TT:
                    scaled(t + 1)
                for b in range(2):
                    act.wait_ge(xg_ok, 2 * t + b + 1)
                    nc.scalar.activation(FTh[:, 4 * b:4 * b + 4, t * P:(t + 1) * P],
                                         xgf[:, b, :].rearrange("p (a b) -> p a b", a=4), ACT.Copy).then_inc(xn_hi, 1)

            def head(i, s, more):
                h = i * 2 + s
                for n in range(4):
                    if n == 0:
                        act.wait_ge(s_mm, h * TT + TT)
                    act.wait_ge(qp_mm, h * 4 + (n + 1))
                    nc.scalar.activation(qpT[:, s, n // 2, (n % 2) * HALF:(n % 2 + 1) * HALF], ps[:, n, 0:HALF],
                                         ACT.Copy).then_inc(qp_ev, 1)
                if more:
                    act.wait_ge(w_in[(11 + s) % 2], i * 16 + 16 * ((11 + s) // 2 + 1))
                    act.wait_ge(w_used, h + 10)
                    nc.scalar.activation(Wh[:, (11 + s) % 2, :, :], Wr[:, (11 + s) % 2, :, :],
                                         ACT.Copy).then_inc(w_hi, 1)

            with act.Fori(0, 3) as i:
                for s in range(2):
                    head(i, s, True)
            for s in range(2):
                head(3, s, False)
            act.wait_ge(w_used, N_W)
            for s in range(2):
                act.wait_ge(u_in[s], 16)
                nc.scalar.activation(uh[:, s, :, :], ur[:, s, :, :], ACT.Copy).then_inc(u_hi, 1)

            def unit(U, Ub, q, hb, prefetch):
                for s in range(2):
                    for half in range(2):
                        if half == 0:
                            act.wait_ge(gel_out[s], U * 32 + 32)
                        act.wait_ge(h_mm, U * 4 + (2 * s + half + 1))
                        nc.scalar.activation(gel[:, s, half * HALF:(half + 1) * HALF], ps[:, 2 * s + half, 0:HALF],
                                             ACT.Gelu).then_inc(gelu_ok, 1)
                        if half == 1 and prefetch:
                            act.wait_ge(u_in[s], U * 16 + 32)
                            nc.scalar.activation(uh[:, s, :, :], ur[:, s, :, :], ACT.Copy).then_inc(u_hi, 1)
                        if Ub is not None:
                            sg = 2 * s + half
                            act.wait_ge(g_mm, Ub * 4 + (sg + 3))
                            nc.scalar.activation(Gst[:, hb, :, ds(q * 16 + sg * SG, SG)],
                                                 ps[:, 4 + sg % 2, :].rearrange("p (t i) -> p i t", t=SG),
                                                 ACT.Copy).then_inc(g_ev, 1)

            def tile_end(T):
                act.wait_ge(ce_ok, T + 1)
                nc.scalar.activation(CE, CE, ACT.Exp).then_inc(ce_exp, 1)

            with act.Fori(0, UNITS_T) as U:
                unit(U, None, None, None, True)
            tile_end(0)
            act.wait_ge(y_out, 16)
            with act.Fori(1, TT) as T:
                for hb in range(2):
                    act.wait_ge(g_out[hb], T * 16)
                    with act.Fori(0, 4) as q:
                        unit(T * 8 + (q + 4 * hb), T * 8 + (q + (4 * hb - 8)), q, hb, True)
                tile_end(T)
            for hb in range(2):
                act.wait_ge(g_out[hb], TT * 16)
                with act.Fori(0, 4) as q:
                    unit(q + (48 + 4 * hb), q + (40 + 4 * hb), q, hb, True)
            with act.Fori(56, 63) as U:
                unit(U, None, None, None, True)
            unit(63, None, None, None, False)
            with act.Fori(0, 32) as i:
                for x in range(8):
                    E = i * 8 + x
                    act.wait_ge(v_mm, E + 1)
                    act.wait_ge(v_in[x % 4], i * 32 + 16 * (x // 4 + 1))
                    nc.scalar.activation(vh[:, x % 2, :], vr[:, x % 4, :], ACT.Copy).then_inc(v_hi, 1)
                    act.wait_ge(a_mul, E + 9)
                    nc.scalar.activation(Ah[:, x % 2, :], Aw[:, x % 2, :], ACT.Copy).then_inc(a_hi, 1)

        @block.gpsimd
        def _(pool):
            pool.sem_inc(a_mul, 8)
            steps = Steps(pool, rope_step)
            for t in range(TT):
                pool.wait_ge(zn_ok, t + 1)
                src = zn[:, t % 2, :].rearrange("p (g a i) -> p g a i", a=2, i=16)
                dst = qkr[:, t, :].rearrange("p (g a i) -> p g a i", a=2, i=16)
                ta = rt[:, 0, :].rearrange("p (h g i) -> p h g i", g=2, i=16)
                tb = rt[:, 1, :].rearrange("p (h g i) -> p h g i", g=2, i=16)
                c = cos[:, t, :, :].unsqueeze(1).to_broadcast([P, 10, 2, 16])
                s = sin[:, t, :, :].unsqueeze(1).to_broadcast([P, 10, 2, 16])

                def part(v, a):
                    return v[:, :, a, :].rearrange("p (h g) i -> p h g i", g=2)

                for first, second, op, o in ((c, s, ALU.subtract, 0), (s, c, ALU.add, 1)):
                    steps.did(nc.gpsimd.tensor_tensor(ta, part(src, 0), first, ALU.mult))
                    steps.step(nc.gpsimd.tensor_tensor(tb, part(src, 1), second, ALU.mult))
                    ins = nc.gpsimd.tensor_tensor(part(dst, o), ta, tb, op)
                    if o == 0:
                        steps.step(ins)
                    else:
                        ins.then_inc(rope_ok, 1)
                        pool.wait_ge(rope_ok, t + 1)
            with pool.Fori(0, 4) as j:
                pool.wait_ge(q_tr, j + 1)
                nc.gpsimd.tensor_copy(qj, qkr[:, :, ds(j * P, P)]).then_inc(q_sel, 1)

            def build_oh2(Tb, h):
                for sg in range(4):
                    if sg == 0:
                        pool.wait_ge(par_ok, Tb + 1)
                    pool.wait_ge(g_mm, Tb * 32 + (h * 4 + sg + 1))
                    nc.gpsimd.tensor_copy(cur2[:, sg % 2, :], par[:, 1, ds(h * 16 + sg * SG, SG)]).then_inc(i2_ok, 1)
                    pool.wait_ge(i2_ok, 1)
                    pool.sem_inc(i2_ok, -1)
                    for k in range(SG):
                        last = nc.gpsimd.tensor_scalar(oh_2[:, sg % 2, k, :], iota[:, :], cur2[:, sg % 2, k:k + 1], None,
                                                       ALU.is_equal)
                    last.then_inc(oh2_ok, 1)

            with pool.Fori(0, TT) as Tb:
                with pool.Fori(0, UNITS_T) as h:
                    build_oh2(Tb, h)
            pool.wait_ge(g_mm, 2 + 4 * 48)
            nc.gpsimd.memset(zero_r.bitcast(F32), 0.0).then_inc(zero_ok, 1)
            with pool.Fori(0, 32) as i:
                for x in range(8):
                    E = i * 8 + x
                    pool.wait_ge(gel_in[x % 4], i * 32 + 16 * (x // 4 + 1))
                    if x % 4 == 0:
                        pool.wait_ge(G_in[x // 4], i * 16 + 16)
                    pool.wait_ge(a_lo, E + 1)
                    nc.gpsimd.tensor_tensor(
                        Aw[:, x % 2, :].rearrange("p (b t) -> p b t", t=BLK),
                        gel2[:, x % 4, :].rearrange("p (b t) -> p b t", t=BLK),
                        G2[:, x // 4, :, (x % 4) * BLK:(x % 4 + 1) * BLK], ALU.mult).then_inc(a_mul, 1)

        @block.vector
        def _(dve):
            dve.sem_inc(o_lo, 2)
            dve.sem_inc(ohg_ok, 1)
            dve.sem_inc(y_ev, 6)
            dve.sem_inc(s_ev, 4)
            dve.sem_inc(a_lo, 2)
            dve.sem_inc(v_lo, 4)
            tt, ts = nc.vector.tensor_tensor, nc.vector.tensor_scalar
            steps = Steps(dve, dve_step)
            dve.wait_ge(small_in, 16 * len(smalls))
            for k in range(KD):
                dve.wait_ge(ft_hi, k + 1)
                nc.vector.scalar_tensor_tensor(FTl[:, k, :], xst[:, k % 2, :], g1[:, k:k + 1],
                                               FTh[:, k, :].bitcast(F32), ALU.mult, ALU.subtract).then_inc(ft_lo, 1)

            def w_split_lo(n):
                dve.wait_ge(w_hi, n + 1)
                tt(Wl[:, n % 2, :, :], Wr[:, n % 2, :, :], Wh[:, n % 2, :, :].bitcast(F32),
                   ALU.subtract).then_inc(w_lo, 1)

            def newton(r, root, a, tmp, ok):
                dve.wait_ge(root, 1)
                steps.step(nc.vector.reciprocal(r, r))
                steps.step(tt(tmp[1], r, r, ALU.mult))
                steps.step(tt(tmp[1], tmp[1], a, ALU.mult))
                steps.step(ts(tmp[1], tmp[1], -0.5, 1.5, ALU.mult, ALU.add))
                return tt(r, r, tmp[1], ALU.mult)

            w_split_lo(0)
            w_split_lo(1)
            dve.wait_ge(sq1, TT)
            ts(tmp6, ss1, 1.0 / D, EPS, ALU.mult, ALU.add).then_inc(var1, 1)
            newton(rs1, root1, tmp6, (None, ss1), None).then_inc(rstd1_ok, 1)
            for n in range(2, 5):
                w_split_lo(n)
            dve.wait_ge(z_ev, 6 + 18)
            for t in range(TT):
                steps.step(tt(zn[:, 0, :], z[:, t, 0:QK], z[:, t, 0:QK], ALU.mult))
                steps.step(nc.vector.tensor_reduce(ss10[:, 10 * t:10 * t + 10],
                                                   zn[:, 0, :].rearrange("p (h d) -> p h d", d=64), AX.X, ALU.add))
            ts(tmp10, ss10, 1.0 / 64, EPS, ALU.mult, ALU.add).then_inc(var10, 1)
            steps.step(newton(rs10, root10, tmp10, (None, ss10), None))
            rq = rs10.rearrange("p (t h) -> p t h", h=10)
            steps.step(ts(rq[:, :, 0:8], rq[:, :, 0:8], 0.125, None, ALU.mult))
            for t in range(TT):
                if t >= 2:
                    dve.wait_ge(rope_ok, t - 1)
                steps.step(tt(zn[:, t % 2, :].rearrange("p (h d) -> p h d", d=64),
                              z[:, t, 0:QK].rearrange("p (h d) -> p h d", d=64),
                              rs10[:, 10 * t:10 * t + 10].unsqueeze(2).to_broadcast([P, 10, 64]), ALU.mult))
                tt(zn[:, t % 2, :], zn[:, t % 2, :], gqk, ALU.mult).then_inc(zn_ok, 1)
            w_split_lo(5)
            w_split_lo(6)
            for gi in range(4):
                for q, (t0, n) in enumerate(SEQ_TILES):
                    dve.wait_ge(mix_hi, 2 * gi + q + 1)
                    nc.vector.scalar_tensor_tensor(
                        FTl[:, 4 + gi, t0 * P:(t0 + n) * P], ps[:, 2 + q, 0:n * P], pool_scale[:, gi:gi + 1],
                        FTh[:, 4 + gi, t0 * P:(t0 + n) * P].bitcast(F32), ALU.mult, ALU.subtract).then_inc(mix_lo, 1)
            steps.rewind()
            with dve.Fori(0, 4) as j:

                def row_max(u):
                    n = SEQ_TILES[units[u][0]][1]
                    dve.wait_ge(qk_mm, j * NU + (u + 1))
                    nc.vector.tensor_reduce(nmax[:, u:u + 1], ps[:, 2 + u % 2, 0:n * P], AX.X, ALU.max,
                                            negate=True).then_inc(max_ok, 1)

                def o_rest(q):
                    t0, n = SEQ_TILES[q]
                    dve.wait_ge(o_hi, j * 2 + (q + 1))
                    tt(FTl[:, ds(j, 1), t0 * P:(t0 + n) * P].squeeze(1), ps[:, 6 + q, 0:n * P],
                       FTh[:, ds(j, 1), t0 * P:(t0 + n) * P].squeeze(1).bitcast(F32), ALU.subtract).then_inc(o_lo, 1)

                row_max(0)
                for u, (q, hh, t, g) in enumerate(units):
                    n = SEQ_TILES[q][1]
                    if u + 1 < NU:
                        row_max(u + 1)
                    dve.wait_ge(exp_ok, j * NU + (u + 3))
                    steps.step(nc.vector.reciprocal(rrec[:, u:u + 1], rsum[:, u:u + 1]))
                    ts(Pb[:, u % 2, 0:n * P], Pb[:, u % 2, 0:n * P], rrec[:, u:u + 1], None,
                       ALU.mult).then_inc(p_ok, 1)
                    if u == 11:
                        o_rest(0)
                o_rest(1)
                steps.rewind()
            dve.wait_ge(xr_in, 16 * TT)
            for c in range(N_WOUT):
                for t in range(TT):
                    dve.wait_ge(y_mm, 6 * c + t + 1)
                    tt(y[:, t, c * WC:(c + 1) * WC], y[:, t, c * WC:(c + 1) * WC], ps[:, t, 0:WC],
                       ALU.add).then_inc(y_ev, 1)
                w_split_lo(7 + c)
            dve.wait_ge(sq2, TT)
            ts(tmp6, ss2, 1.0 / D, EPS, ALU.mult, ALU.add).then_inc(var2, 1)
            newton(rs2, root2, tmp6, (None, ss2), None).then_inc(rstd2_ok, 1)
            for t in range(TT):
                for b in range(2):
                    dve.wait_ge(xn_tr, t + 1)
                    if t:
                        dve.wait_ge(xn_lo, 2 * (t - 1) + b + 1)
                    tt(xgf[:, b, :].rearrange("p (a b) -> p a b", a=4),
                       ps[:, 2 * (t % 2) + b, :].rearrange("p (a b) -> p a b", a=4),
                       g2[:, 4 * b:4 * b + 4].unsqueeze(2).to_broadcast([P, 4, P]), ALU.mult).then_inc(xg_ok, 1)
                for b in range(2):
                    dve.wait_ge(xn_hi, 2 * t + b + 1)
                    tt(FTl[:, 4 * b:4 * b + 4, t * P:(t + 1) * P], xgf[:, b, :].rearrange("p (a b) -> p a b", a=4),
                       FTh[:, 4 * b:4 * b + 4, t * P:(t + 1) * P].bitcast(F32), ALU.subtract).then_inc(xn_lo, 1)

            def head(i, s, more):
                h = i * 2 + s
                dve.wait_ge(s_out[s], i * 16 + 16)
                if more:
                    dve.wait_ge(w_hi, h + 12)
                    tt(Wl[:, (11 + s) % 2, :, :], Wr[:, (11 + s) % 2, :, :], Wh[:, (11 + s) % 2, :, :].bitcast(F32),
                       ALU.subtract).then_inc(w_lo, 1)
                for t in range(TT):
                    dve.wait_ge(s_mm, h * TT + (t + 13))
                    nc.vector.tensor_copy(s_sb[:, s, t, :], ps[:, 4 + (6 * s + t) % 4, 0:256]).then_inc(s_ev, 1)

            with dve.Fori(0, 3) as i:
                for s in range(2):
                    head(i, s, True)
            for s in range(2):
                head(3, s, False)

            def u_split_lo(e1, s):
                dve.wait_ge(u_hi, e1)
                tt(ul[:, s, :, :], ur[:, s, :, :], uh[:, s, :, :].bitcast(F32), ALU.subtract).then_inc(u_lo, 1)

            def one_hots(Tb, h, sg):
                if sg == 0:
                    dve.wait_ge(ohg_ok, Tb * 32 + (h * 4 + 1))
                    steps.step(nc.vector.tensor_copy(cur[:, 0, :], par[:, 0, ds(h * 16, 16)]))
                    steps.step(nc.vector.tensor_copy(cur[:, 1, :], par[:, 2, ds(h * 16, 16)]))
                    steps.step(nc.vector.tensor_copy(cur[:, 2, :], par_gl[:, ds(h * 16, 16)]))
                    steps.rewind()
                dve.wait_ge(g_mm, Tb * 32 + h * 4 + (sg + 1))
                for k in range(SG):
                    n = SG * sg + k
                    ts(oh_gh[:, sg % 2, k, :], iota[:, :], cur[:, 0, n:n + 1], cur[:, 1, n:n + 1],
                       ALU.is_equal, ALU.mult)
                    last = ts(oh_gl[:, sg % 2, k, :], iota[:, :], cur[:, 0, n:n + 1], cur[:, 2, n:n + 1],
                              ALU.is_equal, ALU.mult)
                last.then_inc(ohg_ok, 1)

            def top16(val, idx, src, cut):
                steps.step(nc.vector.max(val[:, 0:8], src))
                steps.did(nc.vector.max_index(idx[:, 0:8], val[:, 0:8], src))
                steps.step(nc.vector.match_replace(cut, val[:, 0:8], src, LOWEST))
                steps.step(nc.vector.max(val[:, 8:16], cut))
                steps.step(nc.vector.max_index(idx[:, 8:16], val[:, 8:16], cut))

            def topk_head(U, h):
                dve.wait_ge(s_load, 16)
                dve.sem_inc(s_load, -16)
                for p in range(2):
                    top16(sv[:, p, :], si_u[:, p, :], s_in[:, p, :], s_cut[:, p, :])
                dve.sem_inc(s_read, 1)
                steps.did(nc.vector.tensor_copy(sif, si_u))
                c3 = comb.rearrange("p (a b) -> p a b", a=TOPK)
                steps.step(tt(c3, sv[:, 0, :].unsqueeze(2).to_broadcast([P, TOPK, TOPK]),
                              sv[:, 1, :].unsqueeze(1).to_broadcast([P, TOPK, TOPK]), ALU.add))
                top16(cvh, ci_u, comb, comb_cut)
                steps.did(nc.vector.tensor_copy(CV[:, ds(h, 1), :].squeeze(1), cvh))
                steps.did(ts(jj_u[:, 0, :], ci_u, 4, None, ALU.logical_shift_right))
                steps.step(ts(jj_u[:, 1, :], ci_u, 15, None, ALU.bitwise_and))
                steps.step(nc.vector.tensor_copy(jf, jj_u))
                steps.step(tt(eq, jf.unsqueeze(3).to_broadcast([P, 2, TOPK, TOPK]),
                              iota[:, 0:TOPK].unsqueeze(1).unsqueeze(1).to_broadcast([P, 2, TOPK, TOPK]), ALU.is_equal))
                steps.step(tt(eq, eq, sif.unsqueeze(2).to_broadcast([P, 2, TOPK, TOPK]), ALU.mult))
                steps.step(nc.vector.tensor_reduce(IDX[:, :, ds(h * TOPK, TOPK)], eq, AX.X, ALU.add))
                steps.rewind()

            def unit(U, h, Tb, topk, prefetch):
                u_split_lo(U * 2 + 2, 1)
                if Tb is not None:
                    one_hots(Tb, h, 0)
                    one_hots(Tb, h, 1)
                if topk:
                    topk_head(U, h)
                if prefetch:
                    u_split_lo(U * 2 + 3, 0)
                if Tb is not None:
                    one_hots(Tb, h, 2)
                    one_hots(Tb, h, 3)

            def tile_end(T, oh2_before):
                tt(CE, CV, CV[:, :, 0:1].to_broadcast([P, HEADS, TOPK]), ALU.subtract).then_inc(ce_ok, 1)
                dve.wait_ge(ce_exp, T + 1)
                steps.step(nc.vector.tensor_reduce(ssum8, CE, AX.X, ALU.add))
                steps.step(nc.vector.reciprocal(srec8, ssum8))
                tt(CE, CE, srec8.unsqueeze(2).to_broadcast([P, HEADS, TOPK]), ALU.mult).then_inc(gate_ok, 1)
                dve.wait_ge(par_tr, T + 1)
                if oh2_before is not None:
                    dve.wait_ge(oh2_ok, oh2_before)
                ins = nc.vector.tensor_copy(par, ps[:, 6, 0:384].rearrange("p (a b) -> p a b", a=3))
                ins.then_inc(par_ok, 1)
                dve.wait_ge(par_ok, T + 1)
                steps.step(nc.vector.tensor_copy(gate_r[:, :], par[:, 2, :]))
                steps.step(tt(par_gl, par[:, 2, :], gate_r[:, :].bitcast(F32), ALU.subtract))
                steps.rewind()

            u_split_lo(1, 0)
            steps.rewind()
            with dve.Fori(0, UNITS_T) as h:
                unit(h, h, None, True, True)
            tile_end(0, None)
            with dve.Fori(1, TT) as T:
                with dve.Fori(0, UNITS_T) as h:
                    unit(T * 8 + h, h, T - 1, True, True)
                tile_end(T, T * 32)
            with dve.Fori(0, UNITS_T) as h:
                unit(h + 48, h, TT - 1, False, True)
            with dve.Fori(56, 63) as U:
                unit(U, None, None, False, True)
            unit(63, None, None, False, False)
            for p in range(2):
                with dve.Fori(16 * p, 16 * p + 16) as i:
                    for x in range(8):
                        E = i * 8 + x
                        dve.wait_ge(v_hi, E + 1)
                        tt(vl[:, x % 2, :], vr[:, x % 4, :], vh[:, x % 2, :].bitcast(F32),
                           ALU.subtract).then_inc(v_lo, 1)
                        dve.wait_ge(a_hi, E + 1)
                        tt(Al[:, x % 2, :], Aw[:, x % 2, :], Ah[:, x % 2, :].bitcast(F32),
                           ALU.subtract).then_inc(a_lo, 1)
                if p == 0:
                    dve.wait_ge(y_in, 16 * TT)
                dve.wait_ge(acc_done, p + 1)
                for n in range(6):
                    t, dh = 3 * p + n // 2, n % 2
                    tt(y[:, t, dh * 512:(dh + 1) * 512], y[:, t, dh * 512:(dh + 1) * 512], ps[:, n, :],
                       ALU.add).then_inc(acc_ev, 1)

        @block.tensor
        def _(pe):
            mm = nc.tensor.matmul
            pe.sem_inc(q_tr, 1)
            pe.sem_inc(p_tr, 2)
            pe.sem_inc(pv_mm, 2)
            pe.sem_inc(s_mm, 12)
            pe.sem_inc(g_mm, 2)
            pe.sem_inc(v_mm, 2)
            pe.wait_ge(ft_lo, KD)
            with pe.Fori(0, N_WIN) as c:
                pe.wait_ge(w_lo, c + 1)
                for t in range(TT):
                    pe.wait_ge(z_ev, c * 6 + (t + 1))
                    for k in range(KD):
                        last = pe_split_product(
                            ps[:, t, 0:WC], FTh[:, k, t * P:(t + 1) * P], FTl[:, k, t * P:(t + 1) * P],
                            Wh[:, ds(c % 2, 1), k, :].squeeze(1), Wl[:, ds(c % 2, 1), k, :].squeeze(1),
                            k == 0, k == KD - 1)
                    last.then_inc(z_mm, 1)
                pe.wait_ge(z_mm, c * 6 + 6)
                pe.sem_inc(w_used, 1)

            def windows(gi):
                pe.wait_ge(band_in[gi % 2], 16 * (gi // 2 + 1))
                for q, (t0, n) in enumerate(SEQ_TILES):
                    if gi:
                        pe.wait_ge(pool_ev, 2 * (gi - 1) + q + 1)
                    for t in range(n):
                        srcs = [(s, 3 if s < t else 4 if s > t else 0 if t == 0 else 2 if t == n - 1 else 1)
                                for s in range(max(t - 1, 0), min(t + 2, n))]
                        for m, (s, kind) in enumerate(srcs):
                            last = mm(ps[:, q, t * P:(t + 1) * P],
                                      z[:, t0 + s, POOL_COL + gi * P:POOL_COL + (gi + 1) * P],
                                      band[:, gi % 2, kind, :], start=m == 0, stop=m == len(srcs) - 1)
                    last.then_inc(pool_mm, 1)

            def group_map(gi):
                for q, (t0, n) in enumerate(SEQ_TILES):
                    pe.wait_ge(pool_ev, 2 * gi + q + 1)
                    if gi:
                        pe.wait_ge(mix_lo, 2 * (gi - 1) + q + 1)
                    mm(ps[:, 2 + q, 0:n * P], poolw[:, gi * P:(gi + 1) * P],
                       pooled[:, gi % 2, t0 * P:(t0 + n) * P], start=True, stop=True).then_inc(mix_mm, 1)

            pe.wait_ge(z_ev, 6 + 30)
            windows(0)
            for gi in range(1, 4):
                windows(gi)
                group_map(gi - 1)
            group_map(3)
            pe.wait_ge(rope_ok, TT)
            for t in range(TT):
                last = nc.tensor.transpose(ps[:, 4 + t // 4, (t % 4) * P:(t % 4 + 1) * P], qkr[:, t, K_COL:K_COL + P],
                                           ident[:, :])
            last.then_inc(k_tr, 1)
            pe.wait_ge(k_ev, 2)
            pe.wait_ge(mix_lo, 8)
            with pe.Fori(0, 4) as j:
                pe.wait_ge(q_sel, j + 1)
                pe.wait_ge(q_ev, j * 2 + 2)
                for t in range(TT):
                    last = nc.tensor.transpose(ps[:, t // 4, (t % 4) * P:(t % 4 + 1) * P], qj[:, t, :], ident[:, :])
                last.then_inc(q_tr, 1)
                pe.wait_ge(q_ev, j * 2 + 4)

                def scores(u):
                    q, hh, t, g = units[u]
                    t0, n = SEQ_TILES[q]
                    pe.wait_ge(exp_ok, j * NU + (u + 1))
                    mm(ps[:, 2 + u % 2, 0:n * P], qT[64 * hh:64 * hh + 64, (t0 + t) * P:(t0 + t + 1) * P],
                       kT[64 * hh:64 * hh + 64, t0 * P:(t0 + n) * P], start=True, stop=True).then_inc(qk_mm, 1)

                def flip(u):
                    q, hh, t, g = units[u]
                    n = SEQ_TILES[q][1]
                    pe.wait_ge(p_ok, j * NU + (u + 1))
                    pe.wait_ge(pt_ev, j * NU + (u + 1))
                    for s in range(n):
                        last = nc.tensor.transpose(ps[:, 4 + u % 2, s * P:(s + 1) * P],
                                                   Pb[:, u % 2, s * P:(s + 1) * P], ident[:, :])
                    last.then_inc(p_tr, 1)

                def values(g):
                    q, hh, t0, n, u_last = groups[g]
                    pe.wait_ge(pt_ev, j * NU + (u_last + 3))
                    pe.wait_ge(o_lo, j * 2 + (q + 1))
                    for s in range(n):
                        last = mm(ps[64 * hh:64 * hh + 64, 6 + q, 0:n * P],
                                  z[:, t0 + s, V_COL + 64 * hh:V_COL + 64 * hh + 64],
                                  PT[:, g % 2, s, 0:n * P], start=s == 0, stop=s == n - 1)
                    last.then_inc(pv_mm, 1)

                scores(0)
                for u in range(NU):
                    if u + 1 < NU:
                        scores(u + 1)
                    flip(u)
                    for g, grp in enumerate(groups):
                        if grp[4] == u - 1:
                            values(g)
                values(3)
            pe.wait_ge(o_lo, 2 + 8)
            with pe.Fori(0, N_WOUT) as c:
                pe.wait_ge(w_lo, c + 6)
                for t in range(TT):
                    pe.wait_ge(y_ev, c * 6 + (t + 1))
                    for k in range(KD):
                        last = pe_split_product(
                            ps[:, t, 0:WC], FTh[:, k, t * P:(t + 1) * P], FTl[:, k, t * P:(t + 1) * P],
                            Wh[:, ds((c + 1) % 2, 1), k, :].squeeze(1), Wl[:, ds((c + 1) % 2, 1), k, :].squeeze(1),
                            k == 0, k == KD - 1)
                    last.then_inc(y_mm, 1)
                pe.wait_ge(y_mm, c * 6 + 6)
                pe.sem_inc(w_used, 1)
            pe.wait_ge(y_ev, 6 + 24)
            for t in range(TT):
                pe.wait_ge(xs_ok, t + 1)
                if t >= 2:
                    pe.wait_ge(xg_ok, 2 * (t - 1))
                for k in range(KD):
                    last = nc.tensor.transpose(ps[:, 2 * (t % 2) + k // 4, (k % 4) * P:(k % 4 + 1) * P],
                                               xs[:, t % 2, k * P:(k + 1) * P], ident[:, :])
                last.then_inc(xn_tr, 1)
            pe.wait_ge(xn_lo, 12)
            pe.wait_ge(sk_in, 16)
            with pe.Fori(0, 4) as i:
                for s in range(2):
                    h = i * 2 + s
                    ws = (9 + s) % 2
                    pe.wait_ge(w_lo, h + 10)
                    for n in range(4):
                        p, half = n // 2, n % 2
                        pe.wait_ge(qp_ev, h * 4 + (n + 1))
                        for k in range(KD):
                            last = pe_split_product(
                                ps[:, n, 0:HALF], Wh[:, ws, k, p * P:(p + 1) * P], Wl[:, ws, k, p * P:(p + 1) * P],
                                FTh[:, k, half * HALF:(half + 1) * HALF], FTl[:, k, half * HALF:(half + 1) * HALF],
                                k == 0, k == KD - 1)
                        last.then_inc(qp_mm, 1)
                    pe.wait_ge(qp_mm, h * 4 + 4)
                    pe.sem_inc(w_used, 1)
                    pe.wait_ge(qp_ev, h * 4 + 8)
                    for t in range(TT):
                        pe.wait_ge(s_ev, h * TT + (t + 1))
                        for p in range(2):
                            last = mm(ps[:, 4 + (6 * s + t) % 4, p * P:(p + 1) * P], qpT[:, s, p, t * P:(t + 1) * P],
                                      skT[:, ds(h * 2 + p, 1), :].squeeze(1), start=True, stop=True)
                        last.then_inc(s_mm, 1)

            def unit(U, Tb, h):
                for s in range(2):
                    for half in range(2):
                        if half == 0:
                            pe.wait_ge(u_lo, U * 2 + (s + 1))
                        pe.wait_ge(gelu_ok, U * 4 + (2 * s + half + 1))
                        for k in range(KD):
                            last = pe_split_product(
                                ps[:, 2 * s + half, 0:HALF], uh[:, s, k, :], ul[:, s, k, :],
                                FTh[:, k, half * HALF:(half + 1) * HALF], FTl[:, k, half * HALF:(half + 1) * HALF],
                                k == 0, k == KD - 1)
                        last.then_inc(h_mm, 1)
                        if Tb is not None:
                            sg = 2 * s + half
                            Q = Tb * 32 + h * 4 + sg
                            pe.wait_ge(ohg_ok, Q + 2)
                            pe.wait_ge(oh2_ok, Q + 1)
                            pe.wait_ge(g_ev, Q + 1)
                            for n in range(SG):
                                out = ps[:, 4 + sg % 2, n * P:(n + 1) * P]
                                mm(out, oh_2[:, sg % 2, n, :], oh_gh[:, sg % 2, n, :], start=True, stop=False)
                                last = mm(out, oh_2[:, sg % 2, n, :], oh_gl[:, sg % 2, n, :], start=False, stop=True)
                            last.then_inc(g_mm, 1)

            def tile_end(T):
                pe.wait_ge(gate_ok, T + 1)
                for n in range(2):
                    nc.tensor.transpose(ps[:, 6, n * P:(n + 1) * P], IDX[:, n, :], ident[:, :])
                nc.tensor.transpose(ps[:, 6, 2 * P:3 * P], B_[:, 3584:3712], ident[:, :]).then_inc(par_tr, 1)

            with pe.Fori(0, UNITS_T) as U:
                unit(U, None, None)
            tile_end(0)
            with pe.Fori(1, TT) as T:
                with pe.Fori(0, UNITS_T) as h:
                    unit(T * 8 + h, T - 1, h)
                tile_end(T)
            with pe.Fori(0, UNITS_T) as h:
                unit(h + 48, TT - 1, h)
            with pe.Fori(56, 64) as U:
                unit(U, None, None)
            pe.wait_ge(zero_ok, 1)
            pe.wait_ge(gelu_ok, 4 + 256)
            for p in range(2):
                if p:
                    pe.wait_ge(acc_ev, 6)
                for n in range(6):
                    mm(ps[:, n, :], zero_r[:, 0:P], zero_r, start=True, stop=False, skip_group_check=True)
                with pe.Fori(16 * p, 16 * p + 16) as i:
                    for x in range(8):
                        E = i * 8 + x
                        pe.wait_ge(v_lo, E + 5)
                        pe.wait_ge(a_lo, E + 3)
                        for t in range(3):
                            for dh in range(2):
                                out = ps[:, 2 * t + dh, :]
                                ah, al = (a[:, x % 2, t * P:(t + 1) * P] for a in (Ah, Al))
                                bh, bl = (b[:, x % 2, dh * 512:(dh + 1) * 512] for b in (vh, vl))
                                mm(out, ah, bh, start=False, stop=False, skip_group_check=True)
                                mm(out, ah, bl, start=False, stop=False, skip_group_check=True)
                                last = mm(out, al, bh, start=False, stop=False, skip_group_check=True)
                        last.then_inc(v_mm, 1)
                for n in range(6):
                    last = mm(ps[:, n, :], zero_r[:, 0:P], zero_r, start=False, stop=True, skip_group_check=True)
                last.then_inc(acc_done, 1)


def tables():
    f = np.float32
    pos = np.concatenate([np.arange(n * P) for _, n in SEQ_TILES])
    inv = (f(1.0) / (f(ROPE_THETA) ** (np.arange(0, ROPE_HALF, 2, dtype=f) / f(ROPE_HALF)))).astype(f)
    ang = np.stack([(pos // GRID_W).astype(f)[:, None] * inv, (pos % GRID_W).astype(f)[:, None] * inv], 1)
    rope = np.stack([np.cos(ang), np.sin(ang)]).astype(f).reshape(2, TT, P, 32).transpose(2, 0, 1, 3).reshape(P, -1)
    band = np.zeros((4, P, 5, P), f)
    n = 3 * P
    for g, w in enumerate(WINDOWS):
        m = np.zeros((n, n), f)
        for t in range(n):
            lo, hi = max(t - w // 2, 0), min(t + w - w // 2, n)
            m[lo:hi, t] = f(1.0) / f(hi - lo)
            m[t, t] -= f(1.0)
        blocks = {0: (0, 0), 1: (1, 1), 2: (2, 2), 3: (0, 1), 4: (1, 0)}
        for kind, (a, b) in blocks.items():
            band[g, :, kind] = m[a * P:(a + 1) * P, b * P:(b + 1) * P]
    return dict(ident=np.eye(P, dtype=f), iota=np.tile(np.arange(P, dtype=f), (P, 1)),
                rope=np.ascontiguousarray(rope), band=band)


def kernel(**inputs):
    import concourse.bacc as bacc
    from concourse.bass_utils import run_bass_kernel_spmd as run

    a = {k: np.asarray(v) for k, v in inputs.items()}
    heads = [0, 4, 1, 5, 2, 6, 3, 7]
    w = a["w_in"][0]
    w_q = w[:, 512:1024].reshape(D, 8, 64)[:, heads].reshape(D, 512)
    w_in = np.concatenate([w_q, w[:, 1024:1280], w[:, 0:512]], 1)
    wo = a["w_out"][0]
    wo = np.concatenate([wo[512:1024].reshape(8, 64, D)[heads].reshape(512, D), wo[0:512]], 0)
    w_all = np.concatenate([w_in, wo, a["peer_wq"][0]], 1)
    x = np.concatenate([a["x_prompt"][0], a["x_sample"][0]], 0)
    data = dict(
        x_prompt=a["x_prompt"], x_sample=a["x_sample"],
        xT=x.T.reshape(KD, P, TOK).transpose(1, 0, 2),
        vecs=np.concatenate([a["norm1_g"][0].reshape(8, P).T, a["norm2_g"][0].reshape(8, P).T,
                             a["pool_scale"][0].reshape(4, P).T], 1),
        gqk=np.concatenate([np.tile(a["q_norm_g"][0], 8), np.tile(a["k_norm_g"][0], 2)]),
        pool_w=a["pool_w"][0].transpose(1, 0, 2).reshape(P, 4 * P),
        w_all=w_all.reshape(KD, P, N_W, WC).transpose(2, 1, 0, 3),
        skT=a["peer_subkeys"][0].transpose(3, 0, 1, 2).reshape(P, 16, P),
        uT=a["peer_u"][0].reshape(NK, P, KD, P).transpose(0, 3, 2, 1),
        v=a["peer_v"][0].reshape(NK, P, D),
        **tables(),
    )
    data = {k: np.ascontiguousarray(v) for k, v in data.items()}
    nc = bacc.Bacc("TRN2", target_bir_lowering=False, num_devices=1)
    f32 = mybir.dt.float32
    io = {k: nc.dram_tensor("in_" + k, v.shape, f32, kind="ExternalInput").ap() for k, v in data.items()}
    scratch = dict(s_dram=(HEADS, P, TT, 256), g_dram=(NBLK, P, NK, BLK), gel_dram=(2, NK, P, HALF), y_dram=(TT, P, D))
    io.update({k: nc.dram_tensor(k, s, f32, kind="Internal").ap() for k, s in scratch.items()})
    outs = dict(y_prompt=(1, 512, D), y_sample=(1, 256, D))
    io.update({k: nc.dram_tensor(k, s, f32, kind="ExternalOutput").ap() for k, s in outs.items()})
    build(nc, io)
    r = run(nc, [{"in_" + k: v for k, v in data.items()}], core_ids=[0])
    return tuple(r.results[0][k] for k in outs)
```

```python
import numpy as np
from contextlib import ExitStack
import concourse.bass as bass
from concourse import mybir

P = 128
D = 1024
KD = D // P
SEQ_TILES = ((0, 4), (4, 2))
TT = 6
TOK = TT * P
HALF = TOK // 2
WC = 256
N_WIN, N_WOUT, HEADS = 5, 4, 8
N_W = N_WIN + N_WOUT + HEADS
QK = 640
K_COL, V_COL, POOL_COL = 512, 640, 768
ZW = 1280
NK = 128
TOPK = 16
EPS = 1e-6
LOWEST = -3.4028234663852886e38
GRID_W, ROPE_HALF, ROPE_THETA = 64, 32, 10000.0
WINDOWS = (2, 4, 8, 16)
UNITS_T = 8
PAIR = 2
SG = 4
NBLK = 12
BLK = 64


class Steps:

    def __init__(self, eng, sem):
        self.eng, self.sem, self.n = eng, sem, 0

    def did(self, instruction):
        instruction.then_inc(self.sem, 1)
        self.n += 1
        return self.n

    def settle(self):
        self.eng.wait_ge(self.sem, self.n)

    def step(self, instruction):
        self.did(instruction)
        self.settle()

    def rewind(self):
        self.settle()
        self.eng.sem_inc(self.sem, -self.n)
        self.n = 0


def build(nc, io):
    F32, F32R, U32 = mybir.dt.float32, mybir.dt.float32r, mybir.dt.uint32
    ALU, ACT, AX = mybir.AluOpType, mybir.ActivationFunctionType, mybir.AxisListType
    ds = bass.ds
    ctx = ExitStack()
    with ctx:
        def sb(name, words, dt=F32):
            return ctx.enter_context(nc.sbuf_tensor(name, [P, words], dt))

        def sem(name):
            return ctx.enter_context(nc.semaphore(name))

        FTh_ = sb("feat_hi", KD * TOK, F32R)
        FTl_ = sb("feat_lo", KD * TOK, F32R)
        Wr_ = sb("w_raw", 2 * KD * WC)
        Wh_ = sb("w_hi", 2 * KD * WC, F32R)
        Wl_ = sb("w_lo", 2 * KD * WC, F32R)
        A_ = sb("arena_a", 17664)
        B_ = sb("arena_b", 7680)
        vecs = sb("vecs", 20)
        ident = sb("ident", P)
        iota = sb("iota", P)
        poolw = sb("poolw", 4 * P)
        st = sb("stats", 384)
        iu = sb("index_u32", 96, U32)
        gate_r = sb("gate_r", P, F32R)
        zero_r = sb("zero_r", P, F32R)
        ps = ctx.enter_context(nc.psum_tensor("ps", [P, 8, 512], F32))

        def view(buf, at, *shape):
            n = int(np.prod(shape))
            v = buf[:, at:at + n]
            if len(shape) == 2:
                return v.rearrange("p (a b) -> p a b", a=shape[0])
            if len(shape) == 3:
                return v.rearrange("p (a b c) -> p a b c", a=shape[0], b=shape[1])
            if len(shape) == 4:
                return v.rearrange("p (a b c d) -> p a b c d", a=shape[0], b=shape[1], c=shape[2])
            return v

        FTh, FTl = view(FTh_, 0, KD, TOK), view(FTl_, 0, KD, TOK)
        Wr, Wh, Wl = (view(w, 0, 2, KD, WC) for w in (Wr_, Wh_, Wl_))
        g1, g2, pool_scale = vecs[:, 0:8], vecs[:, 8:16], vecs[:, 16:20]
        y = view(A_, 0, TT, D)
        z = view(A_, 6144, TT, ZW)
        qkr = view(A_, 13824, TT, QK)
        qj = view(A_, 0, TT, P)
        qT = A_[:, 768:1536]
        PT = view(A_, 1536, 2, 4, 512)
        qpT = view(A_, 6144, 2, 2, TOK)
        s_sb = view(A_, 9216, 2, TT, 256)
        xs = view(A_, 12288, 2, D)
        xgf = view(A_, 9216, 4, 512)
        skT = view(A_, 15360, 16, P)
        xst = view(A_, 6144, KD, TOK)
        pooled = view(B_, 0, 2, TOK)
        zn = view(B_, 1536, 2, QK)
        rt = view(B_, 2816, 2, 320)
        gqk = B_[:, 3456:4096]
        band = view(B_, 4096, 2, 5, P)
        Pb = view(B_, 0, 4, 512)
        kT = B_[:, 6400:7168]
        cos = view(B_, 7168, TT, 2, 16)
        sin = view(B_, 7360, TT, 2, 16)
        ss1, rs1, ss2, rs2, tmp6 = (st[:, 6 * i:6 * i + 6] for i in range(5))
        ss10, rs10, tmp10 = st[:, 32:92], st[:, 92:152], st[:, 152:212]
        nmax, rsum, rrec = st[:, 212:224], st[:, 224:236], st[:, 236:248]
        ssum8, srec8 = st[:, 248:256], st[:, 256:264]
        ur = view(Wr_, 2048, 2, KD, P)
        uh, ul = view(Wh_, 2048, 2, KD, P), view(Wl_, 2048, 2, KD, P)
        oh_g = Wh_[:, 0:2048].rearrange("p (a t c i) -> p a t c i", a=2, t=SG, c=2)
        oh_2 = view(Wl_, 0, 2, SG, P)
        oh_1 = view(Wr_, 0, 2, SG, P)
        Gst = view(A_, 0, 2, NK, BLK)
        gel = view(B_, 0, 2, TOK)
        s_in = view(B_, 1536, 2, P)
        s_cut = view(B_, 1792, 2, P)
        comb = B_[:, 2048:2304]
        comb_cut = B_[:, 2304:2560]
        eq = view(B_, 2560, 2, TOPK, TOPK)
        sv = view(B_, 3072, 2, TOPK)
        sif = view(B_, 3104, 2, TOPK)
        jf = view(B_, 3136, 2, TOPK)
        cvh = B_[:, 3168:3184]
        CV = view(B_, 3200, HEADS, TOPK)
        IDX = view(B_, 3328, 2, P)
        CE = view(B_, 3584, HEADS, TOPK)
        par = view(B_, 3712, 2, 4, P)
        G_ps = [ps[:, b:b + 2, :].rearrange("p b (m c i) -> p c (b m) i", m=2, c=2) for b in (4, 6)]
        si_u = iu[:, 0:32].rearrange("p (a b) -> p a b", a=2)
        ci_u = iu[:, 32:48]
        jj_u = iu[:, 48:80].rearrange("p (a b) -> p a b", a=2)
        G_lo = view(B_, 4736, 2, SG, P)
        vr = view(Wr_, 0, 4, D)
        vh, vl = view(Wh_, 0, 2, D), view(Wl_, 0, 2, D)
        Ah, Al = view(Wh_, 2048, 2, HALF), view(Wl_, 2048, 2, HALF)
        G2 = view(A_, 6144, 2, 6, 4 * BLK)
        gel2 = view(A_, 9216, 4, HALF)
        Aw = view(A_, 10752, 2, HALF)

        small_in = sem("small_in")
        xt_in = [sem(f"xt_in{i}") for i in range(KD)]
        x_in, xr_in, sk_in = sem("x_in"), sem("xr_in"), sem("sk_in")
        w_in = [sem(f"w_in{i}") for i in range(2)]
        band_in = [sem(f"band_in{i}") for i in range(2)]
        ft_hi, ft_lo, w_hi, w_lo, w_used = (sem(n) for n in ("ft_hi", "ft_lo", "w_hi", "w_lo", "w_used"))
        sq1, var1, root1, rstd1_ok = (sem(n) for n in ("sq1", "var1", "root1", "rstd1_ok"))
        z_mm, z_ev = sem("z_mm"), sem("z_ev")
        var10, root10, zn_ok, rope_ok, rope_step = (sem(n) for n in ("var10", "root10", "zn_ok", "rope_ok", "rope_step"))
        pool_mm, pool_ev, mix_mm, mix_hi, mix_lo = (sem(n) for n in ("pool_mm", "pool_ev", "mix_mm", "mix_hi", "mix_lo"))
        k_tr, k_ev, q_sel, q_tr, q_ev = (sem(n) for n in ("k_tr", "k_ev", "q_sel", "q_tr", "q_ev"))
        qk_mm, max_ok, exp_ok, p_ok, p_tr, pt_ev, pv_mm, o_hi, o_lo = (
            sem(n) for n in ("qk_mm", "max_ok", "exp_ok", "p_ok", "p_tr", "pt_ev", "pv_mm", "o_hi", "o_lo"))
        y_mm, y_ev = sem("y_mm"), sem("y_ev")
        sq2, var2, root2, rstd2_ok, xs_ok, xn_tr, xg_ok, xn_hi, xn_lo = (
            sem(n) for n in ("sq2", "var2", "root2", "rstd2_ok", "xs_ok", "xn_tr", "xg_ok", "xn_hi", "xn_lo"))
        y_out, y_in = sem("y_out"), sem("y_in")
        qp_mm, qp_ev, s_mm, s_ev = (sem(n) for n in ("qp_mm", "qp_ev", "s_mm", "s_ev"))
        s_out = [sem(f"s_out{i}") for i in range(2)]
        u_in = [sem(f"u_in{i}") for i in range(2)]
        u_hi, u_lo, h_mm, gelu_ok = (sem(n) for n in ("u_hi", "u_lo", "h_mm", "gelu_ok"))
        gel_out = [sem(f"gel_out{i}") for i in range(2)]
        s_load, s_read, oh2_ok, ohg_ok, g_mm, g_ev = (sem(n) for n in ("s_load", "s_read", "oh2_ok", "ohg_ok", "g_mm", "g_ev"))
        g_out = [sem(f"g_out{i}") for i in range(2)]
        ce_ok, ce_exp, gate_ok, par_tr = (sem(n) for n in ("ce_ok", "ce_exp", "gate_ok", "par_tr"))
        oh1_ok, g_part, par_ev = sem("oh1_ok"), sem("g_part"), sem("par_ev")
        v_in = [sem(f"v_in{i}") for i in range(4)]
        gel_in = [sem(f"gel_in{i}") for i in range(4)]
        G_in = [sem(f"G_in{i}") for i in range(2)]
        a_mul, a_hi, a_lo, v_hi, v_lo, v_mm, zero_ok, acc_done, acc_ev, y_fin, done = (
            sem(n) for n in ("a_mul", "a_hi", "a_lo", "v_hi", "v_lo", "v_mm", "zero_ok", "acc_done", "acc_ev", "y_fin", "done"))
        dve_step = sem("dve_step")

        x_tiles = [io["x_prompt"][0, P * t:P * t + P, :] for t in range(4)] + \
                  [io["x_sample"][0, P * t:P * t + P, :] for t in range(2)]
        out_tiles = [io["y_prompt"][0, P * t:P * t + P, :] for t in range(4)] + \
                    [io["y_sample"][0, P * t:P * t + P, :] for t in range(2)]
        smalls = [(vecs[:, :], io["vecs"]), (ident[:, :], io["ident"]), (iota[:, :], io["iota"]),
                  (poolw[:, :], io["pool_w"]), (gqk, io["gqk"].partition_broadcast(P)),
                  (B_[:, 7168:7552], io["rope"])]
        s_dram, gel_dram, g_dram, y_dram = io["s_dram"], io["gel_dram"], io["g_dram"], io["y_dram"]

        units, groups = [], []
        for q, (t0, n) in enumerate(SEQ_TILES):
            for hh in range(2):
                groups.append((q, hh, t0, n, len(units) + n - 1))
                units += [(q, hh, t, len(groups) - 1) for t in range(n)]
        NU = len(units)

        def pe_split_product(out, lh, ll, rh, rl, first, last):
            nc.tensor.matmul(out, lh, rh, start=first, stop=False)
            nc.tensor.matmul(out, lh, rl, start=False, stop=False)
            return nc.tensor.matmul(out, ll, rh, start=False, stop=last)

        block = ctx.enter_context(nc.Block())

        @block.sync
        def _(sp):
            for dst, src in smalls:
                sp.dma_start(dst, src).then_inc(small_in, 16)

            def load_xt(k):
                sp.dma_start(xst[:, k, :], io["xT"][:, k, :]).then_inc(xt_in[k], 16)

            def load_w(n, slot):
                sp.dma_start(Wr[:, slot, :, :], io["w_all"][ds(n, 1), :, :, :].squeeze(0)).then_inc(w_in[slot], 16)

            for k in range(KD):
                load_xt(k)
                if k == 1:
                    load_w(0, 0)
            load_w(1, 1)
            for t in range(TT):
                sp.dma_start(y[:, t, :], x_tiles[t]).then_inc(x_in, 16)
            for gi in range(2):
                sp.dma_start(band[:, gi, :, :], io["band"][gi]).then_inc(band_in[gi], 16)
            for n in range(2, 2 + N_WIN):
                sp.wait_ge(w_lo, n - 1)
                load_w(n, n % 2)
            for gi in range(2, 4):
                sp.wait_ge(pool_mm, 2 * (gi - 1))
                sp.dma_start(band[:, gi % 2, :, :], io["band"][gi]).then_inc(band_in[gi % 2], 16)
            for n in range(7, 9):
                sp.wait_ge(w_lo, n - 1)
                load_w(n, n % 2)
            sp.wait_ge(o_lo, 2 + 8)
            sp.wait_ge(pv_mm, 2 + 16)
            for t in range(TT):
                sp.dma_start(y[:, t, :], x_tiles[t]).then_inc(xr_in, 16)
            sp.dma_start(skT, io["skT"]).then_inc(sk_in, 16)
            for n in range(9, 11):
                sp.wait_ge(w_lo, n - 1)
                load_w(n, n % 2)

            def head_io(i, s, more):
                h = i * 2 + s
                if more:
                    sp.wait_ge(w_lo, h + 10)
                    load_w(h + 11, (11 + s) % 2)
                sp.wait_ge(s_ev, h * TT + (TT + 4))
                sp.dma_start(s_dram[ds(h, 1), :, :, :].squeeze(0), s_sb[:, s, :, :]).then_inc(s_out[s], 16)

            with sp.Fori(0, 3) as i:
                for s in range(2):
                    head_io(i, s, True)
            sp.wait_ge(w_lo, N_W - 1)
            for s in range(2):
                sp.dma_start(ur[:, s, :, :], io["uT"][s]).then_inc(u_in[s], 16)

            def load_s(t, h):
                sp.dma_start(s_in, s_dram[ds(h, 1), :, ds(t, 1), :].squeeze(2).squeeze(0)
                             .rearrange("p (a b) -> p a b", a=2)).then_inc(s_load, 16)

            sp.wait_ge(s_out[0], 16 + 16)
            load_s(0, 0)
            for s in range(2):
                head_io(3, s, False)
            for s in range(2):
                sp.wait_ge(s_out[s], 16 + 64)

            def unit(U, prefetch, more_scores, piece=None):
                for s in range(2):
                    if prefetch:
                        sp.wait_ge(u_lo, U * 2 + (s + 1))
                        sp.dma_start(ur[:, s, :, :], io["uT"][ds(U * 2 + (s + 2), 1), :, :, :].squeeze(0)
                                     ).then_inc(u_in[s], 16)
                    if s == 0 and piece is not None:
                        store_g(*piece)
                    sp.wait_ge(gelu_ok, U * 4 + (2 * s + 2 + 4))
                    for half in range(2):
                        sp.dma_start(gel_dram[half][ds(U * 2 + s, 1), :, :].squeeze(0),
                                     gel[:, s, half * HALF:(half + 1) * HALF]).then_inc(gel_out[s], 16)
                    if s == 0 and more_scores:
                        sp.wait_ge(s_read, U + 2)
                        load_s((U + 2) // UNITS_T, (U + 2) % UNITS_T)

            def store_g(Tb, hb, piece):
                sp.wait_ge(g_ev, Tb * 32 + (hb * 16 + 16 + 2))
                sp.dma_start(g_dram[ds(Tb * 2 + hb, 1), :, ds(piece * 32, 32), :].squeeze(0),
                             Gst[:, hb, ds(piece * 32, 32), :]).then_inc(g_out[hb], 16)

            sp.wait_ge(s_read, 1)
            load_s(0, 1)
            with sp.Fori(0, UNITS_T) as U:
                unit(U, True, True)
            with sp.Fori(8, 12) as U:
                unit(U, True, True)
            with sp.Fori(0, 4) as q:
                unit(q + 12, True, True, (0, 0, q))
            with sp.Fori(2, TT - 1) as T:
                for hb in range(2):
                    with sp.Fori(0, 4) as q:
                        unit(T * 8 + (q + 4 * hb), True, True, (T - 2 + hb, 1 - hb, q))
            with sp.Fori(0, 4) as q:
                unit(q + 40, True, True, (3, 1, q))
            with sp.Fori(0, 2) as q:
                unit(q + 44, True, True, (4, 0, q))
            with sp.Fori(2, 4) as q:
                unit(q + 44, True, False, (4, 0, q))
            for hb in range(2):
                with sp.Fori(0, 4) as q:
                    unit(q + (48 + 4 * hb), True, False, (4 + hb, 1 - hb, q))
            with sp.Fori(0, 4) as q:
                unit(q + 56, True, False, (5, 1, q))
            with sp.Fori(60, 63) as U:
                unit(U, True, False)

            def expert_loads(p, i, xs_=range(8)):
                for x in xs_:
                    E = i * 8 + (128 * p + x)
                    e = i * 8 + x
                    if x % 4 == 0:
                        b = x // 4
                        sp.wait_ge(a_mul, E + 4)
                        sp.dma_start(G2[:, b, :, :],
                                     g_dram[6 * p:6 * p + 6, :, ds(e, 4), :].rearrange("b p e t -> p b (e t)")
                                     ).then_inc(G_in[b], 16)
                    sp.wait_ge(a_mul, E + 5)
                    sp.dma_start(gel2[:, x % 4, :], gel_dram[p][ds(e, 1), :, :].squeeze(0)).then_inc(gel_in[x % 4], 16)
                    sp.wait_ge(v_lo, E + 1)
                    sp.dma_start(vr[:, x % 4, :], io["v"][ds(e, 1), :, :].squeeze(0)).then_inc(v_in[x % 4], 16)

            sp.wait_ge(u_lo, 2 * 64)
            expert_loads(0, 0, range(4))
            unit(63, False, False)
            for s in range(2):
                sp.wait_ge(gel_out[s], 32 + 32 * 64)
            expert_loads(0, 0, range(4, 8))
            for t in range(TT):
                sp.dma_start(y[:, t, :], y_dram[t]).then_inc(y_in, 16)
            with sp.Fori(1, 16) as i:
                expert_loads(0, i)
            expert_loads(1, 0)
            sp.wait_ge(acc_ev, 6)
            for t in range(3):
                sp.dma_start(out_tiles[t], y[:, t, :]).then_inc(done, 16)
            with sp.Fori(1, 16) as i:
                expert_loads(1, i)
            for t in range(3, 6):
                sp.wait_ge(acc_ev, 2 * t + 2)
                sp.dma_start(out_tiles[t], y[:, t, :]).then_inc(done, 16)
            sp.wait_ge(done, 16 * TT)

        @block.scalar
        def _(act):
            act.sem_inc(exp_ok, 4)
            act.sem_inc(pt_ev, 2)
            act.sem_inc(q_ev, 2)
            act.sem_inc(z_ev, 6)
            act.sem_inc(qp_ev, 4)
            act.sem_inc(gelu_ok, 4)
            for s in range(2):
                act.sem_inc(gel_out[s], 32)
                act.sem_inc(g_out[s], 16)
                act.sem_inc(s_out[s], 16)
            act.wait_ge(small_in, 16 * len(smalls))
            for k in range(KD):
                act.wait_ge(xt_in[k], 16)
                nc.scalar.activation(FTh[:, k, :], xst[:, k, :], ACT.Copy, scale=g1[:, k:k + 1]).then_inc(ft_hi, 1)

            def w_split_hi(n):
                act.wait_ge(w_in[n % 2], 16 * (n // 2 + 1))
                if n >= 2:
                    act.wait_ge(w_used, n - 1)
                nc.scalar.activation(Wh[:, n % 2, :, :], Wr[:, n % 2, :, :], ACT.Copy).then_inc(w_hi, 1)

            w_split_hi(0)
            w_split_hi(1)
            act.wait_ge(x_in, 16 * TT)
            for t in range(TT):
                if t:
                    act.wait_ge(sq1, t)
                nc.scalar.activation(ps[:, 6:8, :], y[:, t, :].rearrange("p (a b) -> p a b", a=2), ACT.Square,
                                     accum_out=ss1[:, t:t + 1]).then_inc(sq1, 1)
            act.wait_ge(var1, 1)
            nc.scalar.activation(rs1, tmp6, ACT.Sqrt).then_inc(root1, 1)
            act.wait_ge(rstd1_ok, 1)

            def z_out(c):
                for t in range(TT):
                    act.wait_ge(z_mm, 6 * c + t + 1)
                    nc.scalar.activation(z[:, t, c * WC:(c + 1) * WC], ps[:, t, 0:WC], ACT.Copy,
                                         scale=rs1[:, t:t + 1]).then_inc(z_ev, 1)

            for c in range(N_WIN):
                z_out(c)
                w_split_hi(c + 2)
                if c == 3:
                    act.wait_ge(var10, 1)
                    nc.scalar.activation(rs10, tmp10, ACT.Sqrt).then_inc(root10, 1)

            def pooled_out(gi):
                for q, (t0, n) in enumerate(SEQ_TILES):
                    act.wait_ge(pool_mm, 2 * gi + q + 1)
                    if gi >= 2:
                        act.wait_ge(mix_mm, 2 * (gi - 2) + q + 1)
                    nc.scalar.activation(pooled[:, gi % 2, t0 * P:(t0 + n) * P], ps[:, q, 0:n * P],
                                         ACT.Copy).then_inc(pool_ev, 1)

            def mix_out(gi):
                for q, (t0, n) in enumerate(SEQ_TILES):
                    act.wait_ge(mix_mm, 2 * gi + q + 1)
                    nc.scalar.activation(FTh[:, 4 + gi, t0 * P:(t0 + n) * P], ps[:, 2 + q, 0:n * P], ACT.Copy,
                                         scale=pool_scale[:, gi:gi + 1]).then_inc(mix_hi, 1)

            pooled_out(0)
            for gi in range(1, 4):
                pooled_out(gi)
                mix_out(gi - 1)
            mix_out(3)
            act.wait_ge(k_tr, 1)
            nc.scalar.activation(kT[:, 0:512], ps[:, 4, :], ACT.Copy).then_inc(k_ev, 1)
            nc.scalar.activation(kT[:, 512:768], ps[:, 5, 0:256], ACT.Copy).then_inc(k_ev, 1)
            with act.Fori(0, 4) as j:
                act.wait_ge(q_tr, j + 2)
                nc.scalar.activation(qT[:, 0:512], ps[:, 0, :], ACT.Copy).then_inc(q_ev, 1)
                nc.scalar.activation(qT[:, 512:768], ps[:, 1, 0:256], ACT.Copy).then_inc(q_ev, 1)

                def pt_out(u):
                    q, hh, t, g = units[u]
                    n = SEQ_TILES[q][1]
                    if t == 0:
                        act.wait_ge(pv_mm, j * 4 + (g + 1))
                    act.wait_ge(p_tr, j * NU + (u + 5))
                    nc.scalar.activation(PT[:, g % 2, 0:n, t * P:(t + 1) * P],
                                         ps[:, 4 + u % 2, 0:n * P].rearrange("p (a b) -> p a b", a=n),
                                         ACT.Copy).then_inc(pt_ev, 1)

                def o_out(q):
                    t0, n = SEQ_TILES[q]
                    act.wait_ge(pv_mm, j * 4 + (2 * q + 4))
                    nc.scalar.activation(FTh[:, ds(j, 1), t0 * P:(t0 + n) * P].squeeze(1), ps[:, 6 + q, 0:n * P],
                                         ACT.Copy).then_inc(o_hi, 1)

                for u, (q, hh, t, g) in enumerate(units):
                    n = SEQ_TILES[q][1]
                    act.wait_ge(max_ok, j * NU + (u + 1))
                    act.wait_ge(p_tr, j * NU + (u + 1))
                    nc.scalar.activation(Pb[:, u % 4, 0:n * P], ps[:, u % 4, 0:n * P], ACT.Exp,
                                         bias=nmax[:, u:u + 1], accum_out=rsum[:, u:u + 1]).then_inc(exp_ok, 1)
                    if u >= 2:
                        pt_out(u - 2)
                    if u == 11:
                        o_out(0)
                pt_out(NU - 2)
                pt_out(NU - 1)
                o_out(1)
            for n in range(7, 11):
                w_split_hi(n)
            for t in range(TT):
                act.wait_ge(y_ev, 6 + 18 + t + 1)
                if t:
                    act.wait_ge(sq2, t)
                nc.scalar.activation(ps[:, 6:8, :], y[:, t, :].rearrange("p (a b) -> p a b", a=2), ACT.Square,
                                     accum_out=ss2[:, t:t + 1]).then_inc(sq2, 1)
            act.dma_start(y_dram.rearrange("t p d -> p t d"), y).then_inc(y_out, 16)
            act.wait_ge(var2, 1)
            nc.scalar.activation(rs2, tmp6, ACT.Sqrt).then_inc(root2, 1)
            act.wait_ge(rstd2_ok, 1)

            def scaled(t):
                if t >= 2:
                    act.wait_ge(xn_tr, t - 1)
                nc.scalar.activation(xs[:, t % 2, :], y[:, t, :], ACT.Copy, scale=rs2[:, t:t + 1]).then_inc(xs_ok, 1)

            scaled(0)
            for t in range(TT):
                if t + 1 < TT:
                    scaled(t + 1)
                for b in range(2):
                    act.wait_ge(xg_ok, 2 * t + b + 1)
                    nc.scalar.activation(FTh[:, 4 * b:4 * b + 4, t * P:(t + 1) * P],
                                         xgf[:, (2 * t + b) % 4, :].rearrange("p (a b) -> p a b", a=4), ACT.Copy).then_inc(xn_hi, 1)

            def head(i, s, more):
                h = i * 2 + s
                for n in range(4):
                    if n == 0:
                        act.wait_ge(s_mm, h * TT + TT)
                    act.wait_ge(qp_mm, h * 4 + (n + 1))
                    nc.scalar.activation(qpT[:, s, n % 2, (n // 2) * HALF:(n // 2 + 1) * HALF], ps[:, n, 0:HALF],
                                         ACT.Copy).then_inc(qp_ev, 1)
                if more:
                    act.wait_ge(w_in[(11 + s) % 2], i * 16 + 16 * ((11 + s) // 2 + 1))
                    act.wait_ge(w_used, h + 10)
                    nc.scalar.activation(Wh[:, (11 + s) % 2, :, :], Wr[:, (11 + s) % 2, :, :],
                                         ACT.Copy).then_inc(w_hi, 1)

            with act.Fori(0, 3) as i:
                for s in range(2):
                    head(i, s, True)
            head(3, 0, False)
            act.wait_ge(w_used, N_W - 1)
            for s in range(2):
                act.wait_ge(u_in[s], 16)
                nc.scalar.activation(uh[:, s, :, :], ur[:, s, :, :], ACT.Copy).then_inc(u_hi, 1)
            head(3, 1, False)

            def unit(U, Ub, prefetch, T=None):
                for s in range(2):
                    for half in range(2):
                        if half == 0:
                            act.wait_ge(gel_out[s], U * 32 + 32)
                        act.wait_ge(h_mm, U * 4 + (2 * s + half + 1))
                        nc.scalar.activation(gel[:, s, half * HALF:(half + 1) * HALF], ps[:, 2 * s + half, 0:HALF],
                                             ACT.Gelu).then_inc(gelu_ok, 1)
                        if half == 1 and prefetch:
                            act.wait_ge(u_in[s], U * 16 + 32)
                            nc.scalar.activation(uh[:, s, :, :], ur[:, s, :, :], ACT.Copy).then_inc(u_hi, 1)
                        if Ub is not None:
                            sg = 2 * s + half
                            act.wait_ge(g_mm, Ub * 4 + (sg + 3))
                            nc.scalar.activation(G_lo[:, sg % 2, :, :], G_ps[sg % 2][:, 1, :, :],
                                                 ACT.Copy).then_inc(g_part, 1)
                        if T is not None and s == half == 0:
                            act.wait_ge(ce_ok, T + 1)
                            nc.scalar.activation(CE, CE, ACT.Exp).then_inc(ce_exp, 1)

            with act.Fori(0, 7) as U:
                unit(U, None, True)
            unit(7, None, True, 0)
            act.wait_ge(y_out, 16)
            with act.Fori(1, TT) as T:
                for hb in range(2):
                    act.wait_ge(g_out[hb], T * 64 - 48)
                    with act.Fori(0, 4 - hb) as q:
                        unit(T * 8 + (q + 4 * hb), T * 8 + (q + (4 * hb - 8)), True)
                unit(T * 8 + 7, T * 8 - 1, True, T)
            for hb in range(2):
                act.wait_ge(g_out[hb], TT * 64 - 48)
                with act.Fori(0, 4) as q:
                    unit(q + (48 + 4 * hb), q + (40 + 4 * hb), True)
            with act.Fori(56, 63) as U:
                unit(U, None, True)

            def v_part(i, x):
                E = i * 8 + x
                act.wait_ge(v_mm, E + 1)
                act.wait_ge(v_in[x % 4], i * 32 + 16 * (x // 4 + 1))
                nc.scalar.activation(vh[:, x % 2, :], vr[:, x % 4, :], ACT.Copy).then_inc(v_hi, 1)

            def a_part(i, x):
                E = i * 8 + x
                act.wait_ge(v_mm, E + 1)
                act.wait_ge(a_mul, E + 9)
                nc.scalar.activation(Ah[:, x % 2, :], Aw[:, x % 2, :], ACT.Copy).then_inc(a_hi, 1)

            v_part(0, 0)
            v_part(0, 1)
            unit(63, None, False)
            for x in range(8):
                if x >= 2:
                    v_part(0, x)
                a_part(0, x)
            with act.Fori(1, 32) as i:
                for x in range(8):
                    v_part(i, x)
                    a_part(i, x)

        @block.gpsimd
        def _(pool):
            pool.sem_inc(a_mul, 8)
            nc.gpsimd.memset(zero_r[:, :].bitcast(F32), 0.0).then_inc(zero_ok, 1)
            steps = Steps(pool, rope_step)
            for t in range(TT):
                pool.wait_ge(zn_ok, t + 1)
                src = zn[:, t % 2, :].rearrange("p (g a i) -> p g a i", a=2, i=16)
                dst = qkr[:, t, :].rearrange("p (g a i) -> p g a i", a=2, i=16)
                ta = rt[:, 0, :].rearrange("p (h g i) -> p h g i", g=2, i=16)
                tb = rt[:, 1, :].rearrange("p (h g i) -> p h g i", g=2, i=16)
                c = cos[:, t, :, :].unsqueeze(1).to_broadcast([P, 10, 2, 16])
                s = sin[:, t, :, :].unsqueeze(1).to_broadcast([P, 10, 2, 16])

                def part(v, a):
                    return v[:, :, a, :].rearrange("p (h g) i -> p h g i", g=2)

                for first, second, op, o in ((c, s, ALU.subtract, 0), (s, c, ALU.add, 1)):
                    steps.did(nc.gpsimd.tensor_tensor(ta, part(src, 0), first, ALU.mult))
                    steps.step(nc.gpsimd.tensor_tensor(tb, part(src, 1), second, ALU.mult))
                    ins = nc.gpsimd.tensor_tensor(part(dst, o), ta, tb, op)
                    if o == 0:
                        steps.step(ins)
                    else:
                        ins.then_inc(rope_ok, 1)
                        pool.wait_ge(rope_ok, t + 1)
            with pool.Fori(0, 4) as j:
                pool.wait_ge(q_tr, j + 1)
                nc.gpsimd.tensor_copy(qj, qkr[:, :, ds(j * P, P)]).then_inc(q_sel, 1)

            def gate_one_hots(Tb, h):
                for sg in range(4):
                    pool.wait_ge(oh1_ok, Tb * 32 + (h * 4 + sg + 1))
                    nc.gpsimd.tensor_tensor(
                        oh_g[:, sg % 2, :, :, :], oh_1[:, sg % 2, :, :].unsqueeze(2).to_broadcast([P, SG, 2, P]),
                        par[:, ds(Tb % 2, 1), 2:4, ds(h * 16 + sg * SG, SG)].squeeze(1).rearrange("p c t -> p t c")
                        .unsqueeze(3).to_broadcast([P, SG, 2, P]), ALU.mult).then_inc(ohg_ok, 1)

            with pool.Fori(0, TT) as Tb:
                with pool.Fori(0, UNITS_T) as h:
                    gate_one_hots(Tb, h)
            with pool.Fori(0, 32) as i:
                for x in range(8):
                    E = i * 8 + x
                    pool.wait_ge(gel_in[x % 4], i * 32 + 16 * (x // 4 + 1))
                    if x % 4 == 0:
                        pool.wait_ge(G_in[x // 4], i * 16 + 16)
                    pool.wait_ge(a_lo, E + 1)
                    nc.gpsimd.tensor_tensor(
                        Aw[:, x % 2, :].rearrange("p (b t) -> p b t", t=BLK),
                        gel2[:, x % 4, :].rearrange("p (b t) -> p b t", t=BLK),
                        G2[:, x // 4, :, (x % 4) * BLK:(x % 4 + 1) * BLK], ALU.mult).then_inc(a_mul, 1)

        @block.vector
        def _(dve):
            dve.sem_inc(o_lo, 2)
            dve.sem_inc(y_ev, 6)
            dve.sem_inc(s_ev, 4)
            dve.sem_inc(g_ev, 2)
            dve.sem_inc(a_lo, 2)
            dve.sem_inc(v_lo, 4)
            tt, ts = nc.vector.tensor_tensor, nc.vector.tensor_scalar
            steps = Steps(dve, dve_step)
            dve.wait_ge(small_in, 16 * len(smalls))
            for k in range(KD):
                dve.wait_ge(ft_hi, k + 1)
                nc.vector.scalar_tensor_tensor(FTl[:, k, :], xst[:, k, :], g1[:, k:k + 1],
                                               FTh[:, k, :].bitcast(F32), ALU.mult, ALU.subtract).then_inc(ft_lo, 1)

            def w_split_lo(n):
                dve.wait_ge(w_hi, n + 1)
                tt(Wl[:, n % 2, :, :], Wr[:, n % 2, :, :], Wh[:, n % 2, :, :].bitcast(F32),
                   ALU.subtract).then_inc(w_lo, 1)

            def newton(r, root, a, tmp, ok):
                dve.wait_ge(root, 1)
                steps.step(nc.vector.reciprocal(r, r))
                steps.step(tt(tmp[1], r, r, ALU.mult))
                steps.step(tt(tmp[1], tmp[1], a, ALU.mult))
                steps.step(ts(tmp[1], tmp[1], -0.5, 1.5, ALU.mult, ALU.add))
                return tt(r, r, tmp[1], ALU.mult)

            w_split_lo(0)
            w_split_lo(1)
            dve.wait_ge(sq1, TT)
            ts(tmp6, ss1, 1.0 / D, EPS, ALU.mult, ALU.add).then_inc(var1, 1)
            newton(rs1, root1, tmp6, (None, ss1), None).then_inc(rstd1_ok, 1)
            for n in range(2, 5):
                w_split_lo(n)
            dve.wait_ge(z_ev, 6 + 18)
            for t in range(TT):
                steps.step(tt(zn[:, 0, :], z[:, t, 0:QK], z[:, t, 0:QK], ALU.mult))
                steps.step(nc.vector.tensor_reduce(ss10[:, 10 * t:10 * t + 10],
                                                   zn[:, 0, :].rearrange("p (h d) -> p h d", d=64), AX.X, ALU.add))
            ts(tmp10, ss10, 1.0 / 64, EPS, ALU.mult, ALU.add).then_inc(var10, 1)
            steps.step(newton(rs10, root10, tmp10, (None, ss10), None))
            rq = rs10.rearrange("p (t h) -> p t h", h=10)
            steps.step(ts(rq[:, :, 0:8], rq[:, :, 0:8], 0.125, None, ALU.mult))
            for t in range(TT):
                if t >= 2:
                    dve.wait_ge(rope_ok, t - 1)
                steps.step(tt(zn[:, t % 2, :].rearrange("p (h d) -> p h d", d=64),
                              z[:, t, 0:QK].rearrange("p (h d) -> p h d", d=64),
                              rs10[:, 10 * t:10 * t + 10].unsqueeze(2).to_broadcast([P, 10, 64]), ALU.mult))
                tt(zn[:, t % 2, :], zn[:, t % 2, :], gqk, ALU.mult).then_inc(zn_ok, 1)
            w_split_lo(5)
            w_split_lo(6)
            for gi in range(4):
                for q, (t0, n) in enumerate(SEQ_TILES):
                    dve.wait_ge(mix_hi, 2 * gi + q + 1)
                    nc.vector.scalar_tensor_tensor(
                        FTl[:, 4 + gi, t0 * P:(t0 + n) * P], ps[:, 2 + q, 0:n * P], pool_scale[:, gi:gi + 1],
                        FTh[:, 4 + gi, t0 * P:(t0 + n) * P].bitcast(F32), ALU.mult, ALU.subtract).then_inc(mix_lo, 1)
            steps.rewind()
            with dve.Fori(0, 4) as j:

                def row_max(u):
                    n = SEQ_TILES[units[u][0]][1]
                    dve.wait_ge(qk_mm, j * NU + (u + 1))
                    nc.vector.tensor_reduce(nmax[:, u:u + 1], ps[:, u % 4, 0:n * P], AX.X, ALU.max,
                                            negate=True).then_inc(max_ok, 1)

                def o_rest(q):
                    t0, n = SEQ_TILES[q]
                    dve.wait_ge(o_hi, j * 2 + (q + 1))
                    tt(FTl[:, ds(j, 1), t0 * P:(t0 + n) * P].squeeze(1), ps[:, 6 + q, 0:n * P],
                       FTh[:, ds(j, 1), t0 * P:(t0 + n) * P].squeeze(1).bitcast(F32), ALU.subtract).then_inc(o_lo, 1)

                row_max(0)
                row_max(1)
                for u, (q, hh, t, g) in enumerate(units):
                    n = SEQ_TILES[q][1]
                    if u + 2 < NU:
                        row_max(u + 2)
                    dve.wait_ge(exp_ok, j * NU + (u + 5))
                    steps.step(nc.vector.reciprocal(rrec[:, u:u + 1], rsum[:, u:u + 1]))
                    ts(Pb[:, u % 4, 0:n * P], Pb[:, u % 4, 0:n * P], rrec[:, u:u + 1], None,
                       ALU.mult).then_inc(p_ok, 1)
                o_rest(0)
                o_rest(1)
                steps.rewind()
            dve.wait_ge(xr_in, 16 * TT)
            for c in range(N_WOUT):
                for t in range(TT):
                    dve.wait_ge(y_mm, 6 * c + t + 1)
                    tt(y[:, t, c * WC:(c + 1) * WC], y[:, t, c * WC:(c + 1) * WC], ps[:, t, 0:WC],
                       ALU.add).then_inc(y_ev, 1)
                w_split_lo(7 + c)
            dve.wait_ge(sq2, TT)
            ts(tmp6, ss2, 1.0 / D, EPS, ALU.mult, ALU.add).then_inc(var2, 1)
            newton(rs2, root2, tmp6, (None, ss2), None).then_inc(rstd2_ok, 1)
            def gained(t):
                for b in range(2):
                    dve.wait_ge(xn_tr, t + 1)
                    if t >= 2:
                        dve.wait_ge(xn_lo, 2 * (t - 2) + b + 1)
                    tt(xgf[:, (2 * t + b) % 4, :].rearrange("p (a b) -> p a b", a=4),
                       ps[:, 2 * (t % 4) + b, :].rearrange("p (a b) -> p a b", a=4),
                       g2[:, 4 * b:4 * b + 4].unsqueeze(2).to_broadcast([P, 4, P]), ALU.mult).then_inc(xg_ok, 1)

            gained(0)
            for t in range(TT):
                if t + 1 < TT:
                    gained(t + 1)
                for b in range(2):
                    dve.wait_ge(xn_hi, 2 * t + b + 1)
                    tt(FTl[:, 4 * b:4 * b + 4, t * P:(t + 1) * P],
                       xgf[:, (2 * t + b) % 4, :].rearrange("p (a b) -> p a b", a=4),
                       FTh[:, 4 * b:4 * b + 4, t * P:(t + 1) * P].bitcast(F32), ALU.subtract).then_inc(xn_lo, 1)

            def head(i, s, more):
                h = i * 2 + s
                dve.wait_ge(s_out[s], i * 16 + 16)
                for t in range(TT):
                    if t == 3 and more:
                        dve.wait_ge(w_hi, h + 12)
                        tt(Wl[:, (11 + s) % 2, :, :], Wr[:, (11 + s) % 2, :, :], Wh[:, (11 + s) % 2, :, :].bitcast(F32),
                           ALU.subtract).then_inc(w_lo, 1)
                    dve.wait_ge(s_mm, h * TT + (t + 13))
                    nc.vector.tensor_copy(s_sb[:, s, t, :], ps[:, 4 + (6 * s + t) % 4, 0:256]).then_inc(s_ev, 1)

            with dve.Fori(0, 3) as i:
                for s in range(2):
                    head(i, s, True)
            def u_split_lo(e1, s):
                dve.wait_ge(u_hi, e1)
                tt(ul[:, s, :, :], ur[:, s, :, :], uh[:, s, :, :].bitcast(F32), ALU.subtract).then_inc(u_lo, 1)

            def one_hot(Tb, h, sg, which, dst, ok):
                dve.wait_ge(g_mm, Tb * 32 + (h * 4 + sg + 1))
                tt(dst[:, sg % 2, :, :], iota[:, :].unsqueeze(1).to_broadcast([P, SG, P]),
                   par[:, ds(Tb % 2, 1), which, ds(h * 16 + sg * SG, SG)].squeeze(1)
                   .unsqueeze(2).to_broadcast([P, SG, P]), ALU.is_equal).then_inc(ok, 1)

            def add_G(Tb, h, sg):
                dve.wait_ge(g_part, Tb * 32 + (h * 4 + sg + 1))
                tt(Gst[:, ds(h // 4, 1), :, ds((h % 4) * 16 + sg * SG, SG)].squeeze(1),
                   G_ps[sg % 2][:, 0, :, :].rearrange("p t i -> p i t"),
                   G_lo[:, sg % 2, :, :].rearrange("p t i -> p i t"), ALU.add).then_inc(g_ev, 1)

            def unit(U, Tb, h, topk, prefetch, T=None, following=None, split=True):
                if T is not None:
                    tt(CE, CV, CV[:, :, 0:1].to_broadcast([P, HEADS, TOPK]), ALU.subtract).then_inc(ce_ok, 1)
                if Tb is not None:
                    one_hot(Tb, h, 1, 0, oh_1, oh1_ok)
                if split:
                    u_split_lo(U * 2 + 2, 1)
                if Tb is not None:
                    one_hot(Tb, h, 1, 1, oh_2, oh2_ok)
                if T is not None:
                    dve.wait_ge(ce_ok, T + 1)
                if topk:
                    dve.wait_ge(s_load, 16)
                    dve.sem_inc(s_load, -16)
                    for p in range(2):
                        steps.did(nc.vector.max(sv[:, p, 0:8], s_in[:, p, :]))
                    steps.settle()
                    for p in range(2):
                        steps.did(nc.vector.max_index(si_u[:, p, 0:8], sv[:, p, 0:8], s_in[:, p, :]))
                        steps.did(nc.vector.match_replace(s_cut[:, p, :], sv[:, p, 0:8], s_in[:, p, :], LOWEST))
                if Tb is not None:
                    one_hot(Tb, h, 2, 0, oh_1, oh1_ok)
                    add_G(Tb, h, 0)
                if topk:
                    steps.settle()
                    dve.sem_inc(s_read, 1)
                    for p in range(2):
                        steps.did(nc.vector.max(sv[:, p, 8:16], s_cut[:, p, :]))
                if Tb is not None:
                    one_hot(Tb, h, 2, 1, oh_2, oh2_ok)
                if topk:
                    steps.settle()
                    for p in range(2):
                        steps.did(nc.vector.max_index(si_u[:, p, 8:16], sv[:, p, 8:16], s_cut[:, p, :]))
                    steps.did(tt(comb.rearrange("p (a b) -> p a b", a=TOPK),
                                 sv[:, 0, :].unsqueeze(2).to_broadcast([P, TOPK, TOPK]),
                                 sv[:, 1, :].unsqueeze(1).to_broadcast([P, TOPK, TOPK]), ALU.add))
                    steps.settle()
                    steps.did(nc.vector.max(cvh[:, 0:8], comb))
                    steps.did(nc.vector.tensor_copy(sif, si_u))
                if T is not None:
                    dve.wait_ge(ce_exp, T + 1)
                    steps.step(nc.vector.tensor_reduce(ssum8, CE, AX.X, ALU.add))
                    steps.step(nc.vector.reciprocal(srec8, ssum8))
                    tt(CE, CE, srec8.unsqueeze(2).to_broadcast([P, HEADS, TOPK]), ALU.mult).then_inc(gate_ok, 1)
                if Tb is not None:
                    one_hot(Tb, h, 3, 0, oh_1, oh1_ok)
                    add_G(Tb, h, 1)
                if topk:
                    steps.settle()
                    steps.did(nc.vector.max_index(ci_u[:, 0:8], cvh[:, 0:8], comb))
                    steps.did(nc.vector.match_replace(comb_cut, cvh[:, 0:8], comb, LOWEST))
                if prefetch:
                    u_split_lo(U * 2 + 3, 0)
                if Tb is not None:
                    one_hot(Tb, h, 3, 1, oh_2, oh2_ok)
                if topk:
                    steps.settle()
                    steps.step(nc.vector.max(cvh[:, 8:16], comb_cut))
                    steps.did(nc.vector.max_index(ci_u[:, 8:16], cvh[:, 8:16], comb_cut))
                    steps.did(nc.vector.tensor_copy(CV[:, ds((U + 1) % UNITS_T, 1), :].squeeze(1), cvh))
                    steps.settle()
                    steps.did(ts(jj_u[:, 0, :], ci_u, 4, None, ALU.logical_shift_right))
                    steps.step(ts(jj_u[:, 1, :], ci_u, 15, None, ALU.bitwise_and))
                    steps.step(nc.vector.tensor_copy(jf, jj_u))
                    steps.did(tt(eq, jf.unsqueeze(3).to_broadcast([P, 2, TOPK, TOPK]),
                                 iota[:, 0:TOPK].unsqueeze(1).unsqueeze(1).to_broadcast([P, 2, TOPK, TOPK]),
                                 ALU.is_equal))
                if T is not None:
                    dve.wait_ge(par_tr, T + 1)
                    nc.vector.tensor_copy(par[:, ds(T % 2, 1), 0:3, :].squeeze(1),
                                          ps[:, 6, 0:384].rearrange("p (a b) -> p a b", a=3)).then_inc(par_ev, 1)
                    dve.wait_ge(par_ev, T + 1)
                    steps.step(nc.vector.tensor_copy(gate_r[:, :], par[:, ds(T % 2, 1), 2, :].squeeze(1)))
                    steps.step(tt(par[:, ds(T % 2, 1), 3, :].squeeze(1), par[:, ds(T % 2, 1), 2, :].squeeze(1),
                                  gate_r[:, :].bitcast(F32), ALU.subtract))
                if following is not None:
                    one_hot(*following, 0, 0, oh_1, oh1_ok)
                if Tb is not None:
                    add_G(Tb, h, 2)
                if topk:
                    steps.settle()
                    steps.did(tt(eq, eq, sif.unsqueeze(2).to_broadcast([P, 2, TOPK, TOPK]), ALU.mult))
                if following is not None:
                    one_hot(*following, 0, 1, oh_2, oh2_ok)
                if topk:
                    steps.settle()
                    steps.did(nc.vector.tensor_reduce(IDX[:, :, ds(((U + 1) % UNITS_T) * TOPK, TOPK)], eq, AX.X,
                                                      ALU.add))
                if Tb is not None:
                    add_G(Tb, h, 3)
                if topk or T is not None:
                    steps.rewind()

            head(3, 0, False)
            u_split_lo(1, 0)
            steps.rewind()
            unit(-1, None, None, True, False, split=False)
            head(3, 1, False)
            with dve.Fori(0, 7) as U:
                unit(U, None, None, True, True)
            unit(7, None, None, True, True, 0, following=(0, 0))
            with dve.Fori(1, TT - 1) as T:
                with dve.Fori(0, 7) as h:
                    unit(T * 8 + h, T - 1, h, True, True, following=(T - 1, h + 1))
                unit(T * 8 + 7, T - 1, 7, True, True, T, following=(T, 0))
            with dve.Fori(0, 7) as h:
                unit(h + 40, 4, h, True, True, following=(4, h + 1))
            unit(47, 4, 7, False, True, 5, following=(5, 0))
            with dve.Fori(0, 7) as h:
                unit(h + 48, 5, h, False, True, following=(5, h + 1))
            unit(55, 5, 7, False, True)
            with dve.Fori(56, 63) as U:
                unit(U, None, None, False, True)
            unit(63, None, None, False, False)
            for p in range(2):
                with dve.Fori(16 * p, 16 * p + 16) as i:
                    for x in range(8):
                        E = i * 8 + x
                        dve.wait_ge(v_hi, E + 1)
                        tt(vl[:, x % 2, :], vr[:, x % 4, :], vh[:, x % 2, :].bitcast(F32),
                           ALU.subtract).then_inc(v_lo, 1)
                        dve.wait_ge(a_hi, E + 1)
                        tt(Al[:, x % 2, :], Aw[:, x % 2, :], Ah[:, x % 2, :].bitcast(F32),
                           ALU.subtract).then_inc(a_lo, 1)
                if p == 0:
                    dve.wait_ge(y_in, 16 * TT)
                dve.wait_ge(acc_done, p + 1)
                for n in range(6):
                    t, dh = 3 * p + n // 2, n % 2
                    tt(y[:, t, dh * 512:(dh + 1) * 512], y[:, t, dh * 512:(dh + 1) * 512], ps[:, n, :],
                       ALU.add).then_inc(acc_ev, 1)

        @block.tensor
        def _(pe):
            mm = nc.tensor.matmul
            pe.sem_inc(q_tr, 1)
            pe.sem_inc(p_tr, 4)
            pe.sem_inc(pv_mm, 2)
            pe.sem_inc(s_mm, 12)
            pe.sem_inc(g_mm, 2)
            pe.sem_inc(v_mm, 2)
            pe.wait_ge(ft_lo, KD)
            with pe.Fori(0, N_WIN) as c:
                pe.wait_ge(w_lo, c + 1)
                for t in range(TT):
                    pe.wait_ge(z_ev, c * 6 + (t + 1))
                    for k in range(KD):
                        last = pe_split_product(
                            ps[:, t, 0:WC], FTh[:, k, t * P:(t + 1) * P], FTl[:, k, t * P:(t + 1) * P],
                            Wh[:, ds(c % 2, 1), k, :].squeeze(1), Wl[:, ds(c % 2, 1), k, :].squeeze(1),
                            k == 0, k == KD - 1)
                    last.then_inc(z_mm, 1)
                pe.wait_ge(z_mm, c * 6 + 6)
                pe.sem_inc(w_used, 1)

            def windows(gi):
                pe.wait_ge(band_in[gi % 2], 16 * (gi // 2 + 1))
                for q, (t0, n) in enumerate(SEQ_TILES):
                    if gi:
                        pe.wait_ge(pool_ev, 2 * (gi - 1) + q + 1)
                    for t in range(n):
                        srcs = [(s, 3 if s < t else 4 if s > t else 0 if t == 0 else 2 if t == n - 1 else 1)
                                for s in range(max(t - 1, 0), min(t + 2, n))]
                        for m, (s, kind) in enumerate(srcs):
                            last = mm(ps[:, q, t * P:(t + 1) * P],
                                      z[:, t0 + s, POOL_COL + gi * P:POOL_COL + (gi + 1) * P],
                                      band[:, gi % 2, kind, :], start=m == 0, stop=m == len(srcs) - 1)
                    last.then_inc(pool_mm, 1)

            def group_map(gi):
                for q, (t0, n) in enumerate(SEQ_TILES):
                    pe.wait_ge(pool_ev, 2 * gi + q + 1)
                    if gi:
                        pe.wait_ge(mix_lo, 2 * (gi - 1) + q + 1)
                    mm(ps[:, 2 + q, 0:n * P], poolw[:, gi * P:(gi + 1) * P],
                       pooled[:, gi % 2, t0 * P:(t0 + n) * P], start=True, stop=True).then_inc(mix_mm, 1)

            pe.wait_ge(z_ev, 6 + 30)
            windows(0)
            for gi in range(1, 4):
                windows(gi)
                group_map(gi - 1)
            group_map(3)
            pe.wait_ge(rope_ok, TT)
            for t in range(TT):
                last = nc.tensor.transpose(ps[:, 4 + t // 4, (t % 4) * P:(t % 4 + 1) * P], qkr[:, t, K_COL:K_COL + P],
                                           ident[:, :])
            last.then_inc(k_tr, 1)
            pe.wait_ge(k_ev, 2)
            pe.wait_ge(mix_lo, 8)
            with pe.Fori(0, 4) as j:
                pe.wait_ge(q_sel, j + 1)
                pe.wait_ge(q_ev, j * 2 + 2)
                pe.wait_ge(exp_ok, j * NU + 4)
                for t in range(TT):
                    last = nc.tensor.transpose(ps[:, t // 4, (t % 4) * P:(t % 4 + 1) * P], qj[:, t, :], ident[:, :])
                last.then_inc(q_tr, 1)
                pe.wait_ge(q_ev, j * 2 + 4)

                def scores(u):
                    q, hh, t, g = units[u]
                    t0, n = SEQ_TILES[q]
                    pe.wait_ge(exp_ok, j * NU + (u + 1))
                    mm(ps[:, u % 4, 0:n * P], qT[64 * hh:64 * hh + 64, (t0 + t) * P:(t0 + t + 1) * P],
                       kT[64 * hh:64 * hh + 64, t0 * P:(t0 + n) * P], start=True, stop=True).then_inc(qk_mm, 1)

                def flip(u):
                    q, hh, t, g = units[u]
                    n = SEQ_TILES[q][1]
                    pe.wait_ge(p_ok, j * NU + (u + 1))
                    pe.wait_ge(pt_ev, j * NU + (u + 1))
                    for s in range(n):
                        last = nc.tensor.transpose(ps[:, 4 + u % 2, s * P:(s + 1) * P],
                                                   Pb[:, u % 4, s * P:(s + 1) * P], ident[:, :])
                    last.then_inc(p_tr, 1)

                def values(g):
                    q, hh, t0, n, u_last = groups[g]
                    pe.wait_ge(pt_ev, j * NU + (u_last + 3))
                    pe.wait_ge(o_lo, j * 2 + (q + 1))
                    for s in range(n):
                        last = mm(ps[64 * hh:64 * hh + 64, 6 + q, 0:n * P],
                                  z[:, t0 + s, V_COL + 64 * hh:V_COL + 64 * hh + 64],
                                  PT[:, g % 2, s, 0:n * P], start=s == 0, stop=s == n - 1)
                    last.then_inc(pv_mm, 1)

                for u in range(3):
                    scores(u)
                for u in range(NU):
                    if u + 3 < NU:
                        scores(u + 3)
                    flip(u)
                    for g, grp in enumerate(groups):
                        if grp[4] == u - 1:
                            values(g)
                values(3)
            pe.wait_ge(o_lo, 2 + 8)
            with pe.Fori(0, N_WOUT) as c:
                pe.wait_ge(w_lo, c + 6)
                for t in range(TT):
                    pe.wait_ge(y_ev, c * 6 + (t + 1))
                    for k in range(KD):
                        last = pe_split_product(
                            ps[:, t, 0:WC], FTh[:, k, t * P:(t + 1) * P], FTl[:, k, t * P:(t + 1) * P],
                            Wh[:, ds((c + 1) % 2, 1), k, :].squeeze(1), Wl[:, ds((c + 1) % 2, 1), k, :].squeeze(1),
                            k == 0, k == KD - 1)
                    last.then_inc(y_mm, 1)
                pe.wait_ge(y_mm, c * 6 + 6)
                pe.sem_inc(w_used, 1)
            pe.wait_ge(y_ev, 6 + 24)
            for t in range(TT):
                pe.wait_ge(xs_ok, t + 1)
                if t >= 4:
                    pe.wait_ge(xg_ok, 2 * (t - 3))
                for k in range(KD):
                    last = nc.tensor.transpose(ps[:, 2 * (t % 4) + k // 4, (k % 4) * P:(k % 4 + 1) * P],
                                               xs[:, t % 2, k * P:(k + 1) * P], ident[:, :])
                last.then_inc(xn_tr, 1)
            pe.wait_ge(xg_ok, 12)
            pe.wait_ge(sk_in, 16)
            def key_scores(h, s, ts_):
                for t in ts_:
                    pe.wait_ge(s_ev, h * TT + (t + 1))
                    for p in range(2):
                        last = mm(ps[:, 4 + (6 * s + t) % 4, p * P:(p + 1) * P], qpT[:, s, p, t * P:(t + 1) * P],
                                  skT[:, ds(h * 2 + p, 1), :].squeeze(1), start=True, stop=True)
                    last.then_inc(s_mm, 1)

            def late_scores(h, s):
                pe.wait_ge(qp_mm, h * 4 + 4)
                pe.sem_inc(w_used, 1)
                pe.wait_ge(qp_ev, h * 4 + 8)
                key_scores(h, s, range(3, TT))

            def head(h, s, first=False):
                ws = (9 + s) % 2
                pe.wait_ge(w_lo, h + 10)
                for n in range(4):
                    half, p = n // 2, n % 2
                    pe.wait_ge(xn_lo, 6 + 6 * half)
                    pe.wait_ge(qp_ev, h * 4 + (n + 1))
                    for k in range(KD):
                        last = pe_split_product(
                            ps[:, n, 0:HALF], Wh[:, ws, k, p * P:(p + 1) * P], Wl[:, ws, k, p * P:(p + 1) * P],
                            FTh[:, k, half * HALF:(half + 1) * HALF], FTl[:, k, half * HALF:(half + 1) * HALF],
                            k == 0, k == KD - 1)
                    last.then_inc(qp_mm, 1)
                    if n == 0 and not first:
                        late_scores(h - 1, 1 - s)
                    if n == 2:
                        pe.wait_ge(qp_ev, h * 4 + 6)
                        key_scores(h, s, range(3))

            head(0, 0, True)
            head(1, 1)
            with pe.Fori(1, 4) as i:
                for s in range(2):
                    head(i * 2 + s, s)
            late_scores(7, 1)

            def unit(U, Tb, h, T=None):
                for s in range(2):
                    for half in range(2):
                        if half == 0:
                            pe.wait_ge(u_lo, U * 2 + (s + 1))
                        pe.wait_ge(gelu_ok, U * 4 + (2 * s + half + 1))
                        for k in range(KD):
                            last = pe_split_product(
                                ps[:, 2 * s + half, 0:HALF], uh[:, s, k, :], ul[:, s, k, :],
                                FTh[:, k, half * HALF:(half + 1) * HALF], FTl[:, k, half * HALF:(half + 1) * HALF],
                                k == 0, k == KD - 1)
                        last.then_inc(h_mm, 1)
                        if Tb is not None:
                            sg = 2 * s + half
                            Q = Tb * 32 + h * 4 + sg
                            pe.wait_ge(oh2_ok, Q + 1)
                            pe.wait_ge(ohg_ok, Q + 1)
                            pe.wait_ge(g_ev, Q + 1)
                            if T is not None and sg == 3:
                                pe.wait_ge(par_ev, T + 1)
                            for n in range(SG):
                                last = mm(ps[:, 4 + 2 * (sg % 2) + n // 2, (n % 2) * 256:(n % 2 + 1) * 256],
                                          oh_2[:, sg % 2, n, :], oh_g[:, sg % 2, n, :, :], start=True, stop=True)
                            last.then_inc(g_mm, 1)
                        if T is not None and s == 1 and half == 0:
                            pe.wait_ge(gate_ok, T + 1)
                            if Tb is not None:
                                pe.wait_ge(g_ev, Tb * 32 + h * 4 + 4)
                            for n in range(2):
                                nc.tensor.transpose(ps[:, 6, n * P:(n + 1) * P], IDX[:, n, :], ident[:, :])
                            nc.tensor.transpose(ps[:, 6, 2 * P:3 * P], B_[:, 3584:3712], ident[:, :]
                                                ).then_inc(par_tr, 1)

            with pe.Fori(0, 7) as U:
                unit(U, None, None)
            unit(7, None, None, 0)
            with pe.Fori(1, TT) as T:
                with pe.Fori(0, 7) as h:
                    unit(T * 8 + h, T - 1, h)
                unit(T * 8 + 7, T - 1, 7, T)
            with pe.Fori(0, UNITS_T) as h:
                unit(h + 48, TT - 1, h)
            with pe.Fori(56, 64) as U:
                unit(U, None, None)
            pe.wait_ge(zero_ok, 1)
            pe.wait_ge(gelu_ok, 4 + 256)
            for p in range(2):
                if p:
                    pe.wait_ge(acc_ev, 6)
                for n in range(6):
                    mm(ps[:, n, :], zero_r[:, :], FTh[:, 0, 0:512], start=True, stop=False, skip_group_check=True)
                with pe.Fori(16 * p, 16 * p + 16) as i:
                    for x in range(8):
                        E = i * 8 + x
                        pe.wait_ge(v_lo, E + 5)
                        pe.wait_ge(a_lo, E + 3)
                        for t in range(3):
                            for dh in range(2):
                                out = ps[:, 2 * t + dh, :]
                                ah, al = (a[:, x % 2, t * P:(t + 1) * P] for a in (Ah, Al))
                                bh, bl = (b[:, x % 2, dh * 512:(dh + 1) * 512] for b in (vh, vl))
                                mm(out, ah, bh, start=False, stop=False, skip_group_check=True)
                                mm(out, ah, bl, start=False, stop=False, skip_group_check=True)
                                last = mm(out, al, bh, start=False, stop=False, skip_group_check=True)
                        last.then_inc(v_mm, 1)
                for n in range(6):
                    last = mm(ps[:, n, :], zero_r[:, :], FTh[:, 0, 0:512], start=False, stop=True, skip_group_check=True)
                last.then_inc(acc_done, 1)


def tables():
    f = np.float32
    pos = np.concatenate([np.arange(n * P) for _, n in SEQ_TILES])
    inv = (f(1.0) / (f(ROPE_THETA) ** (np.arange(0, ROPE_HALF, 2, dtype=f) / f(ROPE_HALF)))).astype(f)
    ang = np.stack([(pos // GRID_W).astype(f)[:, None] * inv, (pos % GRID_W).astype(f)[:, None] * inv], 1)
    rope = np.stack([np.cos(ang), np.sin(ang)]).astype(f).reshape(2, TT, P, 32).transpose(2, 0, 1, 3).reshape(P, -1)
    band = np.zeros((4, P, 5, P), f)
    n = 3 * P
    for g, w in enumerate(WINDOWS):
        m = np.zeros((n, n), f)
        for t in range(n):
            lo, hi = max(t - w // 2, 0), min(t + w - w // 2, n)
            m[lo:hi, t] = f(1.0) / f(hi - lo)
            m[t, t] -= f(1.0)
        blocks = {0: (0, 0), 1: (1, 1), 2: (2, 2), 3: (0, 1), 4: (1, 0)}
        for kind, (a, b) in blocks.items():
            band[g, :, kind] = m[a * P:(a + 1) * P, b * P:(b + 1) * P]
    return dict(ident=np.eye(P, dtype=f), iota=np.tile(np.arange(P, dtype=f), (P, 1)),
                rope=np.ascontiguousarray(rope), band=band)


def kernel(**inputs):
    import concourse.bacc as bacc
    from concourse.bass_utils import run_bass_kernel_spmd as run

    a = {k: np.asarray(v) for k, v in inputs.items()}
    heads = [0, 4, 1, 5, 2, 6, 3, 7]
    w = a["w_in"][0]
    w_q = w[:, 512:1024].reshape(D, 8, 64)[:, heads].reshape(D, 512)
    w_in = np.concatenate([w_q, w[:, 1024:1280], w[:, 0:512]], 1)
    wo = a["w_out"][0]
    wo = np.concatenate([wo[512:1024].reshape(8, 64, D)[heads].reshape(512, D), wo[0:512]], 0)
    w_all = np.concatenate([w_in, wo, a["peer_wq"][0]], 1)
    x = np.concatenate([a["x_prompt"][0], a["x_sample"][0]], 0)
    data = dict(
        x_prompt=a["x_prompt"], x_sample=a["x_sample"],
        xT=x.T.reshape(KD, P, TOK).transpose(1, 0, 2),
        vecs=np.concatenate([a["norm1_g"][0].reshape(8, P).T, a["norm2_g"][0].reshape(8, P).T,
                             a["pool_scale"][0].reshape(4, P).T], 1),
        gqk=np.concatenate([np.tile(a["q_norm_g"][0], 8), np.tile(a["k_norm_g"][0], 2)]),
        pool_w=a["pool_w"][0].transpose(1, 0, 2).reshape(P, 4 * P),
        w_all=w_all.reshape(KD, P, N_W, WC).transpose(2, 1, 0, 3),
        skT=a["peer_subkeys"][0].transpose(3, 0, 1, 2).reshape(P, 16, P),
        uT=a["peer_u"][0].reshape(NK, P, KD, P).transpose(0, 3, 2, 1),
        v=a["peer_v"][0].reshape(NK, P, D),
        **tables(),
    )
    data = {k: np.ascontiguousarray(v) for k, v in data.items()}
    nc = bacc.Bacc("TRN2", target_bir_lowering=False, num_devices=1)
    f32 = mybir.dt.float32
    io = {k: nc.dram_tensor("in_" + k, v.shape, f32, kind="ExternalInput").ap() for k, v in data.items()}
    scratch = dict(s_dram=(HEADS, P, TT, 256), g_dram=(NBLK, P, NK, BLK), gel_dram=(2, NK, P, HALF), y_dram=(TT, P, D))
    io.update({k: nc.dram_tensor(k, s, f32, kind="Internal").ap() for k, s in scratch.items()})
    outs = dict(y_prompt=(1, 512, D), y_sample=(1, 256, D))
    io.update({k: nc.dram_tensor(k, s, f32, kind="ExternalOutput").ap() for k, s in outs.items()})
    build(nc, io)
    r = run(nc, [{"in_" + k: v for k, v in data.items()}], core_ids=[0])
    return tuple(r.results[0][k] for k in outs)
```

```python
import numpy as np
from contextlib import ExitStack
import concourse.bass as bass
from concourse import mybir

P = 128
D = 1024
KD = D // P
SEQ_TILES = ((0, 4), (4, 2))
TT = 6
TOK = TT * P
HALF = TOK // 2
WC = 256
N_WIN, N_WOUT, HEADS = 5, 4, 8
N_W = N_WIN + N_WOUT + HEADS
QK = 640
K_COL, V_COL, POOL_COL = 512, 640, 768
ZW = 1280
NK = 128
TOPK = 16
EPS = 1e-6
LOWEST = -3.4028234663852886e38
GRID_W, ROPE_HALF, ROPE_THETA = 64, 32, 10000.0
WINDOWS = (2, 4, 8, 16)
UNITS_T = 8
PAIR = 2
SG = 4
NBLK = 12
BLK = 64
VB = 4
N_VB = NK // VB


class Steps:

    def __init__(self, eng, sem):
        self.eng, self.sem, self.n = eng, sem, 0

    def did(self, instruction):
        instruction.then_inc(self.sem, 1)
        self.n += 1
        return self.n

    def settle(self):
        self.eng.wait_ge(self.sem, self.n)

    def step(self, instruction):
        self.did(instruction)
        self.settle()

    def rewind(self):
        self.settle()
        self.eng.sem_inc(self.sem, -self.n)
        self.n = 0


def build(nc, io):
    F32, F32R, U32 = mybir.dt.float32, mybir.dt.float32r, mybir.dt.uint32
    ALU, ACT, AX = mybir.AluOpType, mybir.ActivationFunctionType, mybir.AxisListType
    ds = bass.ds
    ctx = ExitStack()
    with ctx:
        def sb(name, words, dt=F32):
            return ctx.enter_context(nc.sbuf_tensor(name, [P, words], dt))

        def sem(name):
            return ctx.enter_context(nc.semaphore(name))

        FTh_ = sb("feat_hi", KD * TOK, F32R)
        FTl_ = sb("feat_lo", KD * TOK, F32R)
        Wr_ = sb("w_raw", 2 * KD * WC)
        Wh_ = sb("w_hi", 2 * KD * WC, F32R)
        Wl_ = sb("w_lo", 2 * KD * WC, F32R)
        A_ = sb("arena_a", 17664)
        B_ = sb("arena_b", 5760)
        KV_ = sb("keys_values", 2 * TOK + 2 * TT * 192, F32R)
        vecs = sb("vecs", 20)
        ident = sb("ident", P)
        iota = sb("iota", P)
        poolw = sb("poolw", 4 * P)
        st = sb("stats", 384)
        iu = sb("index_u32", 96, U32)
        ps = ctx.enter_context(nc.psum_tensor("ps", [P, 8, 512], F32))

        def view(buf, at, *shape):
            n = int(np.prod(shape))
            v = buf[:, at:at + n]
            if len(shape) == 2:
                return v.rearrange("p (a b) -> p a b", a=shape[0])
            if len(shape) == 3:
                return v.rearrange("p (a b c) -> p a b c", a=shape[0], b=shape[1])
            if len(shape) == 4:
                return v.rearrange("p (a b c d) -> p a b c d", a=shape[0], b=shape[1], c=shape[2])
            return v

        FTh, FTl = view(FTh_, 0, KD, TOK), view(FTl_, 0, KD, TOK)
        Wr, Wh, Wl = (view(w, 0, 2, KD, WC) for w in (Wr_, Wh_, Wl_))
        g1, g2, pool_scale = vecs[:, 0:8], vecs[:, 8:16], vecs[:, 16:20]
        y = view(A_, 0, TT, D)
        z = view(A_, 6144, TT, ZW)
        qkr = view(A_, 13824, TT, QK)
        qT_all = view(A_, 0, 4, TOK)
        qTh, qTl = FTh[:, 3, :], FTl[:, 3, :]
        PTh, PTl = (view(w, 0, 2, 4, 2 * P) for w in (Wh_, Wl_))
        qpT = view(A_, 6144, 2, 2, TOK)
        s_sb = view(A_, 9216, 2, TT, 256)
        xs = view(A_, 6144, TT, D)
        skT = view(A_, 15360, 16, P)
        xst = view(A_, 6144, KD, TOK)
        pooled = view(B_, 0, 2, TOK)
        zn = view(B_, 1536, 2, QK)
        rt = view(B_, 2816, 2, 320)
        gqk = B_[:, 3456:4096]
        band = view(B_, 4096, 2, 5, P)
        Pb = view(B_, 0, 4, 512)
        kTh, kTl = KV_[:, 0:TOK], KV_[:, TOK:2 * TOK]
        Vh, Vl = view(KV_, 2 * TOK, TT, 192), view(KV_, 2 * TOK + TT * 192, TT, 192)
        Vh2, Vl2 = (v.rearrange("p t (a b) -> p t a b", a=3)[:, :, 0:3:2, :] for v in (Vh, Vl))
        cos = view(B_, 5376, TT, 2, 16)
        sin = view(B_, 5568, TT, 2, 16)
        ss1, rs1, ss2, rs2, tmp6 = (st[:, 6 * i:6 * i + 6] for i in range(5))
        ss10, rs10, tmp10 = st[:, 32:92], st[:, 92:152], st[:, 152:212]
        nmax, rsum, rrec = st[:, 212:224], st[:, 224:236], st[:, 236:248]
        table_word = st[:, 264:265]
        ssum8, srec8 = st[:, 248:256], st[:, 256:264]
        ur = view(Wr_, 2048, 2, KD, P)
        uh, ul = view(Wh_, 2048, 2, KD, P), view(Wl_, 2048, 2, KD, P)
        oh_g = Wh_[:, 0:2048].rearrange("p (a t c i) -> p a t c i", a=2, t=SG, c=2)
        oh_2 = view(Wl_, 0, 2, SG, P)
        oh_1 = view(Wr_, 0, 2, SG, P)
        Gst = view(A_, 0, 2, NK, BLK)
        gel = view(B_, 0, 2, TOK)
        s_in = view(B_, 1536, 2, P)
        s_cut = view(B_, 1792, 2, P)
        comb = B_[:, 2048:2304]
        comb_cut = B_[:, 2304:2560]
        eq = view(B_, 2560, 2, TOPK, TOPK)
        sv = view(B_, 3072, 2, TOPK)
        sif = view(B_, 3104, 2, TOPK)
        jf = view(B_, 3136, 2, TOPK)
        cvh = B_[:, 3168:3184]
        CV = view(B_, 3200, HEADS, TOPK)
        IDX = view(B_, 3328, 2, P)
        CE = view(B_, 3584, HEADS, TOPK)
        par = view(B_, 3712, 2, 4, P)
        G_ps = [ps[:, b:b + 2, :].rearrange("p b (m c i) -> p c (b m) i", m=2, c=2) for b in (4, 6)]
        si_u = iu[:, 0:32].rearrange("p (a b) -> p a b", a=2)
        ci_u = iu[:, 32:48]
        jj_u = iu[:, 48:80].rearrange("p (a b) -> p a b", a=2)
        G_lo = view(B_, 4736, 2, SG, P)
        gate_r = KV_[:, 0:P]
        vr = view(Wr_, 0, VB, D)
        vh = [view(Wh_, 0, VB, D), view(FTh_, 0, VB, D)]
        vl = [view(Wl_, 0, VB, D), view(FTl_, 0, VB, D)]
        Ah, Al = (view(KV_, a, 2, HALF) for a in (768, 1536))
        G2 = view(A_, 6144, 2, 6, 4 * BLK)
        gel2 = view(A_, 9216, 4, HALF)
        Aw = view(A_, 10752, 2, HALF)

        small_in = sem("small_in")
        xt_in = [sem(f"xt_in{i}") for i in range(KD)]
        vec_in, xr_in, sk_in = sem("vec_in"), sem("xr_in"), sem("sk_in")
        x_in = [sem(f"x_in{t}") for t in range(TT)]
        w_in = [sem(f"w_in{i}") for i in range(2)]
        band_in = [sem(f"band_in{i}") for i in range(2)]
        ft_hi, ft_lo, w_hi, w_lo = (sem(n) for n in ("ft_hi", "ft_lo", "w_hi", "w_lo"))
        sq1, var1, root1, rstd1_ok = (sem(n) for n in ("sq1", "var1", "root1", "rstd1_ok"))
        z_mm, z_ev = sem("z_mm"), sem("z_ev")
        var10, root10, zn_ok, rope_ok, rope_step = (sem(n) for n in ("var10", "root10", "zn_ok", "rope_ok", "rope_step"))
        pool_mm, pool_ev, mix_mm, mix_hi, mix_lo = (sem(n) for n in ("pool_mm", "pool_ev", "mix_mm", "mix_hi", "mix_lo"))
        qk_tr, k_hi, k_lo, q_ev, q_hi, q_lo, v_parts = (
            sem(n) for n in ("qk_tr", "k_hi", "k_lo", "q_ev", "q_hi", "q_lo", "v_parts"))
        qk_mm, max_ok, exp_ok, sum_inv, p_ok, p_tr, pt_hi, pt_lo, pv_mm, o_hi, o_lo = (
            sem(n) for n in ("qk_mm", "max_ok", "exp_ok", "sum_inv", "p_ok", "p_tr", "pt_hi", "pt_lo", "pv_mm", "o_hi",
                             "o_lo"))
        y_mm, y_ev = sem("y_mm"), sem("y_ev")
        sq2, var2, root2, rstd2_ok, xs_act, xs_dve, xn_tr, xn_hi, xn_lo = (
            sem(n) for n in ("sq2", "var2", "root2", "rstd2_ok", "xs_act", "xs_dve", "xn_tr", "xn_hi", "xn_lo"))
        y_out, y_in = sem("y_out"), sem("y_in")
        qp_mm, qp_ev, s_mm, s_ev = (sem(n) for n in ("qp_mm", "qp_ev", "s_mm", "s_ev"))
        s_out = [sem(f"s_out{i}") for i in range(2)]
        u_in = [sem(f"u_in{i}") for i in range(2)]
        u_hi, u_lo, h_mm, gelu_ok = (sem(n) for n in ("u_hi", "u_lo", "h_mm", "gelu_ok"))
        gel_out = [sem(f"gel_out{i}") for i in range(2)]
        s_load, s_read, oh2_ok, ohg_ok, g_mm, g_ev = (sem(n) for n in ("s_load", "s_read", "oh2_ok", "ohg_ok", "g_mm", "g_ev"))
        g_out = [sem(f"g_out{i}") for i in range(2)]
        ce_ok, ce_exp, gate_ok, par_tr = (sem(n) for n in ("ce_ok", "ce_exp", "gate_ok", "par_tr"))
        oh1_ok, g_part, par_ev = sem("oh1_ok"), sem("g_part"), sem("par_ev")
        v_in = [sem(f"v_in{i}") for i in range(4)]
        gel_in = [sem(f"gel_in{i}") for i in range(4)]
        G_in = [sem(f"G_in{i}") for i in range(2)]
        a_mul, a_hi, a_lo, v_hi, v_lo, a_mm, acc_done, acc_ev, done = (
            sem(n) for n in ("a_mul", "a_hi", "a_lo", "v_hi", "v_lo", "a_mm", "acc_done", "acc_ev", "done"))
        dve_step, zero_v = sem("dve_step"), sem("zero_v")

        x_tiles = [io["x_prompt"][0, P * t:P * t + P, :] for t in range(4)] + \
                  [io["x_sample"][0, P * t:P * t + P, :] for t in range(2)]
        out_tiles = [io["y_prompt"][0, P * t:P * t + P, :] for t in range(4)] + \
                    [io["y_sample"][0, P * t:P * t + P, :] for t in range(2)]
        smalls = [(ident[:, :], io["ident"]), (iota[:, :], io["iota"]),
                  (poolw[:, :], io["pool_w"]), (gqk, io["gqk"].partition_broadcast(P)),
                  (B_[:, 5376:5760], io["rope"])]
        s_dram, gel_dram, g_dram, y_dram = io["s_dram"], io["gel_dram"], io["g_dram"], io["y_dram"]

        units = [(q, hh, t + i) for q, (t0, n) in enumerate(SEQ_TILES) for t in range(0, n, 2)
                 for hh in range(2) for i in range(2)]
        NG = len(units) // 2
        NU = len(units)

        def pe_split_product(out, lh, ll, rh, rl, first, last):
            nc.tensor.matmul(out, lh, rh, start=first, stop=False)
            nc.tensor.matmul(out, lh, rl, start=False, stop=False)
            return nc.tensor.matmul(out, ll, rh, start=False, stop=last)

        block = ctx.enter_context(nc.Block())

        @block.sync
        def _(sp):
            def load_xt(k):
                sp.dma_start(xst[:, k, :], io["xT"][:, k, :]).then_inc(xt_in[k], 16)

            def load_w(n, slot):
                sp.dma_start(Wr[:, slot, :, :], io["w_all"][ds(n, 1), :, :, :].squeeze(0)).then_inc(w_in[slot], 16)

            sp.dma_start(vecs[:, :], io["vecs"]).then_inc(vec_in, 16)
            load_w(0, 0)
            for k in range(KD):
                load_xt(k)
            load_w(1, 1)
            for t in range(TT):
                sp.dma_start(y[:, t, :], x_tiles[t]).then_inc(x_in[t], 16)
            for dst, src in smalls:
                sp.dma_start(dst, src).then_inc(small_in, 16)
            for gi in range(2):
                sp.dma_start(band[:, gi, :, :], io["band"][gi]).then_inc(band_in[gi], 16)
            for n in range(2, 2 + N_WIN):
                sp.wait_ge(w_lo, n - 1)
                load_w(n, n % 2)
            for gi in range(2, 4):
                sp.wait_ge(pool_mm, 2 * (gi - 1))
                sp.dma_start(band[:, gi % 2, :, :], io["band"][gi]).then_inc(band_in[gi % 2], 16)
            sp.wait_ge(w_lo, 6)
            load_w(7, 1)
            sp.wait_ge(o_lo, 2 + 8)
            for t in range(TT):
                sp.dma_start(y[:, t, :], x_tiles[t]).then_inc(xr_in, 16)
            sp.dma_start(skT, io["skT"]).then_inc(sk_in, 16)
            for n in range(8, 11):
                sp.wait_ge(w_lo, n - 1)
                load_w(n, n % 2)

            def head_io(i, s, more):
                h = i * 2 + s
                if more:
                    sp.wait_ge(w_lo, h + 10)
                    load_w(h + 11, (11 + s) % 2)
                sp.wait_ge(s_ev, h * TT + (TT + 4))
                sp.dma_start(s_dram[ds(h, 1), :, :, :].squeeze(0), s_sb[:, s, :, :]).then_inc(s_out[s], 16)

            with sp.Fori(0, 3) as i:
                for s in range(2):
                    head_io(i, s, True)
            sp.wait_ge(w_lo, N_W - 1)
            for s in range(2):
                sp.dma_start(ur[:, s, :, :], io["uT"][s]).then_inc(u_in[s], 16)

            def load_s(t, h):
                sp.dma_start(s_in, s_dram[ds(h, 1), :, ds(t, 1), :].squeeze(2).squeeze(0)
                             .rearrange("p (a b) -> p a b", a=2)).then_inc(s_load, 16)

            sp.wait_ge(s_out[0], 16 + 16)
            load_s(0, 0)
            for s in range(2):
                head_io(3, s, False)
            for s in range(2):
                sp.wait_ge(s_out[s], 16 + 64)

            def unit(U, prefetch, more_scores, piece=None):
                for s in range(2):
                    if prefetch:
                        sp.wait_ge(u_lo, U * 2 + (s + 1))
                        sp.dma_start(ur[:, s, :, :], io["uT"][ds(U * 2 + (s + 2), 1), :, :, :].squeeze(0)
                                     ).then_inc(u_in[s], 16)
                    if s == 0 and piece is not None:
                        store_g(*piece)
                    sp.wait_ge(gelu_ok, U * 4 + (2 * s + 2 + 4))
                    sp.dma_start(gel_dram[ds(U * 2 + s, 1), :, :].squeeze(0), gel[:, s, :]).then_inc(gel_out[s], 16)
                    if s == 0 and more_scores:
                        sp.wait_ge(s_read, U + 2)
                        load_s((U + 2) // UNITS_T, (U + 2) % UNITS_T)

            def store_g(Tb, hb, piece):
                sp.wait_ge(g_ev, Tb * 32 + (hb * 16 + 16 + 2))
                sp.dma_start(g_dram[ds(Tb * 2 + hb, 1), :, ds(piece * 32, 32), :].squeeze(0),
                             Gst[:, hb, ds(piece * 32, 32), :]).then_inc(g_out[hb], 16)

            sp.wait_ge(s_read, 1)
            load_s(0, 1)
            with sp.Fori(0, UNITS_T) as U:
                unit(U, True, True)
            with sp.Fori(8, 12) as U:
                unit(U, True, True)
            with sp.Fori(0, 4) as q:
                unit(q + 12, True, True, (0, 0, q))
            with sp.Fori(2, TT - 1) as T:
                for hb in range(2):
                    with sp.Fori(0, 4) as q:
                        unit(T * 8 + (q + 4 * hb), True, True, (T - 2 + hb, 1 - hb, q))
            with sp.Fori(0, 4) as q:
                unit(q + 40, True, True, (3, 1, q))
            with sp.Fori(0, 2) as q:
                unit(q + 44, True, True, (4, 0, q))
            with sp.Fori(2, 4) as q:
                unit(q + 44, True, False, (4, 0, q))
            for hb in range(2):
                with sp.Fori(0, 4) as q:
                    unit(q + (48 + 4 * hb), True, False, (4 + hb, 1 - hb, q))
            with sp.Fori(0, 4) as q:
                unit(q + 56, True, False, (5, 1, q))
            with sp.Fori(60, 63) as U:
                unit(U, True, False)

            def step_loads(i, blk, half, x):
                S = i * 16 + (blk * 8 + half * 4 + x)
                e = i * 8 + (blk * 4 + x)
                if x == 0:
                    sp.wait_ge(a_mul, S + 4)
                    sp.dma_start(G2[:, half, :, :],
                                 g_dram[6 * half:6 * half + 6, :, ds(e, 4), :].rearrange("b p e t -> p b (e t)")
                                 ).then_inc(G_in[half], 16)
                sp.wait_ge(a_mul, S + 5)
                sp.dma_start(gel2[:, x, :], gel_dram[ds(e, 1), :, half * HALF:(half + 1) * HALF].squeeze(0)
                             ).then_inc(gel_in[x], 16)

            def v_load(n, x):
                sp.wait_ge(v_lo, n * 4 + (x + 1))
                sp.dma_start(vr[:, x, :], io["v"][ds(n * 4 + x, 1), :, :].squeeze(0)).then_inc(v_in[x], 16)

            def block_loads(i, blk, more=True):
                for half in range(2):
                    for x in range(VB):
                        step_loads(i, blk, half, x)
                        if half == 0 and more:
                            v_load(i * 2 + (blk + 1), x)

            for hb in range(2):
                sp.wait_ge(g_out[hb], 16 + 6 * 64)
            for x in range(2):
                step_loads(0, 0, 0, x)
                v_load(0, x)
            for t in range(TT):
                sp.dma_start(y[:, t, :], y_dram[t]).then_inc(y_in, 16)
            sp.wait_ge(u_lo, 2 * 64)
            for x in range(2, VB):
                step_loads(0, 0, 0, x)
                v_load(0, x)
            unit(63, False, False)
            for s in range(2):
                sp.wait_ge(gel_out[s], 16 + 16 * 64)
            for x in range(VB):
                v_load(1, x)
                step_loads(0, 0, 1, x)
            block_loads(0, 1)
            with sp.Fori(1, N_VB // 2 - 1) as i:
                block_loads(i, 0)
                block_loads(i, 1)
            block_loads(N_VB // 2 - 1, 0)
            block_loads(N_VB // 2 - 1, 1, False)
            sp.wait_ge(acc_ev, 6 + 12 * N_VB - 6)
            for t in range(3):
                sp.dma_start(out_tiles[t], y[:, t, :]).then_inc(done, 16)
            for t in range(3, 6):
                sp.wait_ge(acc_ev, 12 * N_VB + 2 * (t - 3) + 2)
                sp.dma_start(out_tiles[t], y[:, t, :]).then_inc(done, 16)
            sp.wait_ge(done, 16 * TT)

        @block.scalar
        def _(act):
            act.sem_inc(exp_ok, 3)
            act.sem_inc(z_ev, 6)
            act.sem_inc(qp_ev, 4)
            act.sem_inc(gelu_ok, 4)
            for s in range(2):
                act.sem_inc(gel_out[s], 16)
                act.sem_inc(g_out[s], 16)
                act.sem_inc(s_out[s], 16)

            def w_split_hi(n):
                act.wait_ge(w_in[n % 2], 16 * (n // 2 + 1))
                if 2 <= n < 2 + N_WIN:
                    act.wait_ge(z_mm, 6 * (n - 1))
                elif n >= 2:
                    act.wait_ge(y_mm, 6 * (n - 1 - N_WIN))
                nc.scalar.activation(Wh[:, n % 2, :, :], Wr[:, n % 2, :, :], ACT.Copy).then_inc(w_hi, 1)

            w_split_hi(0)
            act.wait_ge(vec_in, 16)
            for k in range(KD):
                act.wait_ge(xt_in[k], 16)
                nc.scalar.activation(FTh[:, k, :], xst[:, k, :], ACT.Copy, scale=g1[:, k:k + 1]).then_inc(ft_hi, 1)
            w_split_hi(1)
            for t in range(TT):
                act.wait_ge(x_in[t], 16)
                if t:
                    act.wait_ge(sq1, t)
                nc.scalar.activation(ps[:, 6:8, :], y[:, t, :].rearrange("p (a b) -> p a b", a=2), ACT.Square,
                                     accum_out=ss1[:, t:t + 1]).then_inc(sq1, 1)
            act.wait_ge(var1, 1)
            nc.scalar.activation(rs1, tmp6, ACT.Sqrt).then_inc(root1, 1)
            act.wait_ge(rstd1_ok, 1)

            def z_out(c):
                for t in range(TT):
                    if c == 3 and t == 1:
                        act.wait_ge(var10, 1)
                        nc.scalar.activation(rs10, tmp10, ACT.Sqrt).then_inc(root10, 1)
                    act.wait_ge(z_mm, 6 * c + t + 1)
                    nc.scalar.activation(z[:, t, c * WC:(c + 1) * WC], ps[:, t, 0:WC], ACT.Copy,
                                         scale=rs1[:, t:t + 1]).then_inc(z_ev, 1)

            for c in range(N_WIN):
                z_out(c)
                if c + 2 < 6:
                    w_split_hi(c + 2)

            def pooled_out(gi):
                for q, (t0, n) in enumerate(SEQ_TILES):
                    act.wait_ge(pool_mm, 2 * gi + q + 1)
                    if gi >= 2:
                        act.wait_ge(mix_mm, 2 * (gi - 2) + q + 1)
                    nc.scalar.activation(pooled[:, gi % 2, t0 * P:(t0 + n) * P], ps[:, q, 0:n * P],
                                         ACT.Copy).then_inc(pool_ev, 1)

            def mix_out(gi):
                for q, (t0, n) in enumerate(SEQ_TILES):
                    act.wait_ge(mix_mm, 2 * gi + q + 1)
                    nc.scalar.activation(FTh[:, 4 + gi, t0 * P:(t0 + n) * P], ps[:, 2 + q, 0:n * P], ACT.Copy,
                                         scale=pool_scale[:, gi:gi + 1]).then_inc(mix_hi, 1)

            pooled_out(0)
            for gi in range(1, 4):
                pooled_out(gi)
                mix_out(gi - 1)
            act.wait_ge(zero_v, 2)
            nc.scalar.activation(Vh2, z[:, :, V_COL:V_COL + P].rearrange("p t (a b) -> p t a b", a=2),
                                 ACT.Copy).then_inc(v_parts, 1)
            def take_pair(j):
                nc.scalar.activation(qTh, qT_all[:, ds(j, 1), :].squeeze(1), ACT.Copy).then_inc(q_hi, 1)

            for r in range(5):
                if r == 1:
                    mix_out(3)
                act.wait_ge(qk_tr, r + 1)
                dst, b, ok = (kTh, 4, k_hi) if r == 0 else (qT_all[:, r - 1, :], 4 + 2 * (r % 2), q_ev)
                nc.scalar.activation(dst[:, 0:512], ps[:, b, :], ACT.Copy).then_inc(ok, 1)
                nc.scalar.activation(dst[:, 512:768], ps[:, b + 1, 0:256], ACT.Copy).then_inc(ok, 1)
                if r == 1:
                    act.wait_ge(q_ev, 2)
                    take_pair(0)

            def pt_out(j, u):
                n = SEQ_TILES[units[u][0]][1]
                if u % 2 == 0:
                    act.wait_ge(pv_mm, j * NG + (u // 2 + 1))
                act.wait_ge(p_tr, j * NU + (u + 5))
                nc.scalar.activation(PTh[:, u // 2 % 2, 0:n, (u % 2) * P:(u % 2 + 1) * P],
                                     ps[:, 3 + u % 3, 0:n * P].rearrange("p (a b) -> p a b", a=n),
                                     ACT.Copy).then_inc(pt_hi, 1)

            def o_out(j, q):
                t0, n = SEQ_TILES[q]
                act.wait_ge(pv_mm, j * NG + (2 * q + 6))
                nc.scalar.activation(FTh[:, ds(j, 1), t0 * P:(t0 + n) * P].squeeze(1), ps[:, 6 + q, 0:n * P],
                                     ACT.Copy).then_inc(o_hi, 1)

            def pair(j, first=False):
                if not first:
                    act.wait_ge(qk_mm, j * NU)
                    take_pair(j)
                for u, (q, hh, t) in enumerate(units):
                    n = SEQ_TILES[q][1]
                    act.wait_ge(max_ok, j * NU + (u + 1))
                    act.wait_ge(p_tr, j * NU + (u + 1))
                    nc.scalar.activation(Pb[:, u % 4, 0:n * P], ps[:, u % 3, 0:n * P], ACT.Exp,
                                         bias=nmax[:, u:u + 1], accum_out=rsum[:, u:u + 1]).then_inc(exp_ok, 1)
                    if u >= 3:
                        pt_out(j, u - 3)
                    elif not first:
                        pt_out(j - 1, NU + u - 3)
                    if u in (0, 5) and not first:
                        o_out(j - 1, u // 5)

            pair(0, True)
            with act.Fori(1, 4) as j:
                pair(j)
            for u in range(NU - 3, NU):
                pt_out(3, u)
            o_out(3, 0)
            o_out(3, 1)
            for n in range(6, 10):
                w_split_hi(n)
            nc.scalar.activation(table_word, rs10[:, 0:1], ACT.Sqrt)
            for t in range(TT):
                act.wait_ge(y_ev, 6 + 18 + t + 1)
                if t:
                    act.wait_ge(sq2, t)
                nc.scalar.activation(ps[:, 6:8, :], y[:, t, :].rearrange("p (a b) -> p a b", a=2), ACT.Square,
                                     accum_out=ss2[:, t:t + 1]).then_inc(sq2, 1)
            act.dma_start(y_dram.rearrange("t p d -> p t d"), y).then_inc(y_out, 16)
            act.wait_ge(var2, 1)
            nc.scalar.activation(rs2, tmp6, ACT.Sqrt).then_inc(root2, 1)
            act.wait_ge(rstd2_ok, 1)

            for t in (0, 2, 4):
                nc.scalar.activation(xs[:, t, :], y[:, t, :], ACT.Copy, scale=rs2[:, t:t + 1]).then_inc(xs_act, 1)
            for i in range(16):
                half, k = i // 8, i % 8
                act.wait_ge(xn_tr, i + 1)
                nc.scalar.activation(FTh[:, k, half * HALF:(half + 1) * HALF], ps[:, 4 + i % 4, 0:HALF], ACT.Copy,
                                     scale=g2[:, k:k + 1]).then_inc(xn_hi, 1)
            w_split_hi(10)

            def head(i, s, more):
                h = i * 2 + s
                for n in range(4):
                    if n == 0:
                        act.wait_ge(s_mm, h * TT + TT)
                    act.wait_ge(qp_mm, h * 4 + (n + 1))
                    nc.scalar.activation(qpT[:, s, n % 2, (n // 2) * HALF:(n // 2 + 1) * HALF], ps[:, n, 0:HALF],
                                         ACT.Copy).then_inc(qp_ev, 1)
                if more:
                    act.wait_ge(w_in[(11 + s) % 2], i * 16 + 16 * ((11 + s) // 2 + 1))
                    act.wait_ge(qp_mm, h * 4 + 4)
                    nc.scalar.activation(Wh[:, (11 + s) % 2, :, :], Wr[:, (11 + s) % 2, :, :],
                                         ACT.Copy).then_inc(w_hi, 1)

            with act.Fori(0, 3) as i:
                for s in range(2):
                    head(i, s, True)
            head(3, 0, False)
            act.wait_ge(qp_mm, 4 * 7)
            for s in range(2):
                act.wait_ge(u_in[s], 16)
                nc.scalar.activation(uh[:, s, :, :], ur[:, s, :, :], ACT.Copy).then_inc(u_hi, 1)
            head(3, 1, False)

            def unit(U, Ub, prefetch, T=None):
                for s in range(2):
                    for half in range(2):
                        if half == 0:
                            act.wait_ge(gel_out[s], U * 16 + 16)
                        act.wait_ge(h_mm, U * 4 + (2 * s + half + 1))
                        nc.scalar.activation(gel[:, s, half * HALF:(half + 1) * HALF], ps[:, 2 * s + half, 0:HALF],
                                             ACT.Gelu).then_inc(gelu_ok, 1)
                        if half == 1 and prefetch:
                            act.wait_ge(u_in[s], U * 16 + 32)
                            nc.scalar.activation(uh[:, s, :, :], ur[:, s, :, :], ACT.Copy).then_inc(u_hi, 1)
                        if Ub is not None:
                            sg = 2 * s + half
                            act.wait_ge(g_mm, Ub * 4 + (sg + 3))
                            nc.scalar.activation(G_lo[:, sg % 2, :, :], G_ps[sg % 2][:, 1, :, :],
                                                 ACT.Copy).then_inc(g_part, 1)
                        if T is not None and s == half == 0:
                            act.wait_ge(ce_ok, T + 1)
                            nc.scalar.activation(CE, CE, ACT.Exp).then_inc(ce_exp, 1)

            with act.Fori(0, 7) as U:
                unit(U, None, True)
            unit(7, None, True, 0)
            act.wait_ge(y_out, 16)
            with act.Fori(1, TT) as T:
                for hb in range(2):
                    act.wait_ge(g_out[hb], T * 64 - 48)
                    with act.Fori(0, 4 - hb) as q:
                        unit(T * 8 + (q + 4 * hb), T * 8 + (q + (4 * hb - 8)), True)
                unit(T * 8 + 7, T * 8 - 1, True, T)
            for hb in range(2):
                act.wait_ge(g_out[hb], TT * 64 - 48)
                with act.Fori(0, 4) as q:
                    unit(q + (48 + 4 * hb), q + (40 + 4 * hb), True)
            with act.Fori(56, 63) as U:
                unit(U, None, True)

            def v_part(n, blk, x):
                act.wait_ge(v_in[x], n * 16 + 16)
                nc.scalar.activation(vh[blk][:, x, :], vr[:, x, :], ACT.Copy).then_inc(v_hi, 1)

            def a_part(S, x):
                act.wait_ge(a_mm, S + 1)
                act.wait_ge(a_mul, S + 9)
                nc.scalar.activation(Ah[:, x % 2, :], Aw[:, x % 2, :], ACT.Copy).then_inc(a_hi, 1)

            def block_parts(i, blk, first=False, more=True):
                for half in range(2):
                    for x in range(VB):
                        if first and half == 0 and x < 2:
                            continue
                        a_part(i * 16 + (blk * 8 + half * 4 + x), x)
                        if half == 1 and more:
                            v_part(i * 2 + (blk + 1), 1 - blk, x)

            for x in range(2):
                v_part(0, 0, x)
                a_part(x, x)
            unit(63, None, False)
            v_part(0, 0, 2)
            v_part(0, 0, 3)
            block_parts(0, 0, first=True)
            block_parts(0, 1)
            with act.Fori(1, N_VB // 2 - 1) as i:
                block_parts(i, 0)
                block_parts(i, 1)
            block_parts(N_VB // 2 - 1, 0)
            block_parts(N_VB // 2 - 1, 1, more=False)

        @block.gpsimd
        def _(pool):
            pool.sem_inc(a_mul, 8)
            for v in (Vh, Vl):
                nc.gpsimd.memset(v.bitcast(F32), 0.0).then_inc(zero_v, 1)
            steps = Steps(pool, rope_step)
            for t in range(TT):
                pool.wait_ge(zn_ok, t + 1)
                src = zn[:, t % 2, :].rearrange("p (g a i) -> p g a i", a=2, i=16)
                dst = qkr[:, t, :].rearrange("p (g a i) -> p g a i", a=2, i=16)
                ta = rt[:, 0, :].rearrange("p (h g i) -> p h g i", g=2, i=16)
                tb = rt[:, 1, :].rearrange("p (h g i) -> p h g i", g=2, i=16)
                c = cos[:, t, :, :].unsqueeze(1).to_broadcast([P, 10, 2, 16])
                s = sin[:, t, :, :].unsqueeze(1).to_broadcast([P, 10, 2, 16])

                def part(v, a):
                    return v[:, :, a, :].rearrange("p (h g) i -> p h g i", g=2)

                for first, second, op, o in ((c, s, ALU.subtract, 0), (s, c, ALU.add, 1)):
                    steps.did(nc.gpsimd.tensor_tensor(ta, part(src, 0), first, ALU.mult))
                    steps.step(nc.gpsimd.tensor_tensor(tb, part(src, 1), second, ALU.mult))
                    ins = nc.gpsimd.tensor_tensor(part(dst, o), ta, tb, op)
                    if o == 0:
                        steps.step(ins)
                    else:
                        ins.then_inc(rope_ok, 1)
                        pool.wait_ge(rope_ok, t + 1)
            def scale(j):
                for u, (q, hh, t) in enumerate(units):
                    n = SEQ_TILES[q][1]
                    pool.wait_ge(sum_inv, j * NU + (u + 1))
                    nc.gpsimd.tensor_tensor(Pb[:, u % 4, 0:n * P], Pb[:, u % 4, 0:n * P],
                                            rrec[:, u:u + 1].to_broadcast([P, n * P]), ALU.mult).then_inc(p_ok, 1)

            with pool.Fori(0, 4) as j:
                scale(j)

            def gate_one_hots(Tb, h):
                for sg in range(4):
                    pool.wait_ge(oh1_ok, Tb * 32 + (h * 4 + sg + 1))
                    nc.gpsimd.tensor_tensor(
                        oh_g[:, sg % 2, :, :, :], oh_1[:, sg % 2, :, :].unsqueeze(2).to_broadcast([P, SG, 2, P]),
                        par[:, ds(Tb % 2, 1), 2:4, ds(h * 16 + sg * SG, SG)].squeeze(1).rearrange("p c t -> p t c")
                        .unsqueeze(3).to_broadcast([P, SG, 2, P]), ALU.mult).then_inc(ohg_ok, 1)

            with pool.Fori(0, TT) as Tb:
                with pool.Fori(0, UNITS_T) as h:
                    gate_one_hots(Tb, h)
            with pool.Fori(0, N_VB // 2) as i:
                for step in range(4 * VB):
                    blk, half, x = step // 8, step // 4 % 2, step % 4
                    S = i * 16 + step
                    pool.wait_ge(gel_in[x], i * 64 + 16 * (step // 4 + 1))
                    if x == 0:
                        pool.wait_ge(G_in[half], i * 32 + 16 * (blk + 1))
                    pool.wait_ge(a_lo, S + 1)
                    nc.gpsimd.tensor_tensor(
                        Aw[:, x % 2, :].rearrange("p (b t) -> p b t", t=BLK),
                        gel2[:, x, :].rearrange("p (b t) -> p b t", t=BLK),
                        G2[:, half, :, x * BLK:(x + 1) * BLK], ALU.mult).then_inc(a_mul, 1)

        @block.vector
        def _(dve):
            dve.sem_inc(o_lo, 2)
            dve.sem_inc(pt_lo, 3)
            dve.sem_inc(y_ev, 6)
            dve.sem_inc(s_ev, 4)
            dve.sem_inc(g_ev, 2)
            dve.sem_inc(a_lo, 2)
            dve.sem_inc(v_lo, 4)
            dve.sem_inc(acc_ev, 6)
            tt, ts = nc.vector.tensor_tensor, nc.vector.tensor_scalar
            steps = Steps(dve, dve_step)

            def w_split_lo(n):
                dve.wait_ge(w_hi, n + 1)
                tt(Wl[:, n % 2, :, :], Wr[:, n % 2, :, :], Wh[:, n % 2, :, :].bitcast(F32),
                   ALU.subtract).then_inc(w_lo, 1)

            def newton(r, root, a, tmp, ok):
                dve.wait_ge(root, 1)
                steps.step(nc.vector.reciprocal(r, r))
                steps.step(tt(tmp[1], r, r, ALU.mult))
                steps.step(tt(tmp[1], tmp[1], a, ALU.mult))
                steps.step(ts(tmp[1], tmp[1], -0.5, 1.5, ALU.mult, ALU.add))
                return tt(r, r, tmp[1], ALU.mult)

            w_split_lo(0)
            for k in range(KD):
                dve.wait_ge(ft_hi, k + 1)
                nc.vector.scalar_tensor_tensor(FTl[:, k, :], xst[:, k, :], g1[:, k:k + 1],
                                               FTh[:, k, :].bitcast(F32), ALU.mult, ALU.subtract).then_inc(ft_lo, 1)
            w_split_lo(1)
            dve.wait_ge(sq1, TT)
            ts(tmp6, ss1, 1.0 / D, EPS, ALU.mult, ALU.add).then_inc(var1, 1)
            newton(rs1, root1, tmp6, (None, ss1), None).then_inc(rstd1_ok, 1)
            for n in range(2, 4):
                w_split_lo(n)
            dve.wait_ge(small_in, 16 * len(smalls))
            for t in range(TT):
                dve.wait_ge(z_ev, 6 + 12 + t + 1)
                steps.step(tt(zn[:, 0, :], z[:, t, 0:QK], z[:, t, 0:QK], ALU.mult))
                steps.step(nc.vector.tensor_reduce(ss10[:, 10 * t:10 * t + 10],
                                                   zn[:, 0, :].rearrange("p (h d) -> p h d", d=64), AX.X, ALU.add))
            ts(tmp10, ss10, 1.0 / 64, EPS, ALU.mult, ALU.add).then_inc(var10, 1)
            w_split_lo(4)
            steps.step(newton(rs10, root10, tmp10, (None, ss10), None))
            rq = rs10.rearrange("p (t h) -> p t h", h=10)
            steps.step(ts(rq[:, :, 0:8], rq[:, :, 0:8], 0.125, None, ALU.mult))
            for t in range(TT):
                if t >= 2:
                    dve.wait_ge(rope_ok, t - 1)
                steps.step(tt(zn[:, t % 2, :].rearrange("p (h d) -> p h d", d=64),
                              z[:, t, 0:QK].rearrange("p (h d) -> p h d", d=64),
                              rs10[:, 10 * t:10 * t + 10].unsqueeze(2).to_broadcast([P, 10, 64]), ALU.mult))
                tt(zn[:, t % 2, :], zn[:, t % 2, :], gqk, ALU.mult).then_inc(zn_ok, 1)
            w_split_lo(5)

            def mix_rest(gi):
                for q, (t0, n) in enumerate(SEQ_TILES):
                    dve.wait_ge(mix_hi, 2 * gi + q + 1)
                    nc.vector.scalar_tensor_tensor(
                        FTl[:, 4 + gi, t0 * P:(t0 + n) * P], ps[:, 2 + q, 0:n * P], pool_scale[:, gi:gi + 1],
                        FTh[:, 4 + gi, t0 * P:(t0 + n) * P].bitcast(F32), ALU.mult, ALU.subtract).then_inc(mix_lo, 1)
            for gi in range(3):
                mix_rest(gi)
            dve.wait_ge(v_parts, 1)
            tt(Vl2, z[:, :, V_COL:V_COL + P].rearrange("p t (a b) -> p t a b", a=2), Vh2.bitcast(F32),
               ALU.subtract).then_inc(v_parts, 1)
            for b, c in ((0, 512), (1, 256)):
                dve.wait_ge(k_hi, b + 1)
                tt(kTl[:, b * 512:b * 512 + c], ps[:, 4 + b, 0:c], kTh[:, b * 512:b * 512 + c].bitcast(F32),
                   ALU.subtract).then_inc(k_lo, 1)
            mix_rest(3)

            def row_max(j, u):
                n = SEQ_TILES[units[u][0]][1]
                dve.wait_ge(qk_mm, j * NU + (u + 1))
                nc.vector.tensor_reduce(nmax[:, u:u + 1], ps[:, u % 3, 0:n * P], AX.X, ALU.max,
                                        negate=True).then_inc(max_ok, 1)

            def pt_rest(j, u):
                n = SEQ_TILES[units[u][0]][1]
                g, cols = u // 2 % 2, slice((u % 2) * P, (u % 2 + 1) * P)
                dve.wait_ge(pt_hi, j * NU + (u + 1))
                tt(PTl[:, g, 0:n, cols], ps[:, 3 + u % 3, 0:n * P].rearrange("p (a b) -> p a b", a=n),
                   PTh[:, g, 0:n, cols].bitcast(F32), ALU.subtract).then_inc(pt_lo, 1)

            def o_rest(j, q):
                t0, n = SEQ_TILES[q]
                dve.wait_ge(o_hi, j * 2 + (q + 1))
                tt(FTl[:, ds(j, 1), t0 * P:(t0 + n) * P].squeeze(1), ps[:, 6 + q, 0:n * P],
                   FTh[:, ds(j, 1), t0 * P:(t0 + n) * P].squeeze(1).bitcast(F32), ALU.subtract).then_inc(o_lo, 1)

            def pair(j, first=False):
                dve.wait_ge(q_hi, j + 1)
                tt(qTl, qT_all[:, ds(j, 1), :].squeeze(1), qTh.bitcast(F32), ALU.subtract).then_inc(q_lo, 1)
                row_max(j, 0)
                for u in range(NU):
                    if u + 1 < NU:
                        row_max(j, u + 1)
                    dve.wait_ge(exp_ok, j * NU + (u + 4))
                    nc.vector.reciprocal(rrec[:, u:u + 1], rsum[:, u:u + 1]).then_inc(sum_inv, 1)
                    if u >= 3:
                        pt_rest(j, u - 3)
                    elif not first:
                        pt_rest(j - 1, NU + u - 3)
                    if u in (0, 5) and not first:
                        o_rest(j - 1, u // 5)

            pair(0, True)
            with dve.Fori(1, 4) as j:
                pair(j)
            for u in range(NU - 3, NU):
                pt_rest(3, u)
            o_rest(3, 0)
            o_rest(3, 1)
            w_split_lo(6)
            dve.wait_ge(xr_in, 16 * TT)
            for c in range(N_WOUT):
                for t in range(TT):
                    dve.wait_ge(y_mm, 6 * c + t + 1)
                    tt(y[:, t, c * WC:(c + 1) * WC], y[:, t, c * WC:(c + 1) * WC], ps[:, t, 0:WC],
                       ALU.add).then_inc(y_ev, 1)
                if c < 3:
                    w_split_lo(7 + c)
            dve.wait_ge(sq2, TT)
            ts(tmp6, ss2, 1.0 / D, EPS, ALU.mult, ALU.add).then_inc(var2, 1)
            newton(rs2, root2, tmp6, (None, ss2), None).then_inc(rstd2_ok, 1)
            for t in (1, 3, 5):
                dve.wait_ge(rstd2_ok, 1)
                ts(xs[:, t, :], y[:, t, :], rs2[:, t:t + 1], None, ALU.mult).then_inc(xs_dve, 1)
            for i in range(16):
                half, k = i // 8, i % 8
                dve.wait_ge(xn_hi, i + 1)
                nc.vector.scalar_tensor_tensor(
                    FTl[:, k, half * HALF:(half + 1) * HALF], ps[:, 4 + i % 4, 0:HALF], g2[:, k:k + 1],
                    FTh[:, k, half * HALF:(half + 1) * HALF].bitcast(F32), ALU.mult, ALU.subtract).then_inc(xn_lo, 1)
            w_split_lo(10)

            def head(i, s, more):
                h = i * 2 + s
                dve.wait_ge(s_out[s], i * 16 + 16)
                for t in range(TT):
                    if t == 3 and more:
                        dve.wait_ge(w_hi, h + 12)
                        tt(Wl[:, (11 + s) % 2, :, :], Wr[:, (11 + s) % 2, :, :], Wh[:, (11 + s) % 2, :, :].bitcast(F32),
                           ALU.subtract).then_inc(w_lo, 1)
                    dve.wait_ge(s_mm, h * TT + (t + 13))
                    nc.vector.tensor_copy(s_sb[:, s, t, :], ps[:, 4 + (6 * s + t) % 4, 0:256]).then_inc(s_ev, 1)

            with dve.Fori(0, 3) as i:
                for s in range(2):
                    head(i, s, True)
            def u_split_lo(e1, s):
                dve.wait_ge(u_hi, e1)
                tt(ul[:, s, :, :], ur[:, s, :, :], uh[:, s, :, :].bitcast(F32), ALU.subtract).then_inc(u_lo, 1)

            def one_hot(Tb, h, sg, which, dst, ok):
                dve.wait_ge(g_mm, Tb * 32 + (h * 4 + sg + 1))
                tt(dst[:, sg % 2, :, :], iota[:, :].unsqueeze(1).to_broadcast([P, SG, P]),
                   par[:, ds(Tb % 2, 1), which, ds(h * 16 + sg * SG, SG)].squeeze(1)
                   .unsqueeze(2).to_broadcast([P, SG, P]), ALU.is_equal).then_inc(ok, 1)

            def add_G(Tb, h, sg):
                dve.wait_ge(g_part, Tb * 32 + (h * 4 + sg + 1))
                tt(Gst[:, ds(h // 4, 1), :, ds((h % 4) * 16 + sg * SG, SG)].squeeze(1),
                   G_ps[sg % 2][:, 0, :, :].rearrange("p t i -> p i t"),
                   G_lo[:, sg % 2, :, :].rearrange("p t i -> p i t"), ALU.add).then_inc(g_ev, 1)

            def unit(U, Tb, h, topk, prefetch, T=None, following=None, split=True):
                if T is not None:
                    tt(CE, CV, CV[:, :, 0:1].to_broadcast([P, HEADS, TOPK]), ALU.subtract).then_inc(ce_ok, 1)
                if Tb is not None:
                    one_hot(Tb, h, 1, 0, oh_1, oh1_ok)
                if split:
                    u_split_lo(U * 2 + 2, 1)
                if Tb is not None:
                    one_hot(Tb, h, 1, 1, oh_2, oh2_ok)
                if T is not None:
                    dve.wait_ge(ce_ok, T + 1)
                if topk:
                    dve.wait_ge(s_load, 16)
                    dve.sem_inc(s_load, -16)
                    for p in range(2):
                        steps.did(nc.vector.max(sv[:, p, 0:8], s_in[:, p, :]))
                    steps.settle()
                    for p in range(2):
                        steps.did(nc.vector.max_index(si_u[:, p, 0:8], sv[:, p, 0:8], s_in[:, p, :]))
                        steps.did(nc.vector.match_replace(s_cut[:, p, :], sv[:, p, 0:8], s_in[:, p, :], LOWEST))
                if Tb is not None:
                    one_hot(Tb, h, 2, 0, oh_1, oh1_ok)
                    add_G(Tb, h, 0)
                if topk:
                    steps.settle()
                    dve.sem_inc(s_read, 1)
                    for p in range(2):
                        steps.did(nc.vector.max(sv[:, p, 8:16], s_cut[:, p, :]))
                if Tb is not None:
                    one_hot(Tb, h, 2, 1, oh_2, oh2_ok)
                if topk:
                    steps.settle()
                    for p in range(2):
                        steps.did(nc.vector.max_index(si_u[:, p, 8:16], sv[:, p, 8:16], s_cut[:, p, :]))
                    steps.did(tt(comb.rearrange("p (a b) -> p a b", a=TOPK),
                                 sv[:, 0, :].unsqueeze(2).to_broadcast([P, TOPK, TOPK]),
                                 sv[:, 1, :].unsqueeze(1).to_broadcast([P, TOPK, TOPK]), ALU.add))
                    steps.settle()
                    steps.did(nc.vector.max(cvh[:, 0:8], comb))
                    steps.did(nc.vector.tensor_copy(sif, si_u))
                if T is not None:
                    dve.wait_ge(ce_exp, T + 1)
                    steps.step(nc.vector.tensor_reduce(ssum8, CE, AX.X, ALU.add))
                    steps.step(nc.vector.reciprocal(srec8, ssum8))
                    tt(CE, CE, srec8.unsqueeze(2).to_broadcast([P, HEADS, TOPK]), ALU.mult).then_inc(gate_ok, 1)
                if Tb is not None:
                    one_hot(Tb, h, 3, 0, oh_1, oh1_ok)
                    add_G(Tb, h, 1)
                if topk:
                    steps.settle()
                    steps.did(nc.vector.max_index(ci_u[:, 0:8], cvh[:, 0:8], comb))
                    steps.did(nc.vector.match_replace(comb_cut, cvh[:, 0:8], comb, LOWEST))
                if prefetch:
                    u_split_lo(U * 2 + 3, 0)
                if Tb is not None:
                    one_hot(Tb, h, 3, 1, oh_2, oh2_ok)
                if topk:
                    steps.settle()
                    steps.step(nc.vector.max(cvh[:, 8:16], comb_cut))
                    steps.did(nc.vector.max_index(ci_u[:, 8:16], cvh[:, 8:16], comb_cut))
                    steps.did(nc.vector.tensor_copy(CV[:, ds((U + 1) % UNITS_T, 1), :].squeeze(1), cvh))
                    steps.settle()
                    steps.did(ts(jj_u[:, 0, :], ci_u, 4, None, ALU.logical_shift_right))
                    steps.step(ts(jj_u[:, 1, :], ci_u, 15, None, ALU.bitwise_and))
                    steps.step(nc.vector.tensor_copy(jf, jj_u))
                    steps.did(tt(eq, jf.unsqueeze(3).to_broadcast([P, 2, TOPK, TOPK]),
                                 iota[:, 0:TOPK].unsqueeze(1).unsqueeze(1).to_broadcast([P, 2, TOPK, TOPK]),
                                 ALU.is_equal))
                if T is not None:
                    dve.wait_ge(par_tr, T + 1)
                    nc.vector.tensor_copy(par[:, ds(T % 2, 1), 0:3, :].squeeze(1),
                                          ps[:, 6, 0:384].rearrange("p (a b) -> p a b", a=3)).then_inc(par_ev, 1)
                    dve.wait_ge(par_ev, T + 1)
                    steps.step(nc.vector.tensor_copy(gate_r, par[:, ds(T % 2, 1), 2, :].squeeze(1)))
                    steps.step(tt(par[:, ds(T % 2, 1), 3, :].squeeze(1), par[:, ds(T % 2, 1), 2, :].squeeze(1),
                                  gate_r.bitcast(F32), ALU.subtract))
                if following is not None:
                    one_hot(*following, 0, 0, oh_1, oh1_ok)
                if Tb is not None:
                    add_G(Tb, h, 2)
                if topk:
                    steps.settle()
                    steps.did(tt(eq, eq, sif.unsqueeze(2).to_broadcast([P, 2, TOPK, TOPK]), ALU.mult))
                if following is not None:
                    one_hot(*following, 0, 1, oh_2, oh2_ok)
                if topk:
                    steps.settle()
                    steps.did(nc.vector.tensor_reduce(IDX[:, :, ds(((U + 1) % UNITS_T) * TOPK, TOPK)], eq, AX.X,
                                                      ALU.add))
                if Tb is not None:
                    add_G(Tb, h, 3)
                if topk or T is not None:
                    steps.rewind()

            head(3, 0, False)
            u_split_lo(1, 0)
            steps.rewind()
            unit(-1, None, None, True, False, split=False)
            head(3, 1, False)
            with dve.Fori(0, 7) as U:
                unit(U, None, None, True, True)
            unit(7, None, None, True, True, 0, following=(0, 0))
            with dve.Fori(1, TT - 1) as T:
                with dve.Fori(0, 7) as h:
                    unit(T * 8 + h, T - 1, h, True, True, following=(T - 1, h + 1))
                unit(T * 8 + 7, T - 1, 7, True, True, T, following=(T, 0))
            with dve.Fori(0, 7) as h:
                unit(h + 40, 4, h, True, True, following=(4, h + 1))
            unit(47, 4, 7, False, True, 5, following=(5, 0))
            with dve.Fori(0, 7) as h:
                unit(h + 48, 5, h, False, True, following=(5, h + 1))
            unit(55, 5, 7, False, True)
            with dve.Fori(56, 63) as U:
                unit(U, None, None, False, True)
            unit(63, None, None, False, False)
            def v_rest(n, blk, x):
                dve.wait_ge(v_hi, n * 4 + (x + 1))
                tt(vl[blk][:, x, :], vr[:, x, :], vh[blk][:, x, :].bitcast(F32), ALU.subtract).then_inc(v_lo, 1)

            def add_sums(H, half):
                for n in range(6):
                    t, dh = 3 * half + n // 2, n % 2
                    if n < 5:
                        dve.wait_ge(acc_done, H * 5 + (n + 1))
                    else:
                        dve.wait_ge(a_mm, H * 4 + 6)
                    tt(y[:, t, dh * 512:(dh + 1) * 512], y[:, t, dh * 512:(dh + 1) * 512], ps[:, n, :],
                       ALU.add).then_inc(acc_ev, 1)

            def a_rest(S, x):
                dve.wait_ge(a_hi, S + 1)
                tt(Al[:, x % 2, :], Aw[:, x % 2, :], Ah[:, x % 2, :].bitcast(F32), ALU.subtract).then_inc(a_lo, 1)

            def block_rests(i, blk, first=False, more=True):
                for half in range(2):
                    for x in range(VB):
                        if first and half == 0 and x < 2:
                            continue
                        a_rest(i * 16 + (blk * 8 + half * 4 + x), x)
                        if first and half == 1 and x == 0:
                            dve.wait_ge(y_in, 16 * TT)
                        if x == 0 and not (first and half == 0):
                            add_sums(i * 4 + (blk * 2 + half - 1), 1 - half)
                        if half == 1 and more:
                            v_rest(i * 2 + (blk + 1), 1 - blk, x)

            for x in range(2):
                v_rest(0, 0, x)
                a_rest(x, x)
            v_rest(0, 0, 2)
            v_rest(0, 0, 3)
            block_rests(0, 0, first=True)
            block_rests(0, 1)
            with dve.Fori(1, N_VB // 2 - 1) as i:
                block_rests(i, 0)
                block_rests(i, 1)
            block_rests(N_VB // 2 - 1, 0)
            block_rests(N_VB // 2 - 1, 1, more=False)
            add_sums(2 * N_VB - 1, 1)

        @block.tensor
        def _(pe):
            mm = nc.tensor.matmul
            pe.sem_inc(p_tr, 4)
            pe.sem_inc(pv_mm, 2)
            pe.sem_inc(s_mm, 12)
            pe.sem_inc(g_mm, 2)
            pe.sem_inc(a_mm, 2)
            pe.wait_ge(w_lo, 1)
            for k in range(KD):
                pe.wait_ge(ft_lo, k + 1)
                for t in range(TT):
                    last = pe_split_product(ps[:, t, 0:WC], FTh[:, k, t * P:(t + 1) * P], FTl[:, k, t * P:(t + 1) * P],
                                            Wh[:, 0, k, :], Wl[:, 0, k, :], k == 0, k == KD - 1)
                    if k == KD - 1:
                        last.then_inc(z_mm, 1)
            with pe.Fori(1, N_WIN) as c:
                pe.wait_ge(w_lo, c + 1)
                for t in range(TT):
                    pe.wait_ge(z_ev, c * 6 + (t + 1))
                    for k in range(KD):
                        last = pe_split_product(
                            ps[:, t, 0:WC], FTh[:, k, t * P:(t + 1) * P], FTl[:, k, t * P:(t + 1) * P],
                            Wh[:, ds(c % 2, 1), k, :].squeeze(1), Wl[:, ds(c % 2, 1), k, :].squeeze(1),
                            k == 0, k == KD - 1)
                    last.then_inc(z_mm, 1)

            def windows(gi):
                pe.wait_ge(band_in[gi % 2], 16 * (gi // 2 + 1))
                for q, (t0, n) in enumerate(SEQ_TILES):
                    if gi:
                        pe.wait_ge(pool_ev, 2 * (gi - 1) + q + 1)
                    for t in range(n):
                        srcs = [(s, 3 if s < t else 4 if s > t else 0 if t == 0 else 2 if t == n - 1 else 1)
                                for s in range(max(t - 1, 0), min(t + 2, n))]
                        for m, (s, kind) in enumerate(srcs):
                            last = mm(ps[:, q, t * P:(t + 1) * P],
                                      z[:, t0 + s, POOL_COL + gi * P:POOL_COL + (gi + 1) * P],
                                      band[:, gi % 2, kind, :], start=m == 0, stop=m == len(srcs) - 1)
                    last.then_inc(pool_mm, 1)

            def group_map(gi):
                for q, (t0, n) in enumerate(SEQ_TILES):
                    pe.wait_ge(pool_ev, 2 * gi + q + 1)
                    if gi:
                        pe.wait_ge(mix_lo, 2 * (gi - 1) + q + 1)
                    mm(ps[:, 2 + q, 0:n * P], poolw[:, gi * P:(gi + 1) * P],
                       pooled[:, gi % 2, t0 * P:(t0 + n) * P], start=True, stop=True).then_inc(mix_mm, 1)

            pe.wait_ge(z_ev, 6 + 30)
            pe.wait_ge(small_in, 16 * len(smalls))
            windows(0)
            def flip_qk(r):
                pe.wait_ge(rope_ok, TT)
                if r == 2:
                    pe.wait_ge(k_lo, 2)
                elif r >= 3:
                    pe.wait_ge(q_ev, 2 * (r - 2))
                col = K_COL if r == 0 else (r - 1) * P
                for t in range(TT):
                    last = nc.tensor.transpose(ps[:, 4 + 2 * (r % 2) + t // 4, (t % 4) * P:(t % 4 + 1) * P],
                                               qkr[:, t, col:col + P], ident[:, :])
                last.then_inc(qk_tr, 1)

            windows(1)
            group_map(0)
            windows(2)
            group_map(1)
            windows(3)
            group_map(2)
            flip_qk(0)
            group_map(3)
            for r in range(1, 5):
                flip_qk(r)
            pe.wait_ge(k_lo, 2)
            pe.wait_ge(q_ev, 8)
            pe.wait_ge(v_parts, 2)
            pe.wait_ge(mix_lo, 8)

            def scores(j, u):
                q, hh, t = units[u]
                t0, n = SEQ_TILES[q]
                rows, cols = slice(64 * hh, 64 * hh + 64), slice((t0 + t) * P, (t0 + t + 1) * P)
                keys = slice(t0 * P, (t0 + n) * P)
                pe.wait_ge(exp_ok, j * NU + (u + 1))
                pe_split_product(ps[:, u % 3, 0:n * P], qTh[rows, cols], qTl[rows, cols], kTh[rows, keys],
                                 kTl[rows, keys], True, True).then_inc(qk_mm, 1)

            def flip(j, u):
                n = SEQ_TILES[units[u][0]][1]
                pe.wait_ge(p_ok, j * NU + (u + 1))
                pe.wait_ge(pt_lo, j * NU + (u + 1))
                for s in range(n):
                    last = nc.tensor.transpose(ps[:, 3 + u % 3, s * P:(s + 1) * P],
                                               Pb[:, u % 4, s * P:(s + 1) * P], ident[:, :])
                last.then_inc(p_tr, 1)

            def values(j, g):
                q, hh, t = units[2 * g]
                t0, n = SEQ_TILES[q]
                pe.wait_ge(pt_lo, j * NU + (2 * g + 5))
                pe.wait_ge(o_lo, j * 2 + (q + 1))
                feats = slice(64 * hh, 64 * hh + P)
                for s in range(n):
                    last = pe_split_product(ps[:, 6 + q, t * P:(t + 2) * P], Vh[:, t0 + s, feats],
                                            Vl[:, t0 + s, feats], PTh[:, g % 2, s, :], PTl[:, g % 2, s, :],
                                            hh == s == 0, hh == 1 and s == n - 1)
                last.then_inc(pv_mm, 1)

            def pair(j, first=False):
                pe.wait_ge(q_lo, j + 1)
                for u in range(3):
                    scores(j, u)
                for u in range(NU):
                    if u + 3 < NU:
                        scores(j, u + 3)
                    if u >= 1:
                        flip(j, u - 1)
                    elif not first:
                        flip(j - 1, NU - 1)
                    if u in (1, 3) and not first:
                        values(j - 1, NG - 2 + u // 2)
                    if u >= 5 and u % 2 == 1:
                        values(j, u // 2 - 2)

            pair(0, True)
            with pe.Fori(1, 4) as j:
                pair(j)
            flip(3, NU - 1)
            values(3, NG - 2)
            values(3, NG - 1)
            pe.wait_ge(o_lo, 2 + 8)
            with pe.Fori(0, N_WOUT) as c:
                pe.wait_ge(w_lo, c + 6)
                for t in range(TT):
                    pe.wait_ge(y_ev, c * 6 + (t + 1))
                    for k in range(KD):
                        last = pe_split_product(
                            ps[:, t, 0:WC], FTh[:, k, t * P:(t + 1) * P], FTl[:, k, t * P:(t + 1) * P],
                            Wh[:, ds((c + 1) % 2, 1), k, :].squeeze(1), Wl[:, ds((c + 1) % 2, 1), k, :].squeeze(1),
                            k == 0, k == KD - 1)
                    last.then_inc(y_mm, 1)
            pe.wait_ge(y_ev, 6 + 24)
            for i in range(16):
                half, k = i // 8, i % 8
                pe.wait_ge(xs_act, 2 + half)
                pe.wait_ge(xs_dve, 1 + 2 * half)
                if i >= 4:
                    pe.wait_ge(xn_lo, i - 3)
                for t in range(3):
                    last = nc.tensor.transpose(ps[:, 4 + i % 4, t * P:(t + 1) * P],
                                               xs[:, 3 * half + t, k * P:(k + 1) * P], ident[:, :])
                last.then_inc(xn_tr, 1)
            pe.wait_ge(sk_in, 16)
            def key_scores(h, s, ts_):
                for t in ts_:
                    pe.wait_ge(s_ev, h * TT + (t + 1))
                    for p in range(2):
                        last = mm(ps[:, 4 + (6 * s + t) % 4, p * P:(p + 1) * P], qpT[:, s, p, t * P:(t + 1) * P],
                                  skT[:, ds(h * 2 + p, 1), :].squeeze(1), start=True, stop=True)
                    last.then_inc(s_mm, 1)

            def late_scores(h, s):
                pe.wait_ge(qp_ev, h * 4 + 8)
                key_scores(h, s, range(3, TT))

            def head(h, s, first=False):
                ws = (9 + s) % 2
                pe.wait_ge(w_lo, h + 10)
                for n in range(4):
                    half, p = n // 2, n % 2
                    pe.wait_ge(xn_lo, 8 + 8 * half)
                    pe.wait_ge(qp_ev, h * 4 + (n + 1))
                    for k in range(KD):
                        last = pe_split_product(
                            ps[:, n, 0:HALF], Wh[:, ws, k, p * P:(p + 1) * P], Wl[:, ws, k, p * P:(p + 1) * P],
                            FTh[:, k, half * HALF:(half + 1) * HALF], FTl[:, k, half * HALF:(half + 1) * HALF],
                            k == 0, k == KD - 1)
                    last.then_inc(qp_mm, 1)
                    if n == 0 and not first:
                        late_scores(h - 1, 1 - s)
                    if n == 2:
                        pe.wait_ge(qp_ev, h * 4 + 6)
                        key_scores(h, s, range(3))

            head(0, 0, True)
            head(1, 1)
            with pe.Fori(1, 4) as i:
                for s in range(2):
                    head(i * 2 + s, s)
            late_scores(7, 1)

            def unit(U, Tb, h, T=None):
                for s in range(2):
                    for half in range(2):
                        if half == 0:
                            pe.wait_ge(u_lo, U * 2 + (s + 1))
                        pe.wait_ge(gelu_ok, U * 4 + (2 * s + half + 1))
                        for k in range(KD):
                            last = pe_split_product(
                                ps[:, 2 * s + half, 0:HALF], uh[:, s, k, :], ul[:, s, k, :],
                                FTh[:, k, half * HALF:(half + 1) * HALF], FTl[:, k, half * HALF:(half + 1) * HALF],
                                k == 0, k == KD - 1)
                        last.then_inc(h_mm, 1)
                        if Tb is not None:
                            sg = 2 * s + half
                            Q = Tb * 32 + h * 4 + sg
                            pe.wait_ge(oh2_ok, Q + 1)
                            pe.wait_ge(ohg_ok, Q + 1)
                            pe.wait_ge(g_ev, Q + 1)
                            if T is not None and sg == 3:
                                pe.wait_ge(par_ev, T + 1)
                            for n in range(SG):
                                last = mm(ps[:, 4 + 2 * (sg % 2) + n // 2, (n % 2) * 256:(n % 2 + 1) * 256],
                                          oh_2[:, sg % 2, n, :], oh_g[:, sg % 2, n, :, :], start=True, stop=True)
                            last.then_inc(g_mm, 1)
                        if T is not None and s == 1 and half == 0:
                            pe.wait_ge(gate_ok, T + 1)
                            if Tb is not None:
                                pe.wait_ge(g_ev, Tb * 32 + h * 4 + 4)
                            for n in range(2):
                                nc.tensor.transpose(ps[:, 6, n * P:(n + 1) * P], IDX[:, n, :], ident[:, :])
                            nc.tensor.transpose(ps[:, 6, 2 * P:3 * P], B_[:, 3584:3712], ident[:, :]
                                                ).then_inc(par_tr, 1)

            with pe.Fori(0, 7) as U:
                unit(U, None, None)
            unit(7, None, None, 0)
            with pe.Fori(1, TT) as T:
                with pe.Fori(0, 7) as h:
                    unit(T * 8 + h, T - 1, h)
                unit(T * 8 + 7, T - 1, 7, T)
            with pe.Fori(0, UNITS_T) as h:
                unit(h + 48, TT - 1, h)
            with pe.Fori(56, 64) as U:
                unit(U, None, None)
            pe.wait_ge(gelu_ok, 4 + 256)
            with pe.Fori(0, N_VB // 2) as i:
                for step in range(4 * VB):
                    blk, half, x = step // 8, step // 4 % 2, step % 4
                    S, H = i * 16 + step, i * 4 + step // 4
                    if half == 0:
                        pe.wait_ge(v_lo, i * 8 + (blk * 4 + x + 5))
                    pe.wait_ge(a_lo, S + 3)
                    for n in range(6):
                        t, dh = n // 2, n % 2
                        if x == 0:
                            pe.wait_ge(acc_ev, H * 6 + (n + 1))
                        ah, al = (a[:, x % 2, t * P:(t + 1) * P] for a in (Ah, Al))
                        bh, bl = (b[blk][:, x, dh * 512:(dh + 1) * 512] for b in (vh, vl))
                        last = pe_split_product(ps[:, n, :], ah, al, bh, bl, x == 0, x == VB - 1)
                        if x == VB - 1 and n < 5:
                            last.then_inc(acc_done, 1)
                    last.then_inc(a_mm, 1)


def tables():
    f = np.float32
    pos = np.concatenate([np.arange(n * P) for _, n in SEQ_TILES])
    inv = (f(1.0) / (f(ROPE_THETA) ** (np.arange(0, ROPE_HALF, 2, dtype=f) / f(ROPE_HALF)))).astype(f)
    ang = np.stack([(pos // GRID_W).astype(f)[:, None] * inv, (pos % GRID_W).astype(f)[:, None] * inv], 1)
    rope = np.stack([np.cos(ang), np.sin(ang)]).astype(f).reshape(2, TT, P, 32).transpose(2, 0, 1, 3).reshape(P, -1)
    band = np.zeros((4, P, 5, P), f)
    n = 3 * P
    for g, w in enumerate(WINDOWS):
        m = np.zeros((n, n), f)
        for t in range(n):
            lo, hi = max(t - w // 2, 0), min(t + w - w // 2, n)
            m[lo:hi, t] = f(1.0) / f(hi - lo)
            m[t, t] -= f(1.0)
        blocks = {0: (0, 0), 1: (1, 1), 2: (2, 2), 3: (0, 1), 4: (1, 0)}
        for kind, (a, b) in blocks.items():
            band[g, :, kind] = m[a * P:(a + 1) * P, b * P:(b + 1) * P]
    return dict(ident=np.eye(P, dtype=f), iota=np.tile(np.arange(P, dtype=f), (P, 1)),
                rope=np.ascontiguousarray(rope), band=band)


def kernel(**inputs):
    import concourse.bacc as bacc
    from concourse.bass_utils import run_bass_kernel_spmd as run

    a = {k: np.asarray(v) for k, v in inputs.items()}
    heads = [0, 4, 1, 5, 2, 6, 3, 7]
    w = a["w_in"][0]
    w_q = w[:, 512:1024].reshape(D, 8, 64)[:, heads].reshape(D, 512)
    w_in = np.concatenate([w_q, w[:, 1024:1280], w[:, 0:512]], 1)
    wo = a["w_out"][0]
    wo = np.concatenate([wo[512:1024].reshape(8, 64, D)[heads].reshape(512, D), wo[0:512]], 0)
    w_all = np.concatenate([w_in, wo, a["peer_wq"][0]], 1)
    x = np.concatenate([a["x_prompt"][0], a["x_sample"][0]], 0)
    data = dict(
        x_prompt=a["x_prompt"], x_sample=a["x_sample"],
        xT=x.T.reshape(KD, P, TOK).transpose(1, 0, 2),
        vecs=np.concatenate([a["norm1_g"][0].reshape(8, P).T, a["norm2_g"][0].reshape(8, P).T,
                             a["pool_scale"][0].reshape(4, P).T], 1),
        gqk=np.concatenate([np.tile(a["q_norm_g"][0], 8), np.tile(a["k_norm_g"][0], 2)]),
        pool_w=a["pool_w"][0].transpose(1, 0, 2).reshape(P, 4 * P),
        w_all=w_all.reshape(KD, P, N_W, WC).transpose(2, 1, 0, 3),
        skT=a["peer_subkeys"][0].transpose(3, 0, 1, 2).reshape(P, 16, P),
        uT=a["peer_u"][0].reshape(NK, P, KD, P).transpose(0, 3, 2, 1),
        v=a["peer_v"][0].reshape(NK, P, D),
        **tables(),
    )
    data = {k: np.ascontiguousarray(v) for k, v in data.items()}
    nc = bacc.Bacc("TRN2", target_bir_lowering=False, num_devices=1)
    f32 = mybir.dt.float32
    io = {k: nc.dram_tensor("in_" + k, v.shape, f32, kind="ExternalInput").ap() for k, v in data.items()}
    scratch = dict(s_dram=(HEADS, P, TT, 256), g_dram=(NBLK, P, NK, BLK), gel_dram=(NK, P, TOK), y_dram=(TT, P, D))
    io.update({k: nc.dram_tensor(k, s, f32, kind="Internal").ap() for k, s in scratch.items()})
    outs = dict(y_prompt=(1, 512, D), y_sample=(1, 256, D))
    io.update({k: nc.dram_tensor(k, s, f32, kind="ExternalOutput").ap() for k, s in outs.items()})
    build(nc, io)
    r = run(nc, [{"in_" + k: v for k, v in data.items()}], core_ids=[0])
    return tuple(r.results[0][k] for k in outs)
```
